# Optimizing a Trainium2 kernel written in Bass

```python
import jax
import jax.numpy as jnp
from jax import lax
import numpy as np
import math
import jax, jax.numpy as jnp

D_MODEL = 1024
BATCH = 1
SEQ = 256
DEPTH = 1

CTX_LEN = 256
GRID_W = 64

POOL_WINDOWS = (2, 4, 8, 16)
POOL_GROUPS = len(POOL_WINDOWS)
POOL_GROUP_DIM = 128
POOL_WIDTH = POOL_GROUPS * POOL_GROUP_DIM

GLA_HEADS = 4
GLA_DK = D_MODEL // 2
GLA_DV = D_MODEL
GLA_HK = GLA_DK // GLA_HEADS
GLA_HV = GLA_DV // GLA_HEADS
GLA_GATE_RANK = 16
GLA_GATE_NORMALIZER = 16.0
GLA_CHUNK = 64

N_BRANCHES = 2
IN_WIDTHS = (POOL_WIDTH, GLA_DK, GLA_DK, GLA_DV, GLA_DV, N_BRANCHES * D_MODEL, 2 * GLA_GATE_RANK)
IN_SPLITS = tuple(int(s) for s in np.cumsum(IN_WIDTHS)[:-1])
D_IN = int(sum(IN_WIDTHS))

N_GROUPS = 4
EXPERTS_PER_GROUP = 8
N_EXPERTS = N_GROUPS * EXPERTS_PER_GROUP
TOP_K_IN_GROUP = 2
D_EXPERT = D_MODEL // 2

MOD_CHUNKS = 6
EPS = 1e-6


def _rmsnorm(x, g):
    xf = x.astype(jnp.float32)
    y = xf * lax.rsqrt(jnp.mean(xf * xf, axis=-1, keepdims=True) + EPS)
    return (y * g.astype(jnp.float32)).astype(x.dtype)

def _adaln(cond, w_mod, b_mod):
    return jnp.split(jnp.matmul(jax.nn.silu(cond), w_mod) + b_mod, MOD_CHUNKS, axis=-1)

def _heads(t, hd):
    b, l, _ = t.shape
    return t.reshape(b, l, GLA_HEADS, hd).transpose(0, 2, 1, 3)

def _flip(t):
    return jnp.flip(t, axis=2)

def _project(h, w_in, a2_f, ab_f, a2_b, ab_b):
    p = jnp.einsum('bld,de->ble', h, w_in)
    u, q, k, v, g, gates, lr = jnp.split(p, IN_SPLITS, axis=-1)
    lr_f, lr_b = jnp.split(lr, 2, axis=-1)
    la_f = jax.nn.log_sigmoid(jnp.matmul(lr_f, a2_f).astype(jnp.float32) + ab_f.astype(jnp.float32)) / GLA_GATE_NORMALIZER
    la_b = jax.nn.log_sigmoid(jnp.matmul(lr_b, a2_b).astype(jnp.float32) + ab_b.astype(jnp.float32)) / GLA_GATE_NORMALIZER
    return (u, _heads(q, GLA_HK) * (GLA_HK ** -0.5), _heads(k, GLA_HK), _heads(v, GLA_HV),
            _heads(la_f, GLA_HK), _heads(la_b, GLA_HK), g, gates)

def _centred_pool_minus_self(u):
    n, l, _ = u.shape
    uf = u.astype(jnp.float32)
    cs = jnp.concatenate([jnp.zeros((n, 1, POOL_WIDTH), jnp.float32), jnp.cumsum(uf, axis=1)], axis=1)
    t = np.arange(l)
    means = []
    for gi, w in enumerate(POOL_WINDOWS):
        lo = np.clip(t - w // 2, 0, l)
        hi = np.clip(t + w // 2, 0, l)
        cg = cs[..., gi * POOL_GROUP_DIM:(gi + 1) * POOL_GROUP_DIM]
        cnt = jnp.asarray((hi - lo)[:, None], jnp.float32)
        means.append((cg[:, hi] - cg[:, lo]) / cnt)
    return (jnp.concatenate(means, axis=-1) - uf).astype(u.dtype)

def _gla_chunked(q, k, v, log_a, s0):
    b, h, l, _ = q.shape
    dv = v.shape[-1]
    n = l // GLA_CHUNK

    def chunks(t):
        return t.astype(jnp.float32).reshape(b, h, n, GLA_CHUNK, t.shape[-1])

    qc, kc, vc, la = chunks(q), chunks(k), chunks(v), chunks(log_a)
    cum = jnp.cumsum(la, axis=3)
    last = cum[:, :, :, -1:, :]
    q_dec = qc * jnp.exp(cum)
    k_inv = kc * jnp.exp(-cum)
    k_rem = kc * jnp.exp(last - cum)
    lower = np.tril(np.ones((GLA_CHUNK, GLA_CHUNK), dtype=bool))
    scores = jnp.where(lower, jnp.einsum('bhnid,bhnjd->bhnij', q_dec, k_inv), 0.0)
    o_intra = jnp.einsum('bhnij,bhnjv->bhniv', scores, vc)
    decay = jnp.exp(last[:, :, :, 0, :])

    def step(state, inp):
        q_n, k_n, v_n, d_n = inp
        o_n = jnp.einsum('bhid,bhdv->bhiv', q_n, state)
        state = d_n[..., None] * state + jnp.einsum('bhid,bhiv->bhdv', k_n, v_n)
        return state, o_n

    xs = tuple(jnp.moveaxis(t, 2, 0) for t in (q_dec, k_rem, vc, decay))
    s_final, o_inter = lax.scan(step, s0, xs)
    o = o_intra + jnp.moveaxis(o_inter, 0, 2)
    return o.reshape(b, h, l, dv).astype(v.dtype), s_final

def _gla_final_state(k, v, log_a):
    cum = jnp.cumsum(log_a, axis=2)
    k_rem = k.astype(jnp.float32) * jnp.exp(cum[:, :, -1:, :] - cum)
    return jnp.einsum('bhtd,bhtv->bhdv', k_rem, v.astype(jnp.float32))

def _gla_bidirectional(q, k, v, la_f, la_b, s0_f, s0_b):
    o_f, _ = _gla_chunked(q, k, v, la_f, s0_f)
    o_b, _ = _gla_chunked(_flip(q), _flip(k), _flip(v), _flip(la_b), s0_b)
    return o_f + _flip(o_b)

def _mixer_out(pooled, o, g, gates, pool_w, pool_scale, gla_onorm_g, w_pool_br, w_gla_br, w_o):
    b, l, _ = pooled.shape
    y_pool = jnp.einsum('blgc,gce->blge', pooled.reshape(b, l, POOL_GROUPS, POOL_GROUP_DIM), pool_w)
    y_pool = jnp.matmul(y_pool.reshape(b, l, POOL_WIDTH) * pool_scale, w_pool_br)
    o = _rmsnorm(o, gla_onorm_g).transpose(0, 2, 1, 3).reshape(b, l, GLA_DV)
    y_gla = jnp.matmul(o * jax.nn.silu(g), w_gla_br)
    gate_pool, gate_gla = jnp.split(jax.nn.sigmoid(gates), N_BRANCHES, axis=-1)
    return jnp.matmul(gate_pool * y_pool + gate_gla * y_gla, w_o)

def _hier_moe(h, rg_w, rg_b, re_w, re_b, w1, w3, w2):
    b, l, d = h.shape
    t = h.reshape(b * l, d)
    grp_logits = (jnp.matmul(t, rg_w) + rg_b).astype(jnp.float32)
    grp_top, grp_idx = lax.top_k(grp_logits, 1)
    p_grp = jnp.exp(grp_top - jax.nn.logsumexp(grp_logits, axis=-1, keepdims=True))
    exp_logits = (jnp.matmul(t, re_w) + re_b).astype(jnp.float32).reshape(-1, N_GROUPS, EXPERTS_PER_GROUP)
    in_grp = jnp.einsum('tg,tge->te', jax.nn.one_hot(grp_idx[:, 0], N_GROUPS, dtype=jnp.float32), exp_logits)
    top_v, top_i = lax.top_k(in_grp, TOP_K_IN_GROUP)
    w = jax.nn.softmax(top_v, axis=-1) * p_grp
    expert_idx = grp_idx * EXPERTS_PER_GROUP + top_i
    combine = jnp.einsum('tk,tke->te', w, jax.nn.one_hot(expert_idx, N_EXPERTS, dtype=jnp.float32)).astype(h.dtype)
    out = jnp.zeros_like(t)
    for e in range(N_EXPERTS):
        hid = jax.nn.silu(jnp.matmul(t, w1[e])) * jnp.matmul(t, w3[e])
        out = out + combine[:, e:e + 1] * jnp.matmul(hid, w2[e])
    return out.reshape(b, l, d)

def first_inputs(seed: int = 0) -> dict:
    key = jax.random.key(seed)
    ks = jax.random.split(key, 32)
    d = D_MODEL

    def nrm(k, shape, scale):
        return jax.random.normal(k, shape, jnp.float32) * scale

    return {
        'x': nrm(ks[0], (BATCH, SEQ, d), 1.0),
        'c': nrm(ks[1], (BATCH, d), 1.0),
        'ctx': nrm(ks[2], (BATCH, CTX_LEN, d), 1.0),
        'c_ctx': nrm(ks[3], (d,), 1.0),
        'w_mod': nrm(ks[4], (DEPTH, d, MOD_CHUNKS * d), 0.5 * d ** -0.5),
        'b_mod': nrm(ks[5], (DEPTH, MOD_CHUNKS * d), 0.02),
        'norm1_g': 1.0 + nrm(ks[6], (DEPTH, d), 0.05),
        'norm2_g': 1.0 + nrm(ks[7], (DEPTH, d), 0.05),
        'w_in': nrm(ks[8], (DEPTH, d, D_IN), d ** -0.5),
        'gla_a2_f': nrm(ks[9], (DEPTH, GLA_GATE_RANK, GLA_DK), GLA_GATE_RANK ** -0.5),
        'gla_ab_f': nrm(ks[10], (DEPTH, GLA_DK), 0.5),
        'gla_a2_b': nrm(ks[11], (DEPTH, GLA_GATE_RANK, GLA_DK), GLA_GATE_RANK ** -0.5),
        'gla_ab_b': nrm(ks[12], (DEPTH, GLA_DK), 0.5),
        'gla_onorm_g': 1.0 + nrm(ks[13], (DEPTH, GLA_HV), 0.05),
        'pool_w': nrm(ks[14], (DEPTH, POOL_GROUPS, POOL_GROUP_DIM, POOL_GROUP_DIM), POOL_GROUP_DIM ** -0.5),
        'pool_scale': 1.0 + nrm(ks[15], (DEPTH, POOL_WIDTH), 0.1),
        'w_pool_br': nrm(ks[16], (DEPTH, POOL_WIDTH, d), POOL_WIDTH ** -0.5),
        'w_gla_br': nrm(ks[17], (DEPTH, GLA_DV, d), GLA_DV ** -0.5),
        'w_o': nrm(ks[18], (DEPTH, d, d), d ** -0.5),
        'router_grp_w': nrm(ks[19], (DEPTH, d, N_GROUPS), d ** -0.5),
        'router_grp_b': nrm(ks[20], (DEPTH, N_GROUPS), 0.01),
        'router_exp_w': nrm(ks[21], (DEPTH, d, N_EXPERTS), d ** -0.5),
        'router_exp_b': nrm(ks[22], (DEPTH, N_EXPERTS), 0.01),
        'moe_w1': nrm(ks[23], (DEPTH, N_EXPERTS, d, D_EXPERT), d ** -0.5),
        'moe_w3': nrm(ks[24], (DEPTH, N_EXPERTS, d, D_EXPERT), d ** -0.5),
        'moe_w2': nrm(ks[25], (DEPTH, N_EXPERTS, D_EXPERT, d), D_EXPERT ** -0.5),
        'final_norm_g': 1.0 + nrm(ks[26], (d,), 0.05),
    }

def first_block(x, c, ctx, c_ctx, w_mod, b_mod, norm1_g, norm2_g, w_in, gla_a2_f, gla_ab_f, gla_a2_b, gla_ab_b,
              gla_onorm_g, pool_w, pool_scale, w_pool_br, w_gla_br, w_o, router_grp_w, router_grp_b,
              router_exp_w, router_exp_b, moe_w1, moe_w3, moe_w2, final_norm_g):
    b, seq, d = x.shape
    rows = seq // GRID_W
    for i in range(DEPTH):
        proj_params = (w_in[i], gla_a2_f[i], gla_ab_f[i], gla_a2_b[i], gla_ab_b[i])
        mix_params = (pool_w[i], pool_scale[i], gla_onorm_g[i], w_pool_br[i], w_gla_br[i], w_o[i])
        moe_params = (router_grp_w[i], router_grp_b[i], router_exp_w[i], router_exp_b[i],
                      moe_w1[i], moe_w3[i], moe_w2[i])
        sh1, sc1, g1, sh2, sc2, g2 = [m[:, None, :] for m in _adaln(c, w_mod[i], b_mod[i])]
        csh1, csc1, cg1, csh2, csc2, cg2 = _adaln(c_ctx, w_mod[i], b_mod[i])

        hc = _rmsnorm(ctx, norm1_g[i]) * (1 + csc1) + csh1
        uc, qc, kc, vc, lfc, lbc, gc, gtc = _project(hc, *proj_params)
        st_f = _gla_final_state(kc, vc, lfc)
        st_b = _gla_final_state(_flip(kc), _flip(vc), _flip(lbc))

        hx = _rmsnorm(x, norm1_g[i]) * (1 + sc1) + sh1
        ux, qx, kx, vx, lfx, lbx, gx, gtx = _project(hx, *proj_params)
        pooled_x = _centred_pool_minus_self(ux.reshape(b * rows, GRID_W, POOL_WIDTH)).reshape(b, seq, POOL_WIDTH)
        ox = _gla_bidirectional(qx, kx, vx, lfx, lbx, st_f, st_b)
        x = x + g1 * _mixer_out(pooled_x, ox, gx, gtx, *mix_params)
        x = x + g2 * _hier_moe(_rmsnorm(x, norm2_g[i]) * (1 + sc2) + sh2, *moe_params)

        if i + 1 < DEPTH:
            zero_state = jnp.zeros_like(st_f)
            oc = _gla_bidirectional(qc, kc, vc, lfc, lbc, zero_state, zero_state)
            ctx = ctx + cg1 * _mixer_out(_centred_pool_minus_self(uc), oc, gc, gtc, *mix_params)
            ctx = ctx + cg2 * _hier_moe(_rmsnorm(ctx, norm2_g[i]) * (1 + csc2) + csh2, *moe_params)
    return _rmsnorm(x, final_norm_g)


DEPTH_2 = 2

CHUNK = 64
RMS_EPS = 1e-6
DN_WIDTH = D_MODEL // 2
DN_DHEAD = 128
DN_HEADS = DN_WIDTH // DN_DHEAD
DN_CONV = 4
SA_WIDTH = D_MODEL // 4
SA_DHEAD = 64
SA_HEADS = SA_WIDTH // SA_DHEAD
SA_DKV = SA_DHEAD
IDX_HEADS = 4
IDX_DHEAD = 64
IDX_TOPK_MAX = 256
Q_BLOCK = 128
HG_WIDTH = D_MODEL // 4
HG_DHEAD = 64
HG_HEADS = HG_WIDTH // HG_DHEAD
D_MIX = DN_WIDTH + SA_WIDTH + HG_WIDTH
D_FF = 2816
FFN_CONV = 3

SPLIT_SIZES = (DN_WIDTH, DN_WIDTH, DN_WIDTH, DN_WIDTH, DN_HEADS, DN_HEADS,
               SA_WIDTH, SA_DKV, SA_DKV, IDX_HEADS * IDX_DHEAD, IDX_DHEAD, IDX_HEADS,
               HG_WIDTH, HG_WIDTH, HG_WIDTH, HG_WIDTH)
D_IN_2 = sum(SPLIT_SIZES)
SPLIT_POINTS = tuple(int(p) for p in np.cumsum(SPLIT_SIZES)[:-1])


def rmsnorm(x, g):
    xf = x.astype(jnp.float32)
    y = xf * lax.rsqrt(jnp.mean(xf * xf, axis=-1, keepdims=True) + RMS_EPS)
    return (y * g.astype(jnp.float32)).astype(x.dtype)

def l2norm(x):
    return x * lax.rsqrt(jnp.sum(x * x, axis=-1, keepdims=True) + 1e-6)

def causal_depthwise_conv(x, w):
    K, C = w.shape
    return lax.conv_general_dilated(x, w[:, None, :].astype(x.dtype), window_strides=(1,),
                                    padding=[(K - 1, 0)],
                                    dimension_numbers=('NWC', 'WIO', 'NWC'),
                                    feature_group_count=C)

def to_chunks(t, n_heads, d_head):
    B, S = t.shape[:2]
    return t.reshape(B, S // CHUNK, CHUNK, n_heads, d_head).transpose(0, 3, 1, 2, 4)

def gate_chunks(t):
    B, S, H = t.shape
    return t.reshape(B, S // CHUNK, CHUNK, H).transpose(0, 3, 1, 2)

def from_chunks(o):
    N, B, H, C, d = o.shape
    return o.transpose(1, 0, 3, 2, 4).reshape(B, N * C, H, d)

def gated_deltanet(q, k, v, z, b, a, conv_w, a_log, dt_bias, norm_g):
    dtype = q.dtype
    Bsz, S, _ = q.shape
    qkv = jax.nn.silu(causal_depthwise_conv(jnp.concatenate([q, k, v], axis=-1), conv_w))
    q, k, v = jnp.split(qkv.astype(jnp.float32), 3, axis=-1)
    q = l2norm(to_chunks(q, DN_HEADS, DN_DHEAD)) * (DN_DHEAD ** -0.5)
    k = l2norm(to_chunks(k, DN_HEADS, DN_DHEAD))
    v = to_chunks(v, DN_HEADS, DN_DHEAD)
    beta = gate_chunks(jax.nn.sigmoid(b.astype(jnp.float32)))
    g = -jnp.exp(a_log.astype(jnp.float32)) * jax.nn.softplus(
        a.astype(jnp.float32) + dt_bias.astype(jnp.float32))
    G = jnp.cumsum(gate_chunks(g), axis=-1)
    causal = jnp.tril(jnp.ones((CHUNK, CHUNK), bool))
    strict = jnp.tril(jnp.ones((CHUNK, CHUNK), bool), k=-1)
    decay = jnp.exp(jnp.where(causal, G[..., :, None] - G[..., None, :], -jnp.inf))
    kk = jnp.einsum('bhnck,bhnsk->bhncs', k, k)
    M = jnp.where(strict, beta[..., :, None] * kk * decay, 0.0)
    eye = jnp.eye(CHUNK, dtype=jnp.float32)
    T = lax.linalg.triangular_solve(eye + M, jnp.broadcast_to(eye, M.shape),
                                    left_side=True, lower=True, unit_diagonal=True)
    u0 = jnp.einsum('bhncs,bhnsv->bhncv', T, beta[..., None] * v)
    wk = jnp.einsum('bhncs,bhnsk->bhnck', T, (beta * jnp.exp(G))[..., None] * k)
    qk = jnp.einsum('bhnck,bhnsk->bhncs', q, k) * decay
    q_dec = q * jnp.exp(G)[..., None]
    k_dec = k * jnp.exp(G[..., -1:] - G)[..., None]
    g_last = jnp.exp(G[..., -1])

    def step(state, inp):
        u0_c, w_c, qk_c, qd_c, kd_c, gl_c = inp
        u = u0_c - jnp.einsum('bhck,bhkv->bhcv', w_c, state)
        o = jnp.einsum('bhck,bhkv->bhcv', qd_c, state) + jnp.einsum('bhcs,bhsv->bhcv', qk_c, u)
        state = state * gl_c[..., None, None] + jnp.einsum('bhck,bhcv->bhkv', kd_c, u)
        return state, o

    xs = tuple(jnp.moveaxis(t, 2, 0) for t in (u0, wk, qk, q_dec, k_dec, g_last))
    s0 = jnp.zeros((Bsz, DN_HEADS, DN_DHEAD, DN_DHEAD), jnp.float32)
    _, o = lax.scan(step, s0, xs)
    o = rmsnorm(from_chunks(o), norm_g)
    o = o * jax.nn.silu(z.astype(jnp.float32).reshape(Bsz, S, DN_HEADS, DN_DHEAD))
    return o.reshape(Bsz, S, DN_WIDTH).astype(dtype)

def dsa_attention(q, k, v, qi, ki, wi):
    dtype = q.dtype
    Bsz, S, _ = q.shape
    nb = S // Q_BLOCK
    topk = min(IDX_TOPK_MAX, S // 4)
    f32 = jnp.float32
    qb_all = q.astype(f32).reshape(Bsz, nb, Q_BLOCK, SA_HEADS, SA_DHEAD).transpose(1, 0, 2, 3, 4)
    qib_all = qi.astype(f32).reshape(Bsz, nb, Q_BLOCK, IDX_HEADS, IDX_DHEAD).transpose(1, 0, 2, 3, 4)
    wib_all = (wi.astype(f32) * (IDX_HEADS ** -0.5 * IDX_DHEAD ** -0.5)).reshape(
        Bsz, nb, Q_BLOCK, IDX_HEADS).transpose(1, 0, 2, 3)
    k = k.astype(f32)
    v = v.astype(f32)
    ki = ki.astype(f32)
    key_chunk = jnp.arange(S) // CHUNK
    gather = jax.vmap(lambda t, idx: t[idx])

    def block(args):
        qb, qib, wib, blk = args
        q_chunk = (blk * Q_BLOCK + jnp.arange(Q_BLOCK)) // CHUNK
        score = jnp.einsum('bqhs,bqh->bqs',
                           jax.nn.relu(jnp.einsum('bqhd,bsd->bqhs', qib, ki)), wib)
        admissible = key_chunk[None, :] <= q_chunk[:, None]
        score = jnp.where(admissible[None], score, -jnp.inf)
        _, idx = lax.top_k(score, topk)
        k_sel = gather(k, idx)
        v_sel = gather(v, idx)
        valid = key_chunk[idx] <= q_chunk[None, :, None]
        logits = jnp.einsum('bqhd,bqkd->bqhk', qb, k_sel) * (SA_DHEAD ** -0.5)
        logits = jnp.where(valid[:, :, None, :], logits, -jnp.inf)
        p = jax.nn.softmax(logits, axis=-1)
        return jnp.einsum('bqhk,bqkd->bqhd', p, v_sel)

    o = lax.map(block, (qb_all, qib_all, wib_all, jnp.arange(nb)))
    return o.transpose(1, 0, 2, 3, 4).reshape(Bsz, S, SA_WIDTH).astype(dtype)

def hgrn2(q, f, i, g, lb, norm_g):
    dtype = q.dtype
    Bsz, S, _ = q.shape
    f32 = jnp.float32
    fg = lb + (1.0 - lb) * jax.nn.sigmoid(f.astype(f32))
    qc = to_chunks(jax.nn.silu(q.astype(f32)), HG_HEADS, HG_DHEAD)
    kc = to_chunks(1.0 - fg, HG_HEADS, HG_DHEAD)
    vc = to_chunks(i.astype(f32), HG_HEADS, HG_DHEAD)
    Bc = jnp.cumsum(to_chunks(jnp.log(fg), HG_HEADS, HG_DHEAD), axis=-2)
    q_dec = qc * jnp.exp(Bc)
    k_dec = kc * jnp.exp(Bc[..., -1:, :] - Bc)
    g_last = jnp.exp(Bc[..., -1, :])
    causal = jnp.tril(jnp.ones((CHUNK, CHUNK), bool))[..., None]

    def step(state, inp):
        q_c, k_c, v_c, b_c, qd_c, kd_c, gl_c = inp
        dec = jnp.exp(jnp.where(causal, b_c[..., :, None, :] - b_c[..., None, :, :], -jnp.inf))
        A = jnp.einsum('bhck,bhsk,bhcsk->bhcs', q_c, k_c, dec)
        o = jnp.einsum('bhck,bhkv->bhcv', qd_c, state) + jnp.einsum('bhcs,bhsv->bhcv', A, v_c)
        state = gl_c[..., :, None] * state + jnp.einsum('bhck,bhcv->bhkv', kd_c, v_c)
        return state, o

    xs = tuple(jnp.moveaxis(t, 2, 0) for t in (qc, kc, vc, Bc, q_dec, k_dec, g_last))
    s0 = jnp.zeros((Bsz, HG_HEADS, HG_DHEAD, HG_DHEAD), f32)
    _, o = lax.scan(step, s0, xs)
    o = rmsnorm(from_chunks(o), norm_g)
    o = o * jax.nn.silu(g.astype(f32).reshape(Bsz, S, HG_HEADS, HG_DHEAD))
    return o.reshape(Bsz, S, HG_WIDTH).astype(dtype)

def conv_geglu_ffn(h, w_up, conv_w, w_down):
    up = causal_depthwise_conv(h @ w_up, conv_w)
    gate, val = jnp.split(up, 2, axis=-1)
    return (jax.nn.gelu(gate, approximate=True) * val) @ w_down

def second_inputs(seed: int = 0) -> dict:
    key = jax.random.key(seed)
    ks = jax.random.split(key, 16)
    f32 = jnp.float32
    nrm = lambda k, s: jax.random.normal(k, s, f32)
    x = nrm(ks[0], (BATCH, SEQ, D_MODEL))
    w_in = nrm(ks[1], (DEPTH_2, D_MODEL, D_IN_2)) * D_MODEL ** -0.5
    dn_conv = nrm(ks[2], (DEPTH_2, DN_CONV, 3 * DN_WIDTH)) * DN_CONV ** -0.5
    dn_a_log = jnp.log(jax.random.uniform(ks[3], (DEPTH_2, DN_HEADS), f32, 1.0, 16.0))
    dt = jnp.exp(jax.random.uniform(ks[4], (DEPTH_2, DN_HEADS), f32,
                                    math.log(1e-3), math.log(1e-1)))
    dn_dt_bias = dt + jnp.log(-jnp.expm1(-dt))
    dn_norm = 1.0 + 0.02 * nrm(ks[5], (DEPTH_2, DN_DHEAD))
    hg_lb = 0.1 * nrm(ks[6], (DEPTH_2, HG_WIDTH))
    hg_norm = 1.0 + 0.02 * nrm(ks[7], (DEPTH_2, HG_DHEAD))
    w_out = nrm(ks[8], (DEPTH_2, D_MIX, D_MODEL)) * D_MIX ** -0.5
    g_mix_pre = 1.0 + 0.02 * nrm(ks[9], (DEPTH_2, D_MODEL))
    g_mix_post = 1.0 + 0.02 * nrm(ks[10], (DEPTH_2, D_MODEL))
    g_ffn_pre = 1.0 + 0.02 * nrm(ks[11], (DEPTH_2, D_MODEL))
    g_ffn_post = 1.0 + 0.02 * nrm(ks[12], (DEPTH_2, D_MODEL))
    ffn_w_up = nrm(ks[13], (DEPTH_2, D_MODEL, 2 * D_FF)) * D_MODEL ** -0.5
    ffn_conv = nrm(ks[14], (DEPTH_2, FFN_CONV, 2 * D_FF)) * FFN_CONV ** -0.5
    ffn_w_down = nrm(ks[15], (DEPTH_2, D_FF, D_MODEL)) * D_FF ** -0.5
    return {'x': x, 'w_in': w_in, 'dn_conv': dn_conv, 'dn_a_log': dn_a_log,
            'dn_dt_bias': dn_dt_bias, 'dn_norm': dn_norm, 'hg_lb': hg_lb, 'hg_norm': hg_norm,
            'w_out': w_out, 'g_mix_pre': g_mix_pre, 'g_mix_post': g_mix_post,
            'g_ffn_pre': g_ffn_pre, 'g_ffn_post': g_ffn_post, 'ffn_w_up': ffn_w_up,
            'ffn_conv': ffn_conv, 'ffn_w_down': ffn_w_down}

def second_block(x, w_in, dn_conv, dn_a_log, dn_dt_bias, dn_norm, hg_lb, hg_norm, w_out,
              g_mix_pre, g_mix_post, g_ffn_pre, g_ffn_post, ffn_w_up, ffn_conv, ffn_w_down):
    cs = jnp.cumsum(jax.nn.softmax(hg_lb.astype(jnp.float32), axis=0), axis=0)
    lower_bounds = cs - cs[0:1]
    for l in range(DEPTH_2):
        h = rmsnorm(x, g_mix_pre[l])
        (a_q, a_k, a_v, a_z, a_b, a_a,
         b_q, b_k, b_v, b_qi, b_ki, b_wi,
         c_q, c_f, c_i, c_g) = jnp.split(h @ w_in[l], SPLIT_POINTS, axis=-1)
        o_a = gated_deltanet(a_q, a_k, a_v, a_z, a_b, a_a, dn_conv[l], dn_a_log[l],
                             dn_dt_bias[l], dn_norm[l])
        o_b = dsa_attention(b_q, b_k, b_v, b_qi, b_ki, b_wi)
        o_c = hgrn2(c_q, c_f, c_i, c_g, lower_bounds[l], hg_norm[l])
        mix = jnp.concatenate([o_a, o_b, o_c], axis=-1) @ w_out[l]
        x = x + rmsnorm(mix, g_mix_post[l])
        h = rmsnorm(x, g_ffn_pre[l])
        x = x + rmsnorm(conv_geglu_ffn(h, ffn_w_up[l], ffn_conv[l], ffn_w_down[l]), g_ffn_post[l])
    return x


def setup_inputs(seed=0):
    out = dict(first_inputs(seed))
    for name, value in second_inputs(seed + 1).items():
        if name != "x":
            out[name + "_2"] = value
    return out


def reference(
    x, c, ctx, c_ctx, w_mod, b_mod, norm1_g, norm2_g, w_in, gla_a2_f, gla_ab_f, gla_a2_b,
    gla_ab_b, gla_onorm_g, pool_w, pool_scale, w_pool_br, w_gla_br, w_o, router_grp_w,
    router_grp_b, router_exp_w, router_exp_b, moe_w1, moe_w3, moe_w2, final_norm_g, w_in_2,
    dn_conv_2, dn_a_log_2, dn_dt_bias_2, dn_norm_2, hg_lb_2, hg_norm_2, w_out_2, g_mix_pre_2,
    g_mix_post_2, g_ffn_pre_2, g_ffn_post_2, ffn_w_up_2, ffn_conv_2, ffn_w_down_2,
):
    x = first_block(
        x, c, ctx, c_ctx, w_mod, b_mod, norm1_g, norm2_g, w_in, gla_a2_f, gla_ab_f, gla_a2_b,
        gla_ab_b, gla_onorm_g, pool_w, pool_scale, w_pool_br, w_gla_br, w_o, router_grp_w,
        router_grp_b, router_exp_w, router_exp_b, moe_w1, moe_w3, moe_w2, final_norm_g,
    )
    return second_block(
        x, w_in_2, dn_conv_2, dn_a_log_2, dn_dt_bias_2, dn_norm_2, hg_lb_2, hg_norm_2, w_out_2,
        g_mix_pre_2, g_mix_post_2, g_ffn_pre_2, g_ffn_post_2, ffn_w_up_2, ffn_conv_2,
        ffn_w_down_2,
    )


_drawn_inputs = setup_inputs


def setup_inputs(seed=0):
    import zlib

    import numpy as np

    out = dict(_drawn_inputs(seed))
    spreads = {}
    factors = {'router_grp_b': 8.0,
     'router_exp_b': 4.342,
     'hg_lb_2': 8.0,
     'hg_norm_2': 10.397,
     'gla_onorm_g': 2.914,
     'dn_norm_2': 5.892,
     'g_ffn_post_2': 3.044}
    for name, (base, spread) in spreads.items():
        noise = np.random.default_rng([zlib.crc32(name.encode()), seed]).standard_normal(out[name].shape)
        drawn = base * np.exp(spread * noise) if base else spread * noise
        out[name] = jnp.asarray(drawn.astype(out[name].dtype))
    for name, factor in factors.items():
        out[name] = (out[name] * factor).astype(out[name].dtype)
    return out
```

```python
from contextlib import ExitStack

import numpy as np

import concourse.bass as bass
from concourse import mybir

ALU = mybir.AluOpType
ACT = mybir.ActivationFunctionType
F32 = mybir.dt.float32
I32 = mybir.dt.int32
AX = mybir.AxisListType

P = 128
D = 1024
T = 256
KT = D // P
TT = T // P
CH = 64
NCH = T // CH
EPS = 1e-6
BIG = 1e30
NEG = -3e38

POOL_W = 512
POOL_G = 4
GRID_W = 64
ROWS = T // GRID_W
PADW = GRID_W + 16
GH = 4
GDK = 512
GDV = 1024
GATE_NORM = 16.0
N_GRP = 4
N_EXP = 32
D_EXP = 512
SLOTS = 64
PAIRS = N_EXP // 2

DN = 512
DNH = 4
DN_CONV = 4
SA = 256
SAH = 4
SAD = 64
TOPK = 64
HG = 256
D_FF = 2816
FFT = D_FF // P
FFN_CONV = 3
LAYERS = 2

U0, Q0, K0, V0, G0, GT0, LR0 = 0, 512, 1024, 1536, 2560, 3584, 5632
AQ0, AK0, AV0, AZ0, AB0, BQ0, BK0, BV0, BQI0, BKI0, BWI0, CQ0, CI0 = (
    0, 512, 1024, 1536, 2048, 2056, 2312, 2376, 2440, 2696, 2760, 2764, 3276)

SLAB = 4096


def constants():
    i = np.arange(P)
    r, c = i[:, None], i[None, :]
    same = (r // CH) == (c // CH)
    parts = {
        "ident": r == c,
        "ones": np.ones((P, P)),
        "incl": same & (r <= c),
        "rev": same & (r >= c),
        "blk": same,
        "before": r < c,
    }
    for lv in range(6):
        b = 1 << lv
        parts[f"lv{lv}"] = ((r // (2 * b)) == (c // (2 * b))) & ((r // b) % 2 == 0) & ((c // b) % 2 == 1)
    parts["diag16"] = ((r // 16) == (c // 16)) & (r <= c)
    parts["iota"] = np.broadcast_to(np.arange(SLOTS), (P, SLOTS))
    parts["desc"] = np.broadcast_to(N_EXP - np.arange(N_EXP), (P, N_EXP))
    parts["thr"] = np.broadcast_to(np.arange(4) * SLOTS, (P, 4))
    t = np.arange(T)
    adm = []
    for tt in range(TT):
        q = (tt * P + i)[:, None] // CH
        adm.append(np.where(t[None, :] // CH <= q, 0.0, -BIG))
    parts["adm"] = np.concatenate(adm, 1)
    cnt = []
    g = np.arange(GRID_W)
    for w in (2, 4, 8, 16):
        cnt.append(1.0 / (np.minimum(g + w // 2, GRID_W) - np.maximum(g - w // 2, 0)))
    parts["rcnt"] = np.broadcast_to(np.concatenate(cnt), (P, 4 * GRID_W))
    parts["reset"] = np.broadcast_to(np.concatenate([t != 0, t % CH != 0]), (P, 2 * T))
    parts["eps"] = np.full((P, 1), EPS)
    parts["one"] = np.ones((P, 1))
    offs, arrs, at = {}, [], 0
    for k, v in parts.items():
        v = np.asarray(v, np.float32)
        offs[k] = (at, v.shape[1])
        at += v.shape[1]
        arrs.append(v)
    return offs, np.ascontiguousarray(np.concatenate(arrs, 1))


ROWS_A = [("c", 8), ("c_ctx", 8), ("norm1_g", 8), ("norm2_g", 8), ("b_mod", 48), ("gla_ab_f", 4), ("gla_ab_b", 4),
          ("pool_scale", 4), ("gla_onorm_g", 2), ("final_norm_g", 8)]
ROWS_B = [("g_mix_pre_2", 8), ("g_mix_post_2", 8), ("g_ffn_pre_2", 8), ("g_ffn_post_2", 8), ("dn_conv_2", 48),
          ("dn_norm_2", 1), ("hg_norm_2", 1), ("hg_lb_2", 2)]
NA = sum(n for _, n in ROWS_A)
NB = sum(n for _, n in ROWS_B)
NC3 = FFN_CONV * 2 * FFT
NC_HEAD = P - NB
LCOLS = NB + NC3


def row_at(rows, name):
    at = 0
    for n, k in rows:
        if n == name:
            return at
        at += k
    raise KeyError(name)


def build(nc, W, out):
    offs, _ = constants()
    ctx = ExitStack()
    with ctx:
        def sb(name, shape, dt=F32):
            return ctx.enter_context(nc.sbuf_tensor(name, shape, dt))

        sems = {}

        def sem(name):
            if name not in sems:
                sems[name] = ctx.enter_context(nc.semaphore(name))
            return sems[name]

        cst = sb("cst", [P, sum(n for _, n in offs.values())])

        def C(name):
            a, n = offs[name]
            return cst[:, a:a + n]

        ring = sb("ring", [P, 6, SLAB])
        colsA = sb("colsA", [P, NA])
        colsL = sb("colsL", [P, 2, LCOLS])
        logs = sb("logs", [P, 2, 8])
        lbc = sb("lbc", [P, 2, 4])
        mods = sb("mods", [P, 48, 2])
        ada = sb("ada", [P, 8, KT])
        small = sb("small", [P, 64])
        ARENA = 22100
        arena = sb("arena", [P, ARENA])
        xT = sb("xT", [P, KT, T])

        class Area:

            def __init__(self, view, size):
                self.view, self.size, self.at = view, size, 0

            def take(self, *dims):
                n = int(np.prod(dims))
                assert self.at + n <= self.size, (self.at, n, self.size)
                v = self.view[:, self.at:self.at + n]
                self.at += n
                if len(dims) == 1:
                    return v
                names = "abcd"[:len(dims)]
                return v.rearrange("p (%s) -> p %s" % (" ".join(names), " ".join(names)),
                                   **{k: d for k, d in zip(names[1:], dims[1:])})

        ringflat = ring[:, :, :].rearrange("p s n -> p (s n)")

        PS = ctx.enter_context(nc.psum_tensor("PS", [P, 8, 512], F32))

        def colA(name, j=0, n=1):
            a = row_at(ROWS_A, name) + j
            return colsA[:, a:a + n]

        params_in = sem("params_in")
        x_in = sem("x_in")
        wl = [sem(f"slab_in{i}") for i in range(3)]
        ml = [sem(f"expert_in{i}") for i in range(6)]
        w1_read, h_ready, w2_read, y_full = sem("w1_read"), sem("h_ready"), sem("w2_read"), sem("y_full")
        ll = [sem(f"layer_slab_in{i}") for i in range(3)]
        go = {n: sem(f"go_{n}") for n in ("pe", "sp", "act", "dve")}
        out_done = sem("out_done")
        psum_full = sem("psum_full")
        psum_free = [sem(f"psum_free{b}") for b in range(8)]
        idle = sem("idle")
        stages = [psum_full, *psum_free, idle, *ll]

        def S(name):
            if name not in sems:
                stages.append(sem(name))
            return sems[name]

        class Phase:

            def __init__(self):
                self.units = []

            def bank(self, pe, key):
                u = len(self.units)
                self.units.append(key)
                if u >= 8:
                    pe.wait_ge(psum_free[u % 8], u // 8)
                return u % 8

            def read(self, eng, key):
                u = self.units.index(key)
                eng.wait_ge(psum_full, u + 1)
                return u % 8

            def freed(self, eng, key):
                u = self.units.index(key)
                eng.wait_ge(psum_free[u % 8], u // 8 + 1)

        ph1, ph2, ph3 = Phase(), Phase(), Phase()

        class Chain:

            def __init__(self, eng, name):
                self.eng, self.s, self.n = eng, S(name), 0

            def __call__(self, ins):
                self.n += 1
                ins.then_inc(self.s, 1)
                self.eng.wait_ge(self.s, self.n)

        def meet(eng, n):
            eng.drain().then_inc(idle, 1)
            eng.wait_ge(go[n], 1)
            eng.nop().then_inc(go[n], -1)

        out_T = out.rearrange("a t d -> (a t) d")

        A1 = Area(arena, ARENA)
        X1 = Area(ringflat[:, 3 * SLAB:], 3 * SLAB)
        hboth = A1.take(KT, 2 * T)
        vtok = A1.take(4, GDV)
        kT = A1.take(GH, 2 * T)
        qT = A1.take(GH, T)
        la_flat = A1.take(2 * GH * 2 * T)
        la = la_flat.rearrange("p (d h t) -> p d h t", d=2, h=GH)
        krt = A1.take(2, TT, GDK)
        s0 = A1.take(2, GH, 256)
        sg = A1.take(KT, T)
        poolw = A1.take(POOL_G, P)
        rowsA = sg.rearrange("p k t -> p (k t)")[0:NA, 0:P]
        rowsB = sg.rearrange("p k t -> p (k t)")[:, P:3 * P].rearrange("p (l n) -> p l n", l=2)
        rowsC = sg.rearrange("p k t -> p (k t)")[0:NC3 - NC_HEAD, 3 * P:5 * P].rearrange("p (l n) -> p l n", l=2)
        cum_flat = X1.take(2 * GH * 2 * T)
        cum = cum_flat.rearrange("p (d h t) -> p d h t", d=2, h=GH)
        qdki = X1.take(2 * 2 * GH * T)
        qd = qdki[:, 0:2 * GH * T].rearrange("p (d h t) -> p d h t", d=2, h=GH)
        ki = qdki[:, 2 * GH * T:].rearrange("p (d h t) -> p d h t", d=2, h=GH)
        e1 = X1.take(GH, T)
        e2 = X1.take(GH, T)
        lrT = X1.take(2 * T)
        a2 = X1.take(2, GDK)
        wlr = X1.take(KT, 32)
        xraw = cum_flat.rearrange("p (s t d) -> p s t d", s=2, t=TT)
        sqb = la_flat.rearrange("p (k t) -> p k t", k=KT)
        rstd = qdki[:, 0:2 * T]
        Sx = la_flat[:, 0:3072].rearrange("p (i d n v) -> p i d n v", i=2, d=2, n=3)
        scT = e1.rearrange("p h (t c) -> p h t c", t=TT)
        oT = cum_flat[:, 0:2048].rearrange("p (j t) -> p j t", j=KT)
        osq = cum_flat[:, 2048:4096].rearrange("p (j t) -> p j t", j=KT)
        pads = [qdki[:, i * 1280:(i + 1) * 1280].rearrange("p (g r w) -> p g r w", g=POOL_G, r=ROWS) for i in range(3)]
        pooled = e2
        yp = kT.rearrange("p h t -> p (h t)")[:, 0:1024].rearrange("p (g t) -> p g t", g=POOL_G)
        gates = vtok.rearrange("p a b -> p (a b)").rearrange("p (j t) -> p j t", j=16)
        mixed = krt.rearrange("p d t n -> p (d t n)").rearrange("p (j t) -> p j t", j=KT)
        csil = small[:, 0:16].rearrange("p (v k) -> p k v", v=2)
        lastx = small[:, 16:48].rearrange("p (d h n) -> p d h n", d=2, h=GH)
        dec = ada[:, 4:8, :].rearrange("p a b -> p (a b)").rearrange("p (d h n) -> p d h n", d=2, h=GH)
        lastc = small[:, 48:52]

        def mod(m, v, k):
            return mods[:, 8 * m + k, v:v + 1]

        A2 = Area(arena, ARENA)
        h2T = A2.take(KT, T)
        h2n = A2.take(KT, T)
        h2t = A2.take(TT, D)
        hg = A2.take(KT, P)
        s1 = A2.take(2, 256)
        hid = A2.take(2, 4, SLOTS)
        ytok = A2.take(D)
        PT = A2.take(T)
        sel = A2.take(TT, 2, SLOTS)
        selw = A2.take(TT, 2, SLOTS)
        rw = A2.take(KT, N_GRP + N_EXP)
        rb = A2.take(N_GRP + N_EXP)
        rstd2 = A2.take(T)
        lg = A2.take(TT, N_GRP + N_EXP)
        m32 = [A2.take(TT, N_EXP) for _ in range(8)]
        m8 = [A2.take(TT, N_GRP) for _ in range(4)]
        m1 = [A2.take(TT) for _ in range(10)]
        totals = A2.take(N_EXP)
        ranks = A2.take(TT, N_EXP + 2)
        weights = A2.take(TT, N_EXP + 2)
        mx1 = A2.take(4)
        rounds_i = A2.take(1).bitcast(I32)

        A3 = Area(arena, ARENA)
        X3 = Area(ringflat[:, 3 * SLAB:], 3 * SLAB)
        hT = A3.take(KT, T)
        cat = A3.take(KT, T)
        sc3 = A3.take(KT, T)
        cs = A3.take(12, T)
        sz = A3.take(DNH, T)
        eG = A3.take(DNH, T)
        DT = A3.take(DNH, TT, P)
        MT = A3.take(DNH, TT, P)
        QK = A3.take(DNH, TT, P)
        XI = A3.take(DNH, TT, P)
        XIT = A3.take(DNH, TT, P)
        BT = [A3.take(DNH, TT, P) for _ in range(2)]
        Z = A3.take(DNH, TT, P)
        kd = A3.take(TT, DNH, P)
        kvb = sc3.rearrange("p k t -> p (k t)").rearrange("p (a t h c) -> p a t h c", a=2, t=TT, h=DNH)
        kb, vb = kvb[:, 0], kvb[:, 1]
        gx, bx = Z, BT[1]
        u = BT[0].rearrange("p h t c -> p (h t c)").rearrange("p (t h c) -> p t h c", t=TT, h=DNH)
        wk = BT[1].rearrange("p h t c -> p h (t c)")
        Sd = [v.rearrange("p h t c -> p (h t c)")[:, i * 512:(i + 1) * 512].rearrange("p (h v) -> p h v", h=DNH)
              for v, i in ((XI, 0), (XI, 1), (Z, 0))]
        qb = X3.take(2, T)
        kbb = X3.take(T)
        qi = X3.take(2, T)
        kii = X3.take(T)
        vtk = X3.take(TT, SAD)
        cq = X3.take(2, T)
        cf = X3.take(2, T)
        cit = X3.take(TT, HG)
        cg = X3.take(2, T)
        kc = X3.take(2, T)
        room = 3 * SLAB - X3.at
        shared = X3.take(room)
        XB = Area(shared, room)
        relu = XB.take(2, 2, T)
        score = XB.take(TT, T)
        work = XB.take(TT, T)
        pr = XB.take(TT, SAH, T)
        pT = XB.take(SAH, TT, T)
        XC = Area(shared, room)
        args = XC.take(3, 2, 2 * T)
        Bc = XC.take(2, T)
        eB = XC.take(2, T)
        eR = XC.take(2, T)
        AT = XC.take(2, 2, TT, P)
        AT2 = XC.take(2, TT, P)
        kdt = XC.take(TT, HG)
        Sh = XC.take(3, 2, P)
        col = sb("col", [P, LCOLS + 8])
        tok = sb("tok", [P, 120])
        TK = Area(tok, 120)
        ab = TK.take(TT, 8)
        beta, gt, zt, Gc, eGc, eRc, bG = (TK.take(TT, 4) for _ in range(7))
        glast = TK.take(4, 4)
        wi = TK.take(TT, 4)
        hlast = TK.take(2, NCH)
        m8k = TK.take(TT, 8)
        gated = A3.view[:, 4096:4096 + FFT * T].rearrange("p (f t) -> p f t", f=FFT)
        gcv = A3.view[:, 10240:10240 + 2048].rearrange("p (b j t) -> p b j t", b=2, j=4)
        fT = A3.view[:, 12288:12288 + 2048].rearrange("p (k t) -> p k t", k=KT)
        fsq = A3.view[:, 14336:14336 + 2048].rearrange("p (k t) -> p k t", k=KT)
        rs = A3.view[:, 16384:16384 + 256]
        rsb = args.rearrange("p a b t -> p (a b t)")[:, 0:2048]
        outt = fT.rearrange("p k t -> p (k t)").rearrange("p (t d) -> p t d", t=TT)

        def cl(name, j=0, n=1):
            a = row_at(ROWS_B, name) + j
            return col[:, a:a + n]

        def ffn_tap(j, f):
            return col[:, NB + j * 2 * FFT + f:NB + j * 2 * FFT + f + 1]

        PARAMS = [(cst[:, :], W["consts"])]
        at = 0
        for name, n in ROWS_A:
            PARAMS.append((rowsA[at:at + n, :], W[name].rearrange(
                {1: "(r p) -> r p", 2: "a (r p) -> (a r) p"}[len(W[name].shape)], p=P)))
            at += n
        for l in range(LAYERS):
            at = 0
            for name, n in ROWS_B:
                v = W[name][l]
                if name == "dn_conv_2":
                    v = v.rearrange("a (r p) -> (a r) p", p=P)
                elif name != "hg_norm_2":
                    v = v.rearrange("(r p) -> r p", p=P)
                if name == "hg_norm_2":
                    for i in range(2):
                        PARAMS.append((rowsB[at:at + 1, l, i * 64:(i + 1) * 64], v.rearrange("(r p) -> r p", r=1)))
                else:
                    PARAMS.append((rowsB[at:at + n, l, :], v))
                at += n
            v = W["ffn_conv_2"][l].rearrange("a (r p) -> (a r) p", p=P)
            PARAMS.append((rowsB[NB:P, l, :], v[0:NC_HEAD, :]))
            PARAMS.append((rowsC[:, l, :], v[NC_HEAD:NC3, :]))
            for i, name in enumerate(("dn_a_log_2", "dn_dt_bias_2")):
                PARAMS.append((logs[:, l, 4 * i:4 * i + 4], W[name][l].partition_broadcast(P)))
        PARAMS.append((wlr, W["w_in"][0][:, LR0:LR0 + 32].rearrange("(k p) n -> p k n", p=P)))
        PARAMS.append((poolw, W["pool_w"][0].rearrange("g c e -> c g e")))
        PARAMS.append((a2[0:16, 0, :], W["gla_a2_f"][0]))
        PARAMS.append((a2[16:32, 1, :], W["gla_a2_b"][0]))
        N_PARAM = len(PARAMS)

        def cols(w, a, n=512):
            return w[:, a:a + n].rearrange("(k p) n -> p k n", p=P)

        wmod, win = W["w_mod"][0], W["w_in"][0]
        SL1 = [("mod", j, cols(wmod, 512 * j)) for j in range(4)]
        SL1 += [("k", 0, cols(win, K0)), ("v", 0, cols(win, V0)), ("v", 1, cols(win, V0 + 512)),
                ("q", 0, cols(win, Q0)), ("g", 0, cols(win, G0)), ("mod", 4, cols(wmod, 2048)),
                ("g", 1, cols(win, G0 + 512)), ("mod", 5, cols(wmod, 2560)), ("u", 0, cols(win, U0))]
        for j in range(4):
            SL1 += [("mod", 6 + j, cols(wmod, 3072 + 512 * j)), ("gate", j, cols(win, GT0 + 512 * j))]
        SL1 += [("mod", 10, cols(wmod, 5120)), ("mod", 11, cols(wmod, 5632)),
                ("pbr", 0, W["w_pool_br"][0].rearrange("(k p) n -> p k n", p=P)),
                ("gbr", 0, cols(W["w_gla_br"][0], 0)), ("gbr", 1, cols(W["w_gla_br"][0], 512)),
                ("wo", 0, cols(W["w_o"][0], 0)), ("wo", 1, cols(W["w_o"][0], 512))]
        where1 = {(n, j): i for i, (n, j, _) in enumerate(SL1)}
        last_unit1 = {}

        def lw(name, L, r0, r1, c0, c1):
            return W[name][bass.ds(L, 1), r0:r1, c0:c1].rearrange("a (k p) n -> p (a k) n", p=P)

        SL3 = []
        for name, a, b_ in (("aq", AQ0, AK0), ("ak", AK0, AV0), ("av", AV0, AZ0), ("az", AZ0, AB0), ("b", AB0, BQI0),
                            ("bi", BQI0, CQ0), ("cqf", CQ0, CI0), ("cig", CI0, CI0 + 512)):
            SL3.append((name, 0, [("w_in_2", 0, D, a, b_, 0)]))
        for j in range(2):
            SL3.append(("out", j, [("w_out_2", 0, D, 512 * j, 512 * j + 512, 0)]))
        for j in range(FFT // 2):
            SL3.append(("up", j, [("ffn_w_up_2", 0, D, 256 * j, 256 * j + 256, 0),
                                  ("ffn_w_up_2", 0, D, D_FF + 256 * j, D_FF + 256 * j + 256, 256)]))
        for j in range(0, FFT, 4):
            SL3.append(("down", j // 4, [("ffn_w_down_2", j * P, min(j + 4, FFT) * P, 0, D, 0)]))
        where3 = {(n, j): i for i, (n, j, _) in enumerate(SL3)}
        loads3, total3 = [], [0, 0, 0]
        for i, (_, _, parts) in enumerate(SL3):
            total3[i % 3] += 16 * len(parts)
            loads3.append(total3[i % 3])
        last_unit3 = {}

        KV_UNITS = (((0, 0), (1, 2)), ((0, 1), (1, 3)), ((0, 2),), ((1, 1),))

        def slot(i, k=KT):
            return ring[:, i % 3, :].rearrange("p (k n) -> p k n", k=k)

        block = ctx.enter_context(nc.Block())

        @block.tensor
        def _(pe):
            mm = nc.tensor.matmul

            def tiles(ph, key, parts, K, start=0):
                b = ph.bank(pe, key)
                for place, lhsT, rhs in parts:
                    for k in range(K):
                        last = mm(PS[:, b, place] if not isinstance(place, tuple) else PS[place[0], b, place[1]],
                                  lhsT(k), rhs(k), start=(k == 0), stop=(k == K - 1))
                last.then_inc(psum_full, 1)

            def slab(name, j, k=KT):
                i = where1[(name, j)]
                pe.wait_ge(wl[i % 3], 16 * (i // 3 + 1))
                return slot(i, k)

            pe.wait_ge(params_in, 16 * N_PARAM)
            b = ph1.bank(pe, "colsA")
            nc.tensor.transpose(PS[:, b, 0:NA], rowsA[:, :], C("ident")[0:NA, 0:NA]).then_inc(psum_full, 1)
            b = ph1.bank(pe, "colsL")
            for l in range(LAYERS):
                nc.tensor.transpose(PS[:, b, l * LCOLS:l * LCOLS + P], rowsB[:, l, :], C("ident"))
                n = NC3 - NC_HEAD
                last = nc.tensor.transpose(PS[:, b, l * LCOLS + P:(l + 1) * LCOLS], rowsC[:, l, :],
                                           C("ident")[0:n, 0:n])
            last.then_inc(psum_full, 1)
            pe.wait_ge(x_in, 32)
            for s, name in enumerate(("ctxT", "xT")):
                for kp in range(KT // 2):
                    b = ph1.bank(pe, (name, kp))
                    for k in (0, 1):
                        for t in range(TT):
                            last = nc.tensor.transpose(PS[:, b, k * T + t * P:k * T + (t + 1) * P],
                                                       xraw[:, s, t, (2 * kp + k) * P:(2 * kp + k + 1) * P], C("ident"))
                    last.then_inc(psum_full, 1)
            pe.wait_ge(S("squares"), 2)
            tiles(ph1, "ms", [(slice(0, 512), lambda k: C("ones"), lambda k: sqb[:, k, :])], KT)

            def modulation(j):
                b = ph1.bank(pe, ("mod", j))
                w = slab("mod", j)
                for f in range(4):
                    for k in range(KT):
                        last = mm(PS[:, b, 2 * f:2 * f + 2], w[:, k, f * P:(f + 1) * P], csil[:, k, :],
                                  start=(k == 0), stop=(k == KT - 1))
                last.then_inc(psum_full, 1)
                last_unit1[where1[("mod", j)]] = ("mod", j)

            pe.wait_ge(S("silu_c"), 1)
            for j in range(4):
                modulation(j)

            pe.wait_ge(S("h1_ready"), 16)

            def project(name, j, key, rhs, ntile=4, k=KT):
                w = slab(name, j, k)
                n = rhs(0).shape[-1]
                per = 512 // n
                for g in range(ntile // per):
                    tiles(ph1, (key, j, g), [
                        (slice(i * n, (i + 1) * n), lambda k, f=g * per + i: w[:, k, f * P:(f + 1) * P], rhs)
                        for i in range(per)], k)
                last_unit1[where1[(name, j)]] = (key, j, ntile // per - 1)

            hx = lambda k: hboth[:, k, T:2 * T]
            project("k", 0, "k", lambda k: hboth[:, k, :])
            for j in range(2):
                w = slab("v", j)
                for t in range(4):
                    tiles(ph1, ("v", j, t), [(slice(0, 512), lambda k: hboth[:, k, t * P:(t + 1) * P],
                                              lambda k: w[:, k, :])], KT)
                last_unit1[where1[("v", j)]] = ("v", j, 3)
            tiles(ph1, "lr", [((slice(0, 32), slice(0, 512)), lambda k: wlr[:, k, :], lambda k: hboth[:, k, :])], KT)
            ph1.freed(pe, "lr")
            for d in range(2):
                for h in range(GH):
                    tiles(ph1, ("z", d, h), [(slice(0, 512), lambda k: a2[0:32, d, h * P:(h + 1) * P],
                                              lambda k: lrT[0:32, :])], 1)
            project("q", 0, "q", hx)
            project("g", 0, "g", hx)
            modulation(4)
            project("g", 1, "g", hx)
            modulation(5)

            def by_token(name, src, waits):
                for d in range(2):
                    pe.wait_ge(S(waits), d + 1)
                    for t in range(TT):
                        b = ph1.bank(pe, (name, d, t))
                        for h in range(GH):
                            last = nc.tensor.transpose(PS[:, b, h * P:(h + 1) * P], src[d][:, h, t * P:(t + 1) * P],
                                                       C("ident"))
                        last.then_inc(psum_full, 1)

            by_token("krc", (e1, e2), "krc_ready")
            project("u", 0, "u", hx)
            for d in range(2):
                for t in range(TT):
                    ph1.freed(pe, ("krc", d, t))
            for d in range(2):
                for hp in range(2):
                    tiles(ph1, ("s0", d, hp), [
                        (slice(i * 256, (i + 1) * 256),
                         lambda t, h=2 * hp + i: krt[:, d, t, h * P:(h + 1) * P],
                         lambda t, h=2 * hp + i: vtok[:, t, h * 256:(h + 1) * 256]) for i in range(2)], TT)
            modulation(6)
            by_token("krx", (e1, e2), "krx_ready")
            pe.wait_ge(S("qdki_ready"), 4)
            for h in range(GH):
                b = ph1.bank(pe, ("sc", h))
                for d in range(2):
                    for t in range(TT):
                        at = slice(t * P, (t + 1) * P)
                        o = (2 * d + t) * P
                        last = mm(PS[:, b, o:o + P], ki[:, d, h, at], qd[:, d, h, at], start=True, stop=True)
                last.then_inc(psum_full, 1)
            for d in range(2):
                for t in range(TT):
                    ph1.freed(pe, ("krx", d, t))
            for h in range(GH):
                for n, group in enumerate(KV_UNITS):
                    b = ph1.bank(pe, ("kv", h, n))
                    for d, c in group:
                        r = slice(CH * (c % 2), CH * (c % 2) + CH)
                        last = mm(PS[:, b, d * 256:(d + 1) * 256], krt[r, d, c // 2, h * P:(h + 1) * P],
                                  vtok[r, 2 + c // 2, h * 256:(h + 1) * 256], start=True, stop=True)
                    last.then_inc(psum_full, 1)
                pe.wait_ge(S("sc_ready"), h + 1)
                for n in (2, 3):
                    ph1.freed(pe, ("kv", h, n))
                b = ph1.bank(pe, ("o", h))
                for vt in range(2):
                    for t in range(TT):
                        o = vt * T + t * P
                        vs = slice(h * 256 + vt * P, h * 256 + (vt + 1) * P)
                        mm(PS[:, b, o:o + P], vtok[:, 2 + t, vs], scT[:, h, t, :], start=(vt == 0 and t == 0),
                           stop=False, skip_group_check=True)
                        for c in (2 * t, 2 * t + 1):
                            for d in range(2):
                                n = c if d == 0 else NCH - 1 - c
                                st = (s0[:, d, h, vt * P:(vt + 1) * P] if n == 0 else
                                      Sx[:, h % 2, d, n - 1, vt * P:(vt + 1) * P])
                                oo = o + CH * (c % 2)
                                last = mm(PS[:, b, oo:oo + CH], st, qd[:, d, h, c * CH:(c + 1) * CH],
                                          start=False,
                                          stop=(vt == 1 and c == NCH - 1 and d == 1), skip_group_check=True)
                last.then_inc(psum_full, 1)
            for j in range(4):
                if j:
                    modulation(6 + j)
                project("gate", j, "gate", hx)
            modulation(10)
            modulation(11)
            pe.wait_ge(S("osq_ready"), 1)
            for hp in range(2):
                tiles(ph1, ("oms", hp), [(slice(i * T, (i + 1) * T), lambda k: C("ones"),
                                          lambda k, h=2 * hp + i: osq[:, 2 * h + k, :]) for i in range(2)], 2)
            pe.wait_ge(S("pooled_ready"), 1)
            for g in range(2):
                tiles(ph1, ("yp", g), [(slice(i * T, (i + 1) * T), lambda k, f=2 * g + i: poolw[:, f, :],
                                        lambda k, f=2 * g + i: pooled[:, f, :]) for i in range(2)], 1)
            for g in range(2):
                ph1.freed(pe, ("yp", g))
            w = slab("pbr", 0, 4)
            for g in range(4):
                tiles(ph1, ("pbr", g), [(slice(i * T, (i + 1) * T), lambda k, f=2 * g + i: w[:, k, f * P:(f + 1) * P],
                                         lambda k: yp[:, k, :]) for i in range(2)], 4)
            last_unit1[where1[("pbr", 0)]] = ("pbr", 3)
            pe.wait_ge(S("og_ready"), 1)
            for j in range(2):
                project("gbr", j, "gbr", lambda k: oT[:, k, :])
            pe.wait_ge(S("mixed_ready"), 4)
            for j in range(2):
                project("wo", j, "wo", lambda k: mixed[:, k, :])
            meet(pe, "pe")

            pe.wait_ge(S("sq2"), 1)
            tiles(ph2, "ms2", [(slice(0, T), lambda k: C("ones"), lambda k: h2n[:, k, :])], KT)
            pe.wait_ge(S("h2_ready"), KT)
            pe.wait_ge(S("router_in"), 64)
            b = ph2.bank(pe, "route")
            for t in range(TT):
                for k in range(KT):
                    mm(PS[:, b, t * 64:t * 64 + 36], h2T[:, k, t * P:(t + 1) * P], rw[:, k, :], start=(k == 0), stop=False)
                last = mm(PS[:, b, t * 64:t * 64 + 36], C("ones")[0:1, :], rb[0:1, :], start=False, stop=True)
            last.then_inc(psum_full, 1)
            for t in range(TT):
                for g in range(2):
                    b = ph2.bank(pe, ("h2t", t, g))
                    for k in range(4):
                        last = nc.tensor.transpose(PS[:, b, k * P:(k + 1) * P], h2T[:, 4 * g + k, t * P:(t + 1) * P],
                                                   C("ident"))
                    last.then_inc(psum_full, 1)
            pe.wait_ge(S("chosen"), 1)
            b = ph2.bank(pe, "rank")
            mm(PS[:, b, 0:32], C("before"), m32[0][:, 0], start=True, stop=True)
            mm(PS[:, b, 32:64], C("ones"), m32[0][:, 0], start=True, stop=False)
            mm(PS[:, b, 32:64], C("before"), m32[0][:, 1], start=False, stop=True)
            mm(PS[:, b, 64:96], C("ones"), m32[0][:, 0], start=True, stop=False)
            mm(PS[:, b, 64:96], C("ones"), m32[0][:, 1], start=False, stop=True).then_inc(psum_full, 1)
            for key in list(ph2.units):
                ph2.freed(pe, key)
            pe.wait_ge(S("moe_zeroed"), 2)
            for b in range(4):
                last = mm(PS[:, b, :], ytok[:, 0:P], ytok[:, 0:512], start=True, stop=True)
                if b in (2, 3):
                    last.then_inc(S("gathered") if b == 2 else S("pt_turned"), 1)
            pe.wait_ge(S("rounds_ready"), 1)
            rounds = pe.value_load(rounds_i[0:1, 0:1])

            def scatter():
                for f in range(KT):
                    last = mm(PS[:, f // 2, (f % 2) * T:(f % 2 + 1) * T], ytok[:, f * P:(f + 1) * P], PT,
                              start=False, stop=False, skip_group_check=True)
                return last

            def expert_slab(s, k):
                return ring[:, s, :].rearrange("p (k n) -> p k n", k=k)

            with pe.Fori(0, rounds) as r:
                with pe.Fori(0, PAIRS) as p:
                    i1 = pe.snap(r * PAIRS + p + 1)
                    i2 = pe.snap(i1 * 2)
                    pe.wait_ge(S("sel_ready"), i1)
                    pe.wait_ge(S("hid_ready"), i2 - 1)
                    for f in range(KT):
                        for t in range(TT):
                            last = mm(PS[:, 4 + f // 4, (f % 4) * P:(f % 4 + 1) * P], h2t[:, t, f * P:(f + 1) * P],
                                      sel[:, t].rearrange("p e s -> p (e s)"), start=(t == 0), stop=(t == TT - 1))
                    last.then_inc(S("gathered"), 1)
                    pe.wait_ge(S("y_lo"), i1)
                    pe.wait_ge(S("y_hi"), i1)
                    pe.wait_ge(S("pt_ready"), i1)
                    scatter()
                    pe.wait_ge(S("selw_ready"), i1)
                    for t in range(TT):
                        last = nc.tensor.transpose(PS[:, 6, t * P:(t + 1) * P],
                                                   selw[:, t].rearrange("p e s -> p (e s)"), C("ident"))
                    last.then_inc(S("pt_turned"), 1)
                    pe.wait_ge(S("hg_lo"), i1)
                    pe.wait_ge(S("hg_hi"), i1)
                    for e in range(2):
                        for j in range(2):
                            pe.wait_ge(ml[2 * e + j], i1 * 16)
                            w = expert_slab(2 * e + j, KT)
                            for f in range(4):
                                o = j * 256 + f * SLOTS
                                for k in range(KT):
                                    last = mm(PS[:, 4 + e, o:o + SLOTS], w[:, k, f * P:(f + 1) * P],
                                              hg[:, k, e * SLOTS:(e + 1) * SLOTS], start=(k == 0), stop=(k == KT - 1))
                            last.then_inc(w1_read if j == 0 else h_ready, 1)
                    pe.wait_ge(S("pt_ready"), i1 + 1)
                    for e in range(2):
                        pe.wait_ge(S("hid_ready"), i2 + e)
                        pe.wait_ge(ml[4 + e], i1 * 16)
                        w = expert_slab(4 + e, 4)
                        for n in range(2):
                            for f in range(4):
                                last = mm(PS[e * SLOTS:(e + 1) * SLOTS, 6 + n, :], hid[:, e, f, :],
                                          w[:, f, n * 512:(n + 1) * 512], start=(f == 0), stop=(f == 3))
                        last.then_inc(w2_read if e == 0 else y_full, 1)
            pe.wait_ge(S("evacuated"), 2)
            scatter().then_inc(S("moe_out"), 1)
            pe.wait_ge(S("sq3"), 1)
            for k in range(KT):
                last = mm(PS[:, 4, 0:T], C("ones"), h2n[:, k, :], start=(k == 0), stop=(k == KT - 1))
            last.then_inc(S("ms3"), 1)
            meet(pe, "pe")

            half = lambda i: slice(i * T, (i + 1) * T)

            def slab3(name, j=0, k=KT, n=512):
                i = where3[(name, j)]
                pe.wait_ge(ll[i % 3], loads3[i])
                return ring[:, i % 3, 0:k * n].rearrange("p (k n) -> p k n", k=k)

            def by_feature(w, key, c0, ntile, rhs, K=KT):
                for g in range(0, ntile, 2):
                    tiles(ph3, (key, g // 2), [(half(i), lambda k, f=g + i: w[:, k, c0 + f * P:c0 + (f + 1) * P], rhs)
                                               for i in range(2)], K)

            def square_sums(key, src, stage, n=1):
                pe.wait_ge(S(stage), n)
                tiles(ph3, key, [(half(0), lambda k: C("ones"), lambda k: src[:, k, :])], KT)

            def turn(key, parts):
                b = ph3.bank(pe, key)
                for i, v in enumerate(parts):
                    last = nc.tensor.transpose(PS[:, b, i * P:(i + 1) * P], v, C("ident"))
                last.then_inc(psum_full, 1)

            with pe.Fori(0, LAYERS) as L:
                h = lambda k: hT[:, k, :]
                square_sums("ms0", sc3, "sq_x")
                pe.wait_ge(S("h_ready3"), 1)
                for name in ("aq", "ak", "av", "az"):
                    by_feature(slab3(name), name, 0, 4, h)
                    last_unit3[where3[(name, 0)]] = (name, 1)
                w = slab3("b", n=BQI0 - AB0)

                def by_tok(w, c0, n, t):
                    return (lambda k: hT[:, k, t * P:(t + 1) * P], lambda k: w[:, k, c0:c0 + n])

                tiles(ph3, "ab", [(slice(t * 8, t * 8 + 8), *by_tok(w, 0, 8, t)) for t in range(TT)], KT)
                by_feature(w, "bq", BQ0 - AB0, 2, h)
                twice = lambda w, c0: [((slice(i * 64, i * 64 + 64), half(0)), lambda k: w[:, k, c0:c0 + 64], h)
                                       for i in range(2)]
                tiles(ph3, "bk", twice(w, BK0 - AB0), KT)
                tiles(ph3, "bv", [(slice(t * SAD, (t + 1) * SAD), *by_tok(w, BV0 - AB0, SAD, t)) for t in range(TT)], KT)
                last_unit3[where3[("b", 0)]] = "bv"
                w = slab3("bi", n=CQ0 - BQI0)
                by_feature(w, "qi", 0, 2, h)
                tiles(ph3, "ki", twice(w, BKI0 - BQI0), KT)
                tiles(ph3, "wi", [(slice(t * 4, t * 4 + 4), *by_tok(w, BWI0 - BQI0, 4, t)) for t in range(TT)], KT)
                last_unit3[where3[("bi", 0)]] = "wi"
                pe.wait_ge(S("qk_squares"), 1)
                for g in range(4):
                    tiles(ph3, ("l2", g), [(half(i), lambda k: C("ones"), lambda k, f=2 * g + i: sc3[:, f, :])
                                           for i in range(2)], 1)
                pe.wait_ge(S("g_ready"), 1)
                b = ph3.bank(pe, "G")
                for i, m in enumerate(("incl", "blk")):
                    for t in range(TT):
                        o = (2 * i + t) * 4
                        last = mm(PS[:, b, o:o + 4], C(m), gt[:, t, :], start=True, stop=True)
                last.then_inc(psum_full, 1)
                pe.wait_ge(S("gx_ready"), 2)
                for name, src, m in (("Gb", gx, "incl"), ("bb", bx, "ident")):
                    for g in range(2):
                        tiles(ph3, (name, g), [(slice((2 * i + t) * P, (2 * i + t + 1) * P),
                                                lambda k, i=i, t=t: src[:, 2 * g + i, t, :], lambda k: C(m))
                                               for i in range(2) for t in range(TT)], 1)
                w = slab3("cqf")
                by_feature(w, "cq", 0, 2, h)
                by_feature(w, "cf", 256, 2, h)
                last_unit3[where3[("cqf", 0)]] = ("cf", 0)
                pe.wait_ge(S("qk_normed"), 2)
                qn, kn, vn = cs[:, 0:4, :], cs[:, 4:8, :], cs[:, 8:12, :]
                at = lambda t: slice(t * P, (t + 1) * P)
                quads = lambda f: [(slice((2 * i + t) * P, (2 * i + t + 1) * P), *f(i, t)) for i in range(2) for t in range(TT)]
                for name, r_ in (("kk", kn), ("qk", qn)):
                    for g in range(2):
                        tiles(ph3, (name, g), quads(lambda i, t: (lambda k: kn[:, 2 * g + i, at(t)],
                                                                  lambda k: r_[:, 2 * g + i, at(t)])), 1)
                for t in range(TT):
                    turn(("kt", t), [kn[:, h_, at(t)] for h_ in range(DNH)])
                for t in range(TT):
                    turn(("vt", t), [vn[:, h_, at(t)] for h_ in range(DNH)])
                for g in range(2):
                    pe.wait_ge(S("B_ready"), g + 1)
                    turn(("Z", 0, g), [BT[0][:, 2 * g + i, t, :] for i in range(2) for t in range(TT)])
                w = slab3("cig")
                tiles(ph3, "ci", [(slice(t * HG, (t + 1) * HG), *by_tok(w, 0, HG, t)) for t in range(TT)], KT)
                by_feature(w, "cg", 256, 2, h)
                last_unit3[where3[("cig", 0)]] = ("cg", 0)
                for lv in range(1, 6):
                    for g in range(2):
                        pe.wait_ge(S("B_ready"), 2 * lv + g + 1)
                        if lv == 1:
                            ph3.freed(pe, ("Z", 0, g))
                        else:
                            ph3.freed(pe, ("XZ", lv - 1, g))
                        tiles(ph3, ("Z", lv, g), quads(lambda i, t: (lambda k: BT[lv % 2][:, 2 * g + i, t, :],
                                                                     lambda k: XI[:, 2 * g + i, t, :])), 1)
                    for g in range(2):
                        ph3.freed(pe, ("Z", lv, g))
                        if lv == 1:
                            pe.wait_ge(S("X0T_ready"), g + 1)
                        else:
                            ph3.freed(pe, ("ZX", lv - 1, g))
                        if lv < 5:
                            tiles(ph3, ("XZ", lv, g), quads(lambda i, t: (lambda k: XIT[:, 2 * g + i, t, :],
                                                                          lambda k: Z[:, 2 * g + i, t, :])), 1)
                        tiles(ph3, ("ZX", lv, g), quads(lambda i, t: (lambda k: Z[:, 2 * g + i, t, :],
                                                                      lambda k: XIT[:, 2 * g + i, t, :])), 1)
                for g in range(2):
                    ph3.freed(pe, ("ZX", 5, g))
                pe.wait_ge(S("kvb_ready"), 6)
                for t in range(TT):
                    tiles(ph3, ("u0", t), [(slice(i * P, (i + 1) * P), lambda k, i=i: XIT[:, i, t, :],
                                            lambda k, i=i: vb[:, t, i, :]) for i in range(DNH)], 1)
                for g in range(2):
                    tiles(ph3, ("wk", g), quads(lambda i, t: (lambda k: kb[:, t, 2 * g + i, :],
                                                              lambda k: XIT[:, 2 * g + i, t, :])), 1)
                for t in range(TT):
                    ph3.freed(pe, ("u0", t))
                for g in range(2):
                    ph3.freed(pe, ("wk", g))
                for key in (("qi", 0), "ki", ("bq", 0), "bk"):
                    ph3.freed(pe, key)
                pe.wait_ge(S("qdec_ready"), 1)

                def pairs_by_rows(key, lhs, rhs, t):
                    for par in range(2):
                        r_ = slice(64 * par, 64 * par + 64)
                        tiles(ph3, (key, t, par), [(half(i), lambda k, i=i: lhs[r_, i, at(t)], lambda k: rhs[r_, :])
                                                   for i in range(2)], 1)

                for n in range(NCH):
                    t, r_ = n // 2, slice(CH * (n % 2), CH * (n % 2) + CH)
                    if n:
                        ph3.freed(pe, ("dS", n - 1))
                        tiles(ph3, ("wS", n), [((r_, slice(i * P, (i + 1) * P)),
                                                lambda k, i=i: wk[:, i, n * CH:(n + 1) * CH],
                                                lambda k, i=i: Sd[n - 1][:, i, :]) for i in range(DNH)], 1)
                        ph3.freed(pe, ("wS", n))
                    if n < NCH - 1:
                        tiles(ph3, ("dS", n), [(slice(i * P, (i + 1) * P), lambda k, i=i: kd[r_, t, i, :],
                                                lambda k, i=i: u[r_, t, i, :]) for i in range(DNH)], 1)
                    if n < 2:
                        pairs_by_rows("is", qi, kii, n)
                for g in range(2):
                    ph3.freed(pe, ("qk", g))
                for g in range(2):
                    b = ph3.bank(pe, ("oa", g))
                    first = True
                    for i in range(2):
                        f = 2 * g + i
                        for t in range(TT):
                            mm(PS[:, b, i * T + t * P:i * T + (t + 1) * P], u[:, t, f, :], QK[:, f, t, :], start=first,
                               stop=False, skip_group_check=True)
                            first = False
                        for n in range(1, NCH):
                            o = i * T + n * CH
                            last = mm(PS[:, b, o:o + CH], Sd[n - 1][:, f, :], eG[:, f, n * CH:(n + 1) * CH], start=False,
                                      stop=(i == 1 and n == NCH - 1), skip_group_check=True)
                    last.then_inc(psum_full, 1)
                for t in range(TT):
                    pairs_by_rows("lg", qb, kbb, t)
                pe.wait_ge(S("p_ready"), TT)
                for i in range(SAH):
                    turn(("pt", i), [pr[:, t, i, at(s_)] for s_ in range(TT) for t in range(TT)])
                for i in range(SAH):
                    ph3.freed(pe, ("pt", i))
                ph3.freed(pe, "bv")
                b = ph3.bank(pe, "ob")
                for par in range(2):
                    for i in range(2):
                        for s_ in range(TT):
                            last = mm(PS[64 * par:64 * par + 64, b, half(i)], vtk[:, s_, :],
                                      pT[:, 2 * i + par, s_, :], start=(s_ == 0), stop=(s_ == TT - 1))
                last.then_inc(psum_full, 1)
                for lv in range(3):
                    pe.wait_ge(S("qk_levels"), 2)
                    for par in range(2):
                        r_ = slice(64 * par, 64 * par + 64)
                        tiles(ph3, ("hs", lv, par), [
                            (slice((2 * i + t) * P, (2 * i + t + 1) * P),
                             lambda k, i=i, t=t: args[r_, lv, 1, i * T + t * P:i * T + (t + 1) * P],
                             lambda k, i=i, t=t: args[r_, lv, 0, i * T + t * P:i * T + (t + 1) * P])
                            for i in range(2) for t in range(TT)], 1)
                pe.wait_ge(S("kdec_ready"), 1)
                turn("hkt", [eR[:, i, at(t)] for t in range(TT) for i in range(2)])
                ph3.freed(pe, "hkt")
                ph3.freed(pe, "ci")
                for par, ns in ((0, (0, 2)), (1, (1,))):
                    tiles(ph3, ("hS", par), [
                        (slice((2 * j + i) * P, (2 * j + i + 1) * P),
                         lambda k, n=n, i=i: kdt[64 * par:64 * par + 64, n // 2, i * P:(i + 1) * P],
                         lambda k, n=n, i=i: cit[64 * par:64 * par + 64, n // 2, i * P:(i + 1) * P])
                        for j, n in enumerate(ns) for i in range(2)], 1)
                pe.wait_ge(S("Sh_ready"), 1)
                b = ph3.bank(pe, "oc")
                for i in range(2):
                    for n in range(1, NCH):
                        o = i * T + n * CH
                        mm(PS[:, b, o:o + CH], Sh[:, n - 1, i, :], eB[:, i, n * CH:(n + 1) * CH],
                           start=(i == 0 and n == 1), stop=False, skip_group_check=True)
                pe.wait_ge(S("AT_ready"), 2)
                for par in range(2):
                    for i in range(2):
                        for t in range(TT):
                            last = mm(PS[64 * par:64 * par + 64, b, i * T + t * P:i * T + (t + 1) * P],
                                      cit[:, t, (2 * i + par) * 64:(2 * i + par + 1) * 64], AT[:, par, i, t, :],
                                      start=False, stop=(par == 1 and i == 1 and t == TT - 1), skip_group_check=True)
                last.then_inc(psum_full, 1)
                pe.wait_ge(S("oa_squares"), 1)
                for g in range(2):
                    tiles(ph3, ("oam", g), [(half(i), lambda k: C("ones"), lambda k, f=2 * g + i: sc3[:, f, :])
                                            for i in range(2)], 1)
                pe.wait_ge(S("oc_squares"), 1)
                tiles(ph3, "ocm", [(half(i), lambda k: C("blk"), lambda k, i=i: sc3[:, 6 + i, :]) for i in range(2)], 1)
                ph3.freed(pe, "ob")
                pe.wait_ge(S("oa_ready"), 1)
                pe.wait_ge(S("oc_ready"), 1)
                for j in range(2):
                    by_feature(slab3("out", j), ("out", j), 0, 4, lambda k: cat[:, k, :])
                    last_unit3[where3[("out", j)]] = (("out", j), 1)
                square_sums("ms1", fsq, "sq_mix")
                square_sums("ms2", sc3, "sq_x2")
                pe.wait_ge(S("h_ready3"), 2)
                for j in range(FFT // 2):
                    w = slab3("up", j)
                    w2 = ring[:, where3[("up", j)] % 3, :].rearrange("p (v k n) -> p v k n", v=2, k=KT)
                    for v in range(2):
                        tiles(ph3, ("up", j, v), [(half(i), lambda k, i=i: w2[:, v, k, i * P:(i + 1) * P], h)
                                                  for i in range(2)], KT)
                    last_unit3[where3[("up", j)]] = ("up", j, 1)
                banks = [ph3.bank(pe, ("down", g)) for g in range(4)]
                for j in range(0, FFT, 4):
                    kk_ = min(4, FFT - j)
                    w = slab3("down", j // 4, kk_, D)
                    pe.wait_ge(S("gated"), min(j + 4, FFT) // 2)
                    for f in range(KT):
                        for k in range(kk_):
                            last = mm(PS[:, banks[f // 2], half(f % 2)], w[:, k, f * P:(f + 1) * P], gated[:, j + k, :],
                                      start=(f % 2 == 0 and j + k == 0), stop=(f % 2 == 1 and j + k == FFT - 1),
                                      skip_group_check=True)
                            if j + k == FFT - 1 and f % 2 == 1:
                                last.then_inc(psum_full, 1)
                    if j + 4 < FFT:
                        last.then_inc(S("down_read"), 1)
                square_sums("ms3", fsq, "sq_f")
                meet(pe, "pe")
            for t in range(TT):
                for g in range(2):
                    for k in range(4):
                        last = nc.tensor.transpose(PS[:, 2 * t + g, k * P:(k + 1) * P],
                                                   xT[:, 4 * g + k, t * P:(t + 1) * P], C("ident"))
                    last.then_inc(S("out_turned"), 1)

        @block.sync
        def _(sp):
            for s, name in enumerate(("ctx", "x")):
                sp.dma_start(xraw[:, s, :, :], W[name][0].rearrange("(t p) d -> p t d", p=P)).then_inc(x_in, 16)
            for i, (name, j, src) in enumerate(SL1):
                if i >= 3:
                    before = i - 3
                    ph1.read(sp, last_unit1[before])
                sp.dma_start(slot(i, src.shape[1]), src).then_inc(wl[i % 3], 16)
            meet(sp, "sp")
            sp.dma_start(rw[:, :, 0:N_GRP], W["router_grp_w"][0].rearrange("(k p) n -> p k n", p=P)).then_inc(S("router_in"), 16)
            sp.dma_start(rw[:, :, N_GRP:], W["router_exp_w"][0].rearrange("(k p) n -> p k n", p=P)).then_inc(S("router_in"), 16)
            sp.dma_start(rb[0:1, 0:N_GRP], W["router_grp_b"]).then_inc(S("router_in"), 16)
            sp.dma_start(rb[0:1, N_GRP:], W["router_exp_b"]).then_inc(S("router_in"), 16)

            def expert_weights(e):
                for name, s, o, k in (("moe_w1", 0, 0, KT), ("moe_w3", 1, 0, KT), ("moe_w1", 2, 1, KT),
                                      ("moe_w3", 3, 1, KT), ("moe_w2", 4, 0, 4), ("moe_w2", 5, 1, 4)):
                    yield s, W[name][0][bass.ds(e + o, 1)].rearrange("a (k p) n -> p (a k) n", p=P), k

            def fetch(s, src, k):
                sp.dma_start(ring[:, s, :].rearrange("p (k n) -> p k n", k=k), src).then_inc(ml[s], 16)

            for s, src, k in expert_weights(0):
                fetch(s, src, k)
            sp.wait_ge(S("rounds_ready"), 1)
            visits = sp.snap(sp.value_load(rounds_i[0:1, 0:1]) * PAIRS)
            with sp.Fori(1, visits) as v:
                reads = ((w1_read, 1), (h_ready, 1), (w1_read, 0), (h_ready, 0), (w2_read, None), (y_full, None))
                for (s, src, k), (q, back) in zip(expert_weights((v % PAIRS) * 2), reads):
                    sp.wait_ge(q, v if back is None else v * 2 - back)
                    fetch(s, src, k)
            meet(sp, "sp")
            with sp.Fori(0, LAYERS) as L:
                for i, (name, j, parts) in enumerate(SL3):
                    if i >= 3:
                        before = i - 3
                        if before in last_unit3:
                            ph3.read(sp, last_unit3[before])
                        else:
                            sp.wait_ge(S("down_read"), SL3[before][1] + 1)
                    for q, (wn, r0, r1, c0, c1, o) in enumerate(parts):
                        k, n = (r1 - r0) // P, c1 - c0
                        base = q * k * n if len(parts) > 1 else 0
                        sp.dma_start(ring[:, i % 3, base:base + k * n].rearrange("p (k n) -> p k n", k=k),
                                     lw(wn, L, r0, r1, c0, c1)).then_inc(ll[i % 3], 16)
                meet(sp, "sp")
            sp.wait_ge(S("out_copied"), 4)
            sp.dma_start(out_T.rearrange("(t p) d -> p t d", p=P), outt).then_inc(out_done, 16)
            sp.wait_ge(out_done, 16)

        @block.scalar
        def _(act):
            A = nc.scalar.activation
            act.wait_ge(S("a2_zero"), 1)
            for dst, src in PARAMS:
                act.dma_start(dst, src).then_inc(params_in, 16)
            link = Chain(act, "act_step")

            def rsqrt_mean(view, n, src, b=None, after=None):
                ins = A(view, src, ACT.Ln, scale=1.0 / n, bias=C("eps")[0:view.shape[0], :])
                ins.then_inc(psum_free[b], 1)
                after(act)
                return A(view, view, ACT.Exp, scale=-0.5)

            act.wait_ge(S("cols_ready"), 1)
            A(lbc[:, 1, 0:2], lbc[:, 1, 0:2], ACT.Sigmoid).then_inc(S("lb_ready"), 1)
            A(csil, colsA[:, 0:16].rearrange("p (v k) -> p k v", v=2), ACT.Silu).then_inc(S("silu_c"), 1)
            for kp in range(4):
                b = ph1.read(act, ("ctxT", kp))
                A(hboth[:, 2 * kp:2 * kp + 2, 0:T], PS[:, b, :].rearrange("p (k t) -> p k t", k=2),
                  ACT.Copy).then_inc(psum_free[b], 1)
            ph1.freed(act, ("ctxT", 3))
            A(sqb[:, :, 0:T], hboth[:, :, 0:T], ACT.Square).then_inc(S("squares"), 1)
            b = ph1.read(act, "ms")
            rsqrt_mean(rstd, D, PS[:, b, :], b, lambda e: ph1.freed(e, "ms")).then_inc(S("rstd_ready"), 1)
            act.wait_ge(S("ada_ready"), 1)
            act.wait_ge(S("normed"), 2)
            for k in range(KT):
                A(hboth[:, k, 0:T], hboth[:, k, 0:T], ACT.Identity, bias=mod(0, 1, k),
                  scale=ada[:, 1, k:k + 1]).then_inc(S("h1_ready"), 1)
                A(hboth[:, k, T:2 * T], hboth[:, k, T:2 * T], ACT.Identity, bias=mod(0, 0, k),
                  scale=ada[:, 0, k:k + 1]).then_inc(S("h1_ready"), 1)
            for j in range(2):
                for t in range(4):
                    b = ph1.read(act, ("v", j, t))
                    A(vtok[:, t, j * 512:(j + 1) * 512], PS[:, b, :], ACT.Copy).then_inc(psum_free[b], 1)
            b = ph1.read(act, "lr")
            A(lrT[0:32, :], PS[0:32, b, :], ACT.Copy).then_inc(psum_free[b], 1)
            for d in range(2):
                for h in range(GH):
                    act.wait_ge(S("absz"), d * GH + h + 1)
                    link(A(cum[:, d, h, :], cum[:, d, h, :], ACT.Exp))
                    A(cum[:, d, h, :], cum[:, d, h, :], ACT.Ln, bias=C("one")).then_inc(S("lnz"), 1)
            for g in range(2):
                b = ph1.read(act, ("q", 0, g))
                A(qT[:, 2 * g:2 * g + 2, :], PS[:, b, :].rearrange("p (h t) -> p h t", h=2), ACT.Copy,
                  scale=float((GDK // GH) ** -0.5)).then_inc(psum_free[b], 1)
            for j in range(2):
                for g in range(2):
                    b = ph1.read(act, ("g", j, g))
                    A(sg[:, 4 * j + 2 * g:4 * j + 2 * g + 2, :], PS[:, b, :].rearrange("p (h t) -> p h t", h=2),
                      ACT.Silu).then_inc(psum_free[b], 1)
            inv = 1.0 / GATE_NORM
            for d, e in ((0, e1), (1, e2)):
                act.wait_ge(S("krc_arg"), d + 1)
                A(e, e, ACT.Exp, scale=inv).then_inc(S("krc_exp"), 1)
            for g in range(2):
                b = ph1.read(act, ("u", 0, g))
                A(hboth[:, 2 * g:2 * g + 2, 0:T], PS[:, b, :].rearrange("p (h t) -> p h t", h=2),
                  ACT.Copy).then_inc(psum_free[b], 1)
            act.wait_ge(S("decays"), 1)
            A(dec, lastx, ACT.Exp, scale=inv).then_inc(S("dec_ready"), 1)
            for d in range(2):
                if d:
                    act.wait_ge(S("cumb_ready"), 1)
                A(qd[:, d], cum[:, d, :, T:2 * T], ACT.Exp, scale=inv).then_inc(S("qdki_exp"), 1)
                A(ki[:, d], cum[:, d, :, T:2 * T], ACT.Exp, scale=-inv).then_inc(S("qdki_exp"), 1)
            for d, e in ((0, e1), (1, e2)):
                act.wait_ge(S("krx_arg" if d == 0 else "cumb_ready"), 1)
                A(e, e, ACT.Exp, scale=inv).then_inc(S("krx_exp"), 1)
            for d in range(2):
                for hp in range(2):
                    b = ph1.read(act, ("s0", d, hp))
                    A(s0[:, d, 2 * hp:2 * hp + 2, :], PS[:, b, :].rearrange("p (h v) -> p h v", h=2),
                      ACT.Copy).then_inc(psum_free[b], 1)
            for h in range(GH):
                b = ph1.read(act, ("o", h))
                A(oT[:, 2 * h:2 * h + 2, :], PS[:, b, :].rearrange("p (j t) -> p j t", j=2),
                  ACT.Copy).then_inc(psum_free[b], 1)
            ph1.freed(act, ("o", GH - 1))
            A(osq, oT, ACT.Square).then_inc(S("osq_ready"), 1)
            for j in range(4):
                for g in range(2):
                    b = ph1.read(act, ("gate", j, g))
                    o = 4 * j + 2 * g
                    A(gates[:, o:o + 2, :], PS[:, b, :].rearrange("p (h t) -> p h t", h=2),
                      ACT.Sigmoid).then_inc(psum_free[b], 1)
            for hp in range(2):
                b = ph1.read(act, ("oms", hp))
                orstd = e1.rearrange("p h t -> p (h t)")[:, hp * 512:(hp + 1) * 512]
                rsqrt_mean(orstd, 256, PS[:, b, :], b,
                           lambda e, hp=hp: ph1.freed(e, ("oms", hp))).then_inc(S("orstd_ready"), 1)
            meet(act, "act")

            b = ph2.read(act, "ms2")
            rsqrt_mean(rstd2, D, PS[:, b, 0:T], b, lambda e: ph2.freed(e, "ms2")).then_inc(S("rstd2_ready"), 1)
            act.wait_ge(S("normed2"), 1)
            for k in range(KT):
                A(h2T[:, k, :], h2n[:, k, :], ACT.Identity, bias=mod(3, 0, k), scale=ada[:, 2, k:k + 1])\
                    .then_inc(S("h2_ready"), 1)
            act.wait_ge(S("route_arg"), 1)
            A(m8[1], m8[0], ACT.Exp).then_inc(S("route_exp"), 1)
            for t in range(TT):
                for g in range(2):
                    b = ph2.read(act, ("h2t", t, g))
                    A(h2t[:, t, g * 512:(g + 1) * 512], PS[:, b, :], ACT.Copy).then_inc(psum_free[b], 1)
            act.wait_ge(S("route_arg"), 2)
            A(m1[3], m1[2], ACT.Exp).then_inc(S("route_exp"), 1)
            act.wait_ge(S("rounds_ready"), 1)
            rounds = act.value_load(rounds_i[0:1, 0:1])
            with act.Fori(0, rounds) as r:
                with act.Fori(0, PAIRS) as p:
                    i1 = act.snap(r * PAIRS + p + 1)
                    i2 = act.snap(i1 * 2)
                    act.wait_ge(S("gathered"), i1 + 1)
                    A(hg[:, 0:4, :], PS[:, 4, :].rearrange("p (k s) -> p k s", k=4), ACT.Copy).then_inc(S("hg_lo"), 1)
                    for e in range(2):
                        act.wait_ge(h_ready, i2 - 1 + e)
                        A(s1[:, e, :], PS[:, 4 + e, 0:256], ACT.Silu).then_inc(S("s1_ready"), 1)
                    act.wait_ge(y_full, i1)
                    A(ytok[:, 0:512], PS[:, 6, :], ACT.Copy).then_inc(S("y_lo"), 1)
            act.drain().then_inc(S("evacuated"), 1)
            act.wait_ge(S("ms3"), 1)
            link = Chain(act, "act_step")
            link(A(rstd2, PS[:, 4, 0:T], ACT.Ln, scale=1.0 / D, bias=C("eps")))
            A(rstd2, rstd2, ACT.Exp, scale=-0.5).then_inc(S("rstd3_ready"), 1)
            meet(act, "act")

            v2 = lambda v: v.rearrange("p (j t) -> p j t", j=2)
            with act.Fori(0, LAYERS) as L:
                link = Chain(act, "act_step")

                def rs3(view, n, key, width=T):
                    b = ph3.read(act, key)
                    return rsqrt_mean(view, n, PS[:, b, 0:width], b, lambda e: ph3.freed(e, key))

                def evac(key, dst, fn=ACT.Copy, **kw):
                    b = ph3.read(act, key)
                    A(dst, v2(PS[:, b, :]), fn, **kw).then_inc(psum_free[b], 1)

                rs3(rs, D, "ms0").then_inc(S("rs_ready"), 1)
                act.wait_ge(S("conv_ready"), 1)
                link(A(cs[:, 0:8, :], cs[:, 0:8, :], ACT.Silu))
                A(sc3[:, :, :], cs[:, 0:8, :], ACT.Square).then_inc(S("qk_squares"), 1)
                act.wait_ge(S("conv_ready"), 2)
                A(cs[:, 8:12, :], cs[:, 8:12, :], ACT.Silu).then_inc(S("v_silu"), 1)
                for g in range(2):
                    evac(("az", g), sz[:, 2 * g:2 * g + 2, :], ACT.Silu)
                b = ph3.read(act, "ab")
                A(ab, PS[:, b, 0:16].rearrange("p (t n) -> p t n", t=TT), ACT.Copy).then_inc(psum_free[b], 1)
                ph3.freed(act, "ab")
                A(beta, ab[:, :, 0:4], ACT.Sigmoid).then_inc(S("beta_ready"), 1)
                act.wait_ge(S("zt_ready"), 1)
                A(col[:, LCOLS:LCOLS + 4], col[:, LCOLS:LCOLS + 4], ACT.Exp).then_inc(S("alog_exp"), 1)
                link(A(eRc, eRc, ACT.Exp))
                A(eRc, eRc, ACT.Ln, bias=C("one")).then_inc(S("softplus"), 1)
                evac(("bq", 0), qb)
                b = ph3.read(act, "bk")
                A(kbb, PS[:, b, 0:T], ACT.Copy).then_inc(psum_free[b], 1)
                b = ph3.read(act, "bv")
                A(vtk, PS[:, b, 0:TT * SAD].rearrange("p (t n) -> p t n", t=TT), ACT.Copy).then_inc(psum_free[b], 1)
                evac(("qi", 0), qi)
                b = ph3.read(act, "ki")
                A(kii, PS[:, b, 0:T], ACT.Copy).then_inc(psum_free[b], 1)
                b = ph3.read(act, "wi")
                A(wi, PS[:, b, 0:8].rearrange("p (t n) -> p t n", t=TT), ACT.Copy, scale=float(4 ** -0.5 * 64 ** -0.5))\
                    .then_inc(psum_free[b], 1)
                for g in range(4):
                    rs3(rsb[:, g * 512:(g + 1) * 512], 1.0, ("l2", g), 512).then_inc(S("l2_ready"), 1)
                act.wait_ge(S("Gc_ready"), 1)
                A(eGc, Gc, ACT.Exp).then_inc(S("eGc_ready"), 1)
                A(eRc, eRc, ACT.Exp).then_inc(S("eGc_ready"), 1)
                act.wait_ge(S("DT_arg"), 2)
                A(DT, DT, ACT.Exp).then_inc(S("DT_exp"), 1)
                for g in range(2):
                    b = ph3.read(act, ("Gb", g))
                    A(eG[:, 2 * g:2 * g + 2, :], v2(PS[:, b, :]), ACT.Exp).then_inc(psum_free[b], 1)
                evac(("cq", 0), cq, ACT.Silu)
                evac(("cf", 0), cf, ACT.Sigmoid)
                act.wait_ge(S("fg_ready"), 1)
                A(cf, cf, ACT.Ln).then_inc(S("lf_ready"), 1)
                b = ph3.read(act, "ci")
                A(cit, PS[:, b, :].rearrange("p (t n) -> p t n", t=TT), ACT.Copy).then_inc(psum_free[b], 1)
                evac(("cg", 0), cg, ACT.Silu)
                z4 = lambda v, g: v[:, 2 * g:2 * g + 2].rearrange("p h t c -> p (h t c)")
                for lv in range(1, 6):
                    for g in range(2):
                        b = ph3.read(act, ("Z", lv, g))
                        A(z4(Z, g), PS[:, b, :], ACT.Copy).then_inc(psum_free[b], 1)
                for t in range(TT):
                    b = ph3.read(act, ("u0", t))
                    A(u[:, t].rearrange("p h c -> p (h c)"), PS[:, b, :], ACT.Copy).then_inc(psum_free[b], 1)
                for g in range(2):
                    evac(("wk", g), wk[:, 2 * g:2 * g + 2, :])
                for t in range(TT):
                    for par in range(2):
                        if t:
                            act.wait_ge(S("relu_used"), par + 1)
                        evac(("is", t, par), relu[:, par], ACT.Relu)
                for g in range(2):
                    evac(("oa", g), cat[:, 2 * g:2 * g + 2, :])
                ph3.freed(act, ("oa", 1))
                A(sc3[:, 0:4, :], cat[:, 0:4, :], ACT.Square).then_inc(S("oa_squares"), 1)
                for t in range(TT):
                    act.wait_ge(S("p_arg"), t + 1)
                    A(pr[:, t], pr[:, t], ACT.Exp, scale=SAD ** -0.5).then_inc(S("p_exp"), 1)
                for i in range(SAH):
                    b = ph3.read(act, ("pt", i))
                    A(pT[:, i], v2(PS[:, b, :]), ACT.Copy).then_inc(psum_free[b], 1)
                evac("ob", cat[:, 4:6, :])
                act.wait_ge(S("hg_args"), 1)
                A(args, args, ACT.Exp).then_inc(S("hg_exp"), 1)
                A(eB, Bc, ACT.Exp).then_inc(S("hg_exp"), 1)
                A(eR, eR, ACT.Exp).then_inc(S("hg_exp"), 1)
                b = ph3.read(act, "hkt")
                A(kdt, PS[:, b, :].rearrange("p (t n) -> p t n", t=TT), ACT.Copy).then_inc(psum_free[b], 1)
                evac("oc", cat[:, 6:8, :])
                ph3.freed(act, "oc")
                A(sc3[:, 6:8, :], cat[:, 6:8, :], ACT.Square).then_inc(S("oc_squares"), 1)
                for g in range(2):
                    rs3(fT[:, 2 * g:2 * g + 2, :].rearrange("p k t -> p (k t)"), P, ("oam", g), 512).then_inc(S("oam_ready"), 1)
                rs3(fT[:, 4:6, :].rearrange("p k t -> p (k t)"), 64, "ocm", 512).then_inc(S("oam_ready"), 1)

                def post(key, n, stage):
                    for g in range(n):
                        evac(key(g), fT[:, 2 * g:2 * g + 2, :])
                    ph3.freed(act, key(n - 1))
                    A(fsq, fT, ACT.Square).then_inc(S(stage), 1)

                post(lambda g: (("out", g // 2), g % 2), 4, "sq_mix")
                rs3(rs, D, "ms1").then_inc(S("rs_ready"), 1)
                rs3(rs, D, "ms2").then_inc(S("rs_ready"), 1)
                for j in range(FFT // 2):
                    ph3.freed(act, ("up", j, 0))
                    A(gcv[:, j % 2, 0:2, :], gcv[:, j % 2, 0:2, :], ACT.Gelu_apprx_tanh).then_inc(S("gelu_ready"), 1)
                post(lambda g: ("down", g), 4, "sq_f")
                rs3(rs, D, "ms3").then_inc(S("rs_ready"), 1)
                meet(act, "act")

        @block.vector
        def _(dve):
            V = nc.vector
            link = Chain(dve, "vec_step")
            V.memset(a2[0:32, :, :], 0.0).then_inc(S("a2_zero"), 1)
            b = ph1.read(dve, "colsA")
            V.tensor_copy(colsA[:, :], PS[:, b, 0:NA]).then_inc(psum_free[b], 1)
            ph1.freed(dve, "colsA")
            b = ph1.read(dve, "colsL")
            V.tensor_copy(colsL[:, :, :], PS[:, b, 0:2 * LCOLS].rearrange("p (l n) -> p l n", l=2)).then_inc(psum_free[b], 1)
            ph1.freed(dve, "colsL")
            o = row_at(ROWS_B, "hg_lb_2")
            link(V.memset(lbc[:, 0, 0:2], 0.0))
            link(V.memset(lbc[:, 0, 2:4], 1.0))
            V.tensor_tensor(lbc[:, 1, 0:2], colsL[:, 1, o:o + 2], colsL[:, 0, o:o + 2], ALU.subtract)\
                .then_inc(S("cols_ready"), 1)
            dve.wait_ge(S("lb_ready"), 1)
            V.tensor_scalar(lbc[:, 1, 2:4], lbc[:, 1, 0:2], -1.0, 1.0, ALU.mult, ALU.add)
            for kp in range(4):
                b = ph1.read(dve, ("xT", kp))
                V.tensor_copy(xT[:, 2 * kp:2 * kp + 2, :], PS[:, b, :].rearrange("p (k t) -> p k t", k=2))\
                    .then_inc(psum_free[b], 1)
            ph1.freed(dve, ("xT", 3))
            V.tensor_tensor(sqb[:, :, T:2 * T], xT[:, :, :], xT[:, :, :], ALU.mult).then_inc(S("squares"), 1)
            dve.wait_ge(S("rstd_ready"), 1)
            V.tensor_tensor(hboth[:, :, T:2 * T], xT[:, :, :],
                            rstd[:, T:2 * T].unsqueeze(1).broadcast_to([P, KT, T]), ALU.mult).then_inc(S("normed"), 1)
            V.tensor_tensor(hboth[:, :, 0:T], hboth[:, :, 0:T],
                            rstd[:, 0:T].unsqueeze(1).broadcast_to([P, KT, T]), ALU.mult).then_inc(S("normed"), 1)
            bm = row_at(ROWS_A, "b_mod")

            def modulate(j):
                b = ph1.read(dve, ("mod", j))
                V.tensor_tensor(mods[:, 4 * j:4 * j + 4, :], PS[:, b, 0:8].rearrange("p (j v) -> p j v", v=2),
                                colsA[:, bm + 4 * j:bm + 4 * j + 4].unsqueeze(2).broadcast_to([P, 4, 2]),
                                ALU.add).then_inc(psum_free[b], 1)

            for j in range(4):
                modulate(j)
            ph1.freed(dve, ("mod", 3))
            for v in range(2):
                ins = V.scalar_tensor_tensor(ada[:, v, :], mods[:, 8:16, v], 1.0, colA("norm1_g", 0, 8), ALU.add, ALU.mult)
                if v == 0:
                    link(ins)
            ins.then_inc(S("ada_ready"), 1)
            for h in range(GH):
                b = ph1.read(dve, ("k", 0, h))
                V.tensor_copy(kT[:, h, :], PS[:, b, :]).then_inc(psum_free[b], 1)
            for d in range(2):
                for h in range(GH):
                    b = ph1.read(dve, ("z", d, h))
                    bias = colA("gla_ab_f" if d == 0 else "gla_ab_b", h)
                    V.tensor_scalar(la[:, d, h, :], PS[:, b, :], bias, 0.0, ALU.add, ALU.min)
                    V.tensor_scalar(cum[:, d, h, :], PS[:, b, :], bias, None, ALU.add).then_inc(psum_free[b], 1)
                    ph1.freed(dve, ("z", d, h))
                    V.scalar_tensor_tensor(cum[:, d, h, :], cum[:, d, h, :], -1.0, cum[:, d, h, :], ALU.mult,
                                           ALU.min).then_inc(S("absz"), 1)
            for d in range(2):
                for h in range(GH):
                    dve.wait_ge(S("lnz"), d * GH + h + 1)
                    link(V.tensor_tensor(la[:, d, h, :], la[:, d, h, :], cum[:, d, h, :], ALU.subtract))
                    link(V.tensor_tensor_scan(cum[:, d, h, :], C("reset"), la[:, d, h, :], 0.0, ALU.mult, ALU.add))
            link(V.tensor_copy(lastc, cum[:, 0, :, T - 1]))
            V.tensor_tensor(e1, lastc.unsqueeze(2).broadcast_to([P, GH, T]), cum[:, 0, :, 0:T], ALU.subtract)\
                .then_inc(S("krc_arg"), 1)
            V.tensor_tensor(e2, cum[:, 1, :, 0:T], la[:, 1, :, 0:T], ALU.subtract).then_inc(S("krc_arg"), 1)
            V.tensor_copy(lastx, cum[:, :, :, T + CH - 1:2 * T:CH]).then_inc(S("decays"), 1)
            dve.wait_ge(S("decays"), 1)
            for d, e in ((0, e1), (1, e2)):
                dve.wait_ge(S("krc_exp"), d + 1)
                V.tensor_tensor(e, e, kT[:, :, 0:T], ALU.mult).then_inc(S("krc_ready"), 1)
            modulate(4)
            modulate(5)
            for d in range(2):
                for t in range(TT):
                    b = ph1.read(dve, ("krc", d, t))
                    V.tensor_copy(krt[:, d, t, :], PS[:, b, :]).then_inc(psum_free[b], 1)
            V.tensor_tensor(e1.rearrange("p h (n c) -> p h n c", n=NCH), lastx[:, 0].unsqueeze(3).broadcast_to([P, GH, NCH, CH]),
                            cum[:, 0, :, T:2 * T].rearrange("p h (n c) -> p h n c", n=NCH), ALU.subtract)\
                .then_inc(S("krx_arg"), 1)
            link(V.tensor_tensor(e2, cum[:, 1, :, T:2 * T], la[:, 1, :, T:2 * T], ALU.subtract))
            V.tensor_tensor(cum[:, 1, :, T:2 * T].rearrange("p h (n c) -> p h n c", n=NCH),
                            lastx[:, 1].unsqueeze(3).broadcast_to([P, GH, NCH, CH]),
                            e2.rearrange("p h (n c) -> p h n c", n=NCH), ALU.subtract).then_inc(S("cumb_ready"), 1)
            ph1.freed(dve, ("q", 0, 1))
            for d in range(2):
                dve.wait_ge(S("qdki_exp"), 2 * d + 1)
                V.tensor_tensor(qd[:, d], qd[:, d], qT, ALU.mult).then_inc(S("qdki_ready"), 1)
                dve.wait_ge(S("qdki_exp"), 2 * d + 2)
                V.tensor_tensor(ki[:, d], ki[:, d], kT[:, :, T:2 * T], ALU.mult).then_inc(S("qdki_ready"), 1)
            for d, e in ((0, e1), (1, e2)):
                dve.wait_ge(S("krx_exp"), d + 1)
                V.tensor_tensor(e, e, kT[:, :, T:2 * T], ALU.mult).then_inc(S("krx_ready"), 1)
            modulate(6)
            for d in range(2):
                for t in range(TT):
                    b = ph1.read(dve, ("krx", d, t))
                    V.tensor_copy(krt[:, d, t, :], PS[:, b, :]).then_inc(psum_free[b], 1)
            for h in range(GH):
                b = ph1.read(dve, ("sc", h))
                both = PS[:, b, :].rearrange("p (d t c) -> p d t c", d=2, t=TT)
                V.tensor_tensor(scT[:, h], both[:, 0], C("incl").unsqueeze(1).broadcast_to([P, TT, P]), ALU.mult)
                o2 = e2[:, h, :].rearrange("p (t c) -> p t c", t=TT)
                V.tensor_tensor(o2, both[:, 1], C("rev").unsqueeze(1).broadcast_to([P, TT, P]), ALU.mult)\
                    .then_inc(psum_free[b], 1)
                ph1.freed(dve, ("sc", h))
                V.tensor_tensor(scT[:, h], scT[:, h], o2, ALU.add).then_inc(S("sc_ready"), 1)
            for d in range(2):
                for hp in range(2):
                    ph1.freed(dve, ("s0", d, hp))
            dve.wait_ge(S("dec_ready"), 1)
            for h in range(GH):
                if h >= 2:
                    ph1.read(dve, ("o", h - 2))
                banks = [ph1.read(dve, ("kv", h, n)) for n in range(4)]

                def update(d, n):
                    c = n if d == 0 else NCH - 1 - n
                    prev = s0[:, d, h, :] if n == 0 else Sx[:, h % 2, d, n - 1, :]
                    b = banks[[(d, c) in g for g in KV_UNITS].index(True)]
                    return V.scalar_tensor_tensor(Sx[:, h % 2, d, n, :], prev, dec[:, d, h, c:c + 1],
                                                  PS[:, b, d * 256:(d + 1) * 256], ALU.mult, ALU.add)

                update(0, 0)
                link(update(1, 0))
                update(0, 1).then_inc(psum_free[banks[1]], 1)
                update(1, 1).then_inc(psum_free[banks[0]], 1)
                for n in range(2):
                    ph1.freed(dve, ("kv", h, n))
                update(0, 2).then_inc(psum_free[banks[2]], 1)
                update(1, 2).then_inc(psum_free[banks[3]], 1)
            for g in range(2):
                ph1.freed(dve, ("u", 0, g))
            ph1.read(dve, ("o", GH - 1))
            link(V.memset(qdki[:, 0:1280], 0.0))
            u4 = hboth[:, 0:4, 0:T].rearrange("p g (r w) -> p g r w", r=ROWS)
            for g in range(POOL_G):
                ins = V.tensor_copy(pads[0][:, g, :, 8:8 + GRID_W], u4[:, g])
            link(ins)
            src = pads[0]
            pg = pooled.rearrange("p g (r w) -> p g r w", r=ROWS)
            rc = C("rcnt").rearrange("p (g w) -> p g w", g=POOL_G)
            for g in range(POOL_G):
                half = 1 << g
                lo = max(half, 1)
                a, z = {0: (1, 80), 1: (2, 79), 2: (4, 77), 3: (8, 73)}[g]
                dst = pads[1 + g % 2]
                if g == 0:
                    ins = V.tensor_tensor(dst[:, :, :, a:z], src[:, :, :, a - 1:z - 1], src[:, :, :, a:z], ALU.add)
                else:
                    q = half // 2
                    for gg in range(g, POOL_G):
                        ins = V.tensor_tensor(dst[:, gg, :, a:z], src[:, gg, :, a - q:z - q], src[:, gg, :, a + q:z + q], ALU.add)
                link(ins)
                ins = V.tensor_tensor(pg[:, g], dst[:, g, :, 8:8 + GRID_W],
                                      rc[:, g].unsqueeze(1).broadcast_to([P, ROWS, GRID_W]), ALU.mult)
                src = dst
            link(ins)
            V.tensor_tensor(pooled, pooled, hboth[:, 0:4, 0:T], ALU.subtract).then_inc(S("pooled_ready"), 1)
            for j in range(7, 12):
                modulate(j)
            ph1.freed(dve, ("mod", 11))
            dve.wait_ge(S("orstd_ready"), 2)
            orstd = e1
            o4 = oT.rearrange("p (h v) t -> p h v t", h=GH)
            link(V.tensor_tensor(o4, o4, orstd.unsqueeze(2).broadcast_to([P, GH, 2, T]), ALU.mult))
            for j in range(2):
                ph1.freed(dve, ("g", j, 1))
            for j in range(KT):
                ins = V.scalar_tensor_tensor(oT[:, j, :], oT[:, j, :], colA("gla_onorm_g", j % 2), sg[:, j, :],
                                             ALU.mult, ALU.mult)
            ins.then_inc(S("og_ready"), 1)
            for g in range(2):
                b = ph1.read(dve, ("yp", g))
                for i in range(2):
                    ins = V.tensor_scalar(yp[:, 2 * g + i, :], PS[:, b, i * T:(i + 1) * T],
                                          colA("pool_scale", 2 * g + i), None, ALU.mult)
                ins.then_inc(psum_free[b], 1)
            ph1.freed(dve, ("gate", 3, 1))
            for g in range(4):
                b = ph1.read(dve, ("pbr", g))
                V.tensor_tensor(mixed[:, 2 * g:2 * g + 2, :], PS[:, b, :].rearrange("p (j t) -> p j t", j=2),
                                gates[:, 2 * g:2 * g + 2, :], ALU.mult).then_inc(psum_free[b], 1)
            ph1.freed(dve, ("pbr", 3))
            for j in range(2):
                for g in range(2):
                    b = ph1.read(dve, ("gbr", j, g))
                    o = 4 * j + 2 * g
                    V.tensor_tensor(sg[:, o:o + 2, :], PS[:, b, :].rearrange("p (j t) -> p j t", j=2),
                                    gates[:, 8 + o:10 + o, :], ALU.mult).then_inc(psum_free[b], 1)
                    ph1.freed(dve, ("gbr", j, g))
                    V.tensor_tensor(mixed[:, o:o + 2, :], mixed[:, o:o + 2, :], sg[:, o:o + 2, :], ALU.add)\
                        .then_inc(S("mixed_ready"), 1)
            for j in range(2):
                for g in range(2):
                    b = ph1.read(dve, ("wo", j, g))
                    for i in range(2):
                        k = 4 * j + 2 * g + i
                        ins = V.scalar_tensor_tensor(xT[:, k, :], PS[:, b, i * T:(i + 1) * T], mod(2, 0, k), xT[:, k, :],
                                                     ALU.mult, ALU.add)
                    ins.then_inc(psum_free[b], 1)
            meet(dve, "dve")

            link = Chain(dve, "vec_step")
            V.tensor_tensor(h2n, xT[:, :, :], xT[:, :, :], ALU.mult).then_inc(S("sq2"), 1)
            link(V.scalar_tensor_tensor(ada[:, 2, :], mods[:, 32:40, 0], 1.0, colA("norm2_g", 0, 8), ALU.add, ALU.mult))
            V.memset(ytok, 0.0).then_inc(S("moe_zeroed"), 1)
            V.memset(PT, 0.0).then_inc(S("moe_zeroed"), 1)
            dve.wait_ge(S("rstd2_ready"), 1)
            V.tensor_tensor(h2n, xT[:, :, :], rstd2.unsqueeze(1).broadcast_to([P, KT, T]), ALU.mult).then_inc(S("normed2"), 1)
            b = ph2.read(dve, "route")
            V.tensor_copy(lg, PS[:, b, 0:128].rearrange("p (t n) -> p t n", t=TT)[:, :, 0:36]).then_inc(psum_free[b], 1)
            ph2.freed(dve, "route")

            def first_of_max(view, out, n, scratch):
                link(V.tensor_reduce(scratch, view, AX.X, ALU.max))
                link(V.tensor_tensor(out, view, scratch.unsqueeze(2).broadcast_to([P, TT, n]), ALU.is_equal))
                link(V.tensor_tensor(out, out, C("desc")[:, 0:n].unsqueeze(1).broadcast_to([P, TT, n]), ALU.mult))
                link(V.tensor_reduce(m1[9], out, AX.X, ALU.max))
                link(V.tensor_tensor(out, out, m1[9].unsqueeze(2).broadcast_to([P, TT, n]), ALU.is_equal))

            first_of_max(lg[:, :, 0:4], m8[2], N_GRP, m1[0])
            V.tensor_tensor(m8[0], lg[:, :, 0:4], m1[0].unsqueeze(2).broadcast_to([P, TT, N_GRP]), ALU.subtract)\
                .then_inc(S("route_arg"), 1)
            link(V.tensor_scalar(m8[3], m8[2], BIG, -BIG, ALU.mult, ALU.add))
            e4 = lambda v: v.rearrange("p t (g e) -> p t g e", g=N_GRP)
            for i in range(TT):
                ins = V.tensor_tensor(e4(m32[1])[:, i], lg[:, i, 4:36].rearrange("p (g e) -> p g e", g=N_GRP),
                                      m8[2][:, i].unsqueeze(2).broadcast_to([P, N_GRP, 8]), ALU.mult)
            link(ins)
            for i in range(TT):
                ins = V.tensor_tensor(e4(m32[1])[:, i], e4(m32[1])[:, i], m8[3][:, i].unsqueeze(2).broadcast_to([P, N_GRP, 8]),
                                      ALU.add)
            link(ins)
            first_of_max(m32[1], m32[2], N_EXP, m1[1])
            link(V.scalar_tensor_tensor(m32[3], m32[2], -2 * BIG, m32[1], ALU.mult, ALU.add))
            first_of_max(m32[3], m32[4], N_EXP, m1[4])
            V.tensor_tensor(m32[0], m32[2], m32[4], ALU.add).then_inc(S("chosen"), 1)
            V.tensor_tensor(m1[2], m1[4], m1[1], ALU.subtract).then_inc(S("route_arg"), 1)
            dve.wait_ge(S("route_exp"), 2)
            link(V.tensor_reduce(m1[5], m8[1], AX.X, ALU.add))
            link(V.tensor_scalar(m1[6], m1[3], 1.0, None, ALU.add))
            link(V.tensor_tensor(m1[5], m1[5], m1[6], ALU.mult))
            link(V.reciprocal(m1[5], m1[5]))
            link(V.tensor_tensor(m1[6], m1[5], m1[3], ALU.mult))
            link(V.tensor_tensor(m32[5], m32[2], m1[5].unsqueeze(2).broadcast_to([P, TT, N_EXP]), ALU.mult))
            link(V.tensor_tensor(m32[6], m32[4], m1[6].unsqueeze(2).broadcast_to([P, TT, N_EXP]), ALU.mult))
            link(V.tensor_tensor(weights[:, :, 0:N_EXP], m32[5], m32[6], ALU.add))
            link(V.tensor_copy(weights[:, :, N_EXP:], weights[:, :, 0:2]))
            b = ph2.read(dve, "rank")
            link(V.scalar_tensor_tensor(m32[7], PS[:, b, 0:64].rearrange("p (t n) -> p t n", t=TT), 1.0, m32[0],
                                        ALU.add, ALU.mult))
            V.tensor_copy(totals, PS[:, b, 64:96]).then_inc(psum_free[b], 1)
            ph2.freed(dve, "rank")
            link(V.tensor_scalar(ranks[:, :, 0:N_EXP], m32[7], -1.0, None, ALU.add))
            link(V.tensor_scalar(ranks[:, :, N_EXP:], ranks[:, :, 0:2], -float(SLOTS), None, ALU.add))
            link(V.tensor_reduce(mx1[:, 0:1], totals, AX.X, ALU.max))
            link(V.tensor_tensor(m8[3][:, 0], mx1[:, 0:1].broadcast_to([P, 4]), C("thr"), ALU.is_gt))
            link(V.tensor_reduce(mx1[:, 1:2], m8[3][:, 0], AX.X, ALU.add))
            V.tensor_copy(rounds_i, mx1[:, 1:2]).then_inc(S("rounds_ready"), 1)
            dve.wait_ge(S("rounds_ready"), 1)
            rounds = dve.value_load(rounds_i[0:1, 0:1])
            link(V.memset(s1, 0.0))
            dve.sem_inc(S("y_hi"), 1)
            dve.sem_inc(S("y_lo"), 1)
            dve.sem_inc(S("pt_ready"), 1)
            dve.sem_inc(S("hid_ready"), 1)
            def masks(two):
                V.tensor_tensor(sel, C("iota").unsqueeze(1).unsqueeze(1).broadcast_to([P, TT, 2, SLOTS]),
                                ranks[:, :, two].unsqueeze(3).broadcast_to([P, TT, 2, SLOTS]),
                                ALU.is_equal).then_inc(S("sel_ready"), 1)

            def weigh(two):
                V.tensor_tensor(selw, sel, weights[:, :, two].unsqueeze(3).broadcast_to([P, TT, 2, SLOTS]),
                                ALU.mult).then_inc(S("selw_ready"), 1)

            masks(slice(0, 2))
            dve.wait_ge(S("sel_ready"), 1)
            weigh(slice(0, 2))
            with dve.Fori(0, rounds) as r:
                with dve.Fori(0, PAIRS) as p:
                    i1 = dve.snap(r * PAIRS + p + 1)
                    i2 = dve.snap(i1 * 2)
                    dve.wait_ge(S("gathered"), i1 + 1)
                    V.tensor_copy(hg[:, 4:8, :], PS[:, 5, :].rearrange("p (k s) -> p k s", k=4)).then_inc(S("hg_hi"), 1)
                    dve.wait_ge(S("pt_turned"), i1 + 1)
                    V.tensor_copy(PT, PS[:, 6, 0:T]).then_inc(S("pt_ready"), 1)
                    masks(bass.ds(p * 2 + 2, 2))
                    dve.wait_ge(S("sel_ready"), i1 + 1)
                    weigh(bass.ds(p * 2 + 2, 2))
                    for e in range(2):
                        dve.wait_ge(S("s1_ready"), i2 - 1 + e)
                        V.tensor_tensor(hid[:, e].rearrange("p f s -> p (f s)"), s1[:, e, :], PS[:, 4 + e, 256:512],
                                        ALU.mult).then_inc(S("hid_ready"), 1)
                    dve.wait_ge(y_full, i1)
                    V.tensor_copy(ytok[:, 512:1024], PS[:, 7, :]).then_inc(S("y_hi"), 1)
                V.tensor_scalar(ranks, ranks, -float(SLOTS), None, ALU.add).then_inc(S("ranks_moved"), 1)
                dve.wait_ge(S("ranks_moved"), r + 1)
            dve.drain().then_inc(S("evacuated"), 1)
            dve.wait_ge(S("moe_out"), 1)
            for k in range(KT):
                ins = V.scalar_tensor_tensor(xT[:, k, :], PS[:, k // 2, (k % 2) * T:(k % 2 + 1) * T], mod(5, 0, k),
                                             xT[:, k, :], ALU.mult, ALU.add)
            link(ins)
            V.tensor_tensor(h2n, xT[:, :, :], xT[:, :, :], ALU.mult).then_inc(S("sq3"), 1)
            dve.wait_ge(S("rstd3_ready"), 1)
            for k in range(KT):
                V.scalar_tensor_tensor(xT[:, k, :], xT[:, k, :], colA("final_norm_g", k), rstd2, ALU.mult, ALU.mult)
            meet(dve, "dve")

            v2 = lambda v: v.rearrange("p (j t) -> p j t", j=2)
            with dve.Fori(0, LAYERS) as L:
                link = Chain(dve, "vec_step")
                link(V.tensor_copy(col[:, 0:LCOLS], colsL[:, bass.ds(L, 1), :].rearrange("p a n -> p (a n)")))
                link(V.tensor_copy(col[:, LCOLS:], logs[:, bass.ds(L, 1), :].rearrange("p a n -> p (a n)")))
                link(V.tensor_copy(small[:, 0:4], lbc[:, bass.ds(L, 1), :].rearrange("p a n -> p (a n)")))
                V.tensor_tensor(sc3, xT[:, :, :], xT[:, :, :], ALU.mult).then_inc(S("sq_x"), 1)

                def norm(n, name):
                    dve.wait_ge(S("rs_ready"), n)
                    for k in range(KT):
                        ins = V.scalar_tensor_tensor(hT[:, k, :], xT[:, k, :], cl(name, k), rs, ALU.mult, ALU.mult)
                    ins.then_inc(S("h_ready3"), 1)

                norm(1, "g_mix_pre_2")

                def conv(dsts, srcs, taps):
                    n = len(taps[0])
                    for d in range(n):
                        done = []
                        for dst, src, w in zip(dsts, srcs, taps):
                            if d == 0:
                                done.append(V.tensor_scalar(dst, src, w[-1], None, ALU.mult))
                            else:
                                done.append(V.scalar_tensor_tensor(dst[:, d:], src[:, 0:T - d], w[n - 1 - d], dst[:, d:],
                                                                   ALU.mult, ALU.add))
                        if d < n - 1:
                            link(done[-1])
                    return done

                for q_, name in enumerate(("aq", "ak", "av")):
                    for g in range(2):
                        b = ph3.read(dve, (name, g))
                        fs = [4 * q_ + 2 * g + i for i in range(2)]
                        conv([cs[:, f, :] for f in fs], [PS[:, b, i * T:(i + 1) * T] for i in range(2)],
                             [[cl("dn_conv_2", 12 * j + f) for j in range(DN_CONV)] for f in fs])[-1]\
                            .then_inc(psum_free[b], 1)
                        ph3.freed(dve, (name, g))
                    if q_:
                        dve.sem_inc(S("conv_ready"), 1)
                dve.wait_ge(S("beta_ready"), 1)
                bc = lambda v: v.unsqueeze(1).broadcast_to([P, TT, 4])
                link(V.tensor_tensor(zt, ab[:, :, 4:8], bc(col[:, LCOLS + 4:LCOLS + 8]), ALU.add))
                V.scalar_tensor_tensor(eRc, zt, -1.0, zt, ALU.mult, ALU.min).then_inc(S("zt_ready"), 1)
                link(V.tensor_scalar(zt, zt, 0.0, None, ALU.max))
                dve.wait_ge(S("softplus"), 1)
                link(V.tensor_tensor(zt, zt, eRc, ALU.add))
                dve.wait_ge(S("alog_exp"), 1)
                link(V.tensor_tensor(zt, zt, bc(col[:, LCOLS:LCOLS + 4]), ALU.mult))
                V.tensor_scalar(gt, zt, -1.0, None, ALU.mult).then_inc(S("g_ready"), 1)
                dve.wait_ge(S("g_ready"), 1)
                per_head = lambda v: v.rearrange("p t h -> p h t").unsqueeze(3).broadcast_to([P, DNH, TT, P])
                V.tensor_copy(gx, per_head(gt)).then_inc(S("gx_ready"), 1)
                V.tensor_copy(bx, per_head(beta)).then_inc(S("gx_ready"), 1)
                dve.wait_ge(S("l2_ready"), 4)
                rq = rsb.rearrange("p (h t) -> p h t", h=8)
                V.scalar_tensor_tensor(cs[:, 0:4, :], cs[:, 0:4, :], float(P ** -0.5), rq[:, 0:4, :], ALU.mult, ALU.mult)\
                    .then_inc(S("qk_normed"), 1)
                dve.wait_ge(S("v_silu"), 1)
                V.tensor_tensor(cs[:, 4:8, :], cs[:, 4:8, :], rq[:, 4:8, :], ALU.mult).then_inc(S("qk_normed"), 1)
                b = ph3.read(dve, "G")
                G4 = PS[:, b, 0:16].rearrange("p (i t h) -> p i t h", i=2, t=TT)
                link(V.tensor_copy(Gc, G4[:, 0]))
                V.tensor_tensor(eRc, G4[:, 1], Gc, ALU.subtract).then_inc(psum_free[b], 1)
                ph3.freed(dve, "G")
                dve.sem_inc(S("Gc_ready"), 1)
                for g in range(2):
                    b = ph3.read(dve, ("Gb", g))
                    for i in range(2):
                        for t in range(TT):
                            o = (2 * i + t) * P
                            ins = V.tensor_scalar(DT[:, 2 * g + i, t, :], PS[:, b, o:o + P], Gc[:, t, 2 * g + i:2 * g + i + 1],
                                                  0.0, ALU.subtract, ALU.min)
                    ins.then_inc(S("DT_arg"), 1)
                dve.wait_ge(S("eGc_ready"), 2)
                link(V.tensor_tensor(bG, beta, eGc, ALU.mult))
                dve.wait_ge(S("DT_exp"), 1)
                f4 = lambda v: v.rearrange("p h t c -> p (h t) c")
                link(V.tensor_tensor(f4(DT), f4(DT), C("incl").unsqueeze(1).broadcast_to([P, 8, P]), ALU.mult))
                z4 = lambda v, g: v[:, 2 * g:2 * g + 2].rearrange("p h t c -> p (h t c)")
                for g in range(2):
                    ph3.freed(dve, ("Gb", g))
                link(V.tensor_copy(glast, eG[:, :, CH - 1:T:CH]))
                V.tensor_tensor(eG, eG, cs[:, 0:4, :], ALU.mult).then_inc(S("qdec_ready"), 1)
                for g in range(2):
                    b = ph3.read(dve, ("bb", g))
                    V.tensor_tensor(z4(MT, g), PS[:, b, :], z4(DT, g), ALU.mult).then_inc(psum_free[b], 1)
                    ph3.freed(dve, ("bb", g))
                ph3.freed(dve, ("cf", 0))
                for i in range(2):
                    ins = V.tensor_scalar(cf[:, i, :], cf[:, i, :], small[:, 2 + i:3 + i], small[:, i:i + 1], ALU.mult, ALU.add)
                link(ins)
                V.tensor_scalar(kc, cf, -1.0, 1.0, ALU.mult, ALU.add)\
                    .then_inc(S("fg_ready"), 1)
                for g in range(2):
                    b = ph3.read(dve, ("kk", g))
                    V.tensor_tensor(z4(MT, g), PS[:, b, :], z4(MT, g), ALU.mult).then_inc(psum_free[b], 1)
                    ph3.freed(dve, ("kk", g))
                for g in range(2):
                    b = ph3.read(dve, ("qk", g))
                    V.tensor_tensor(z4(QK, g), PS[:, b, :], z4(DT, g), ALU.mult).then_inc(psum_free[b], 1)
                h3 = lambda v: v.unsqueeze(2).broadcast_to([P, DNH, P])
                for t in range(TT):
                    b = ph3.read(dve, ("kt", t))
                    p3 = PS[:, b, :].rearrange("p (h c) -> p h c", h=DNH)
                    V.tensor_tensor(kd[:, t], p3, h3(eRc[:, t]), ALU.mult).then_inc(S("kvb_ready"), 1)
                    V.tensor_tensor(kb[:, t], p3, h3(bG[:, t]), ALU.mult).then_inc(psum_free[b], 1)
                    ph3.freed(dve, ("kt", t))
                    dve.sem_inc(S("kvb_ready"), 1)
                for t in range(TT):
                    b = ph3.read(dve, ("vt", t))
                    V.tensor_tensor(vb[:, t], PS[:, b, :].rearrange("p (h c) -> p h c", h=DNH), h3(beta[:, t]), ALU.mult)\
                        .then_inc(psum_free[b], 1)
                    ph3.freed(dve, ("vt", t))
                    dve.sem_inc(S("kvb_ready"), 1)

                def joins(lv):
                    for g in range(2):
                        V.tensor_tensor(f4(BT[lv % 2][:, 2 * g:2 * g + 2]), f4(MT[:, 2 * g:2 * g + 2]),
                                        C(f"lv{lv}").unsqueeze(1).broadcast_to([P, 4, P]), ALU.mult).then_inc(S("B_ready"), 1)

                joins(0)
                ident4 = C("ident").unsqueeze(1).broadcast_to([P, 4, P])
                for g in range(2):
                    dve.wait_ge(S("B_ready"), g + 1)
                    V.tensor_tensor(f4(XIT[:, 2 * g:2 * g + 2]), ident4, f4(BT[0][:, 2 * g:2 * g + 2]), ALU.subtract)\
                        .then_inc(S("X0T_ready"), 1)
                joins(1)
                for g in range(2):
                    b = ph3.read(dve, ("Z", 0, g))
                    V.tensor_tensor(f4(XI[:, 2 * g:2 * g + 2]), ident4, PS[:, b, :].rearrange("p (q c) -> p q c", q=4),
                                    ALU.subtract).then_inc(psum_free[b], 1)
                for lv in range(1, 6):
                    if lv == 1:
                        dve.wait_ge(S("X0T_ready"), 2)
                    if lv < 5:
                        joins(lv + 1)
                    for g in range(2):
                        if lv < 5:
                            b = ph3.read(dve, ("XZ", lv, g))
                            V.tensor_tensor(z4(XI, g), z4(XI, g), PS[:, b, :], ALU.subtract).then_inc(psum_free[b], 1)
                        b = ph3.read(dve, ("ZX", lv, g))
                        V.tensor_tensor(z4(XIT, g), z4(XIT, g), PS[:, b, :], ALU.subtract).then_inc(psum_free[b], 1)
                    for g in range(2):
                        if lv < 5:
                            ph3.freed(dve, ("XZ", lv, g))
                        ph3.freed(dve, ("ZX", lv, g))
                for t in range(TT):
                    ph3.freed(dve, ("u0", t))
                ph3.freed(dve, "wi")

                def index_scores(t):
                    n = 0
                    for par in range(2):
                        ph3.freed(dve, ("is", t, par))
                        for i in range(2):
                            wcol = wi[:, t, 2 * i + par:2 * i + par + 1]
                            other = C("adm")[:, t * T:(t + 1) * T] if n == 0 else score[:, t, :]
                            ins = V.scalar_tensor_tensor(score[:, t, :], relu[:, par, i, :], wcol, other, ALU.mult, ALU.add)
                            n += 1
                            if i == 1:
                                ins.then_inc(S("relu_used"), 1)
                                dve.wait_ge(S("relu_used"), 2 * t + par + 1)
                            else:
                                link(ins)

                for n in range(NCH):
                    t, r_ = n // 2, slice(CH * (n % 2), CH * (n % 2) + CH)
                    if n:
                        b = ph3.read(dve, ("wS", n))
                        ur = u[r_, t].rearrange("p h c -> p (h c)")
                        V.tensor_tensor(ur, ur, PS[r_, b, :], ALU.subtract).then_inc(psum_free[b], 1)
                    if n < NCH - 1:
                        b = ph3.read(dve, ("dS", n))
                        for i in range(DNH):
                            p3 = PS[:, b, i * P:(i + 1) * P]
                            if n == 0:
                                ins = V.tensor_copy(Sd[0][:, i, :], p3)
                            else:
                                ins = V.scalar_tensor_tensor(Sd[n][:, i, :], Sd[n - 1][:, i, :], glast[:, i, n:n + 1], p3,
                                                             ALU.mult, ALU.add)
                        ins.then_inc(psum_free[b], 1)
                        ph3.freed(dve, ("dS", n))
                    if n < 2:
                        index_scores(n)
                NEGV = NEG
                for r_ in range(TOPK // 8):
                    for t in range(TT):
                        ins = V.max(m8k[:, t, :], (score if r_ == 0 else work)[:, t, :])
                    link(ins)
                    for t in range(TT):
                        ins = V.match_replace(out=work[:, t, :], in_to_replace=m8k[:, t, :],
                                              in_values=(score if r_ == 0 else work)[:, t, :], imm_value=NEGV)
                    link(ins)
                link(V.tensor_tensor(work, work, score, ALU.not_equal))
                link(V.tensor_scalar(score, work, BIG, -BIG, ALU.mult, ALU.add))
                for t in range(TT):
                    for par in range(2):
                        b = ph3.read(dve, ("lg", t, par))
                        V.tensor_tensor(pr[:, t].rearrange("p (i q) s -> p q i s", q=2)[:, par], v2(PS[:, b, :]),
                                        score[:, t, :].unsqueeze(1).broadcast_to([P, 2, T]), ALU.add)\
                            .then_inc(psum_free[b], 1)
                    for par in range(2):
                        ph3.freed(dve, ("lg", t, par))
                    link(V.tensor_reduce(ab[:, t, 0:4], pr[:, t], AX.X, ALU.max))
                    V.tensor_tensor(pr[:, t], pr[:, t], ab[:, t, 0:4].unsqueeze(2).broadcast_to([P, SAH, T]),
                                    ALU.subtract).then_inc(S("p_arg"), 1)
                for t in range(TT):
                    dve.wait_ge(S("p_exp"), t + 1)
                    link(V.tensor_reduce(ab[:, t, 0:4], pr[:, t], AX.X, ALU.add))
                    link(V.reciprocal(ab[:, t, 4:8], ab[:, t, 0:4]))
                    V.tensor_tensor(pr[:, t], pr[:, t], ab[:, t, 4:8].unsqueeze(2).broadcast_to([P, SAH, T]),
                                    ALU.mult).then_inc(S("p_ready"), 1)
                dve.wait_ge(S("lf_ready"), 1)
                ph3.freed(dve, "ob")
                for i in range(2):
                    ins = V.tensor_tensor_scan(Bc[:, i, :], C("reset")[:, T:2 * T], cf[:, i, :], 0.0, ALU.mult, ALU.add)
                link(ins)
                for lv, size in enumerate((64, 32, 16)):
                    by_block = lambda v: v.rearrange("p (m c) -> p m c", c=size)
                    Bb = by_block(Bc.rearrange("p i t -> p (i t)"))
                    ins = V.tensor_tensor(by_block(args[:, lv, 0, :]), Bb,
                                          Bb[:, :, size // 2 - 1:size // 2].broadcast_to([P, 2 * T // size, size]), ALU.subtract)
                Bb = Bc.rearrange("p i (n c) -> p (i n) c", c=CH)
                link(V.tensor_tensor(eR.rearrange("p i (n c) -> p (i n) c", c=CH),
                                     Bb[:, :, CH - 1:CH].broadcast_to([P, 2 * NCH, CH]), Bb, ALU.subtract))
                link(V.tensor_scalar(args[:, 2, 0, :], args[:, 2, 0, :], 80.0, -80.0, ALU.min, ALU.max))
                V.tensor_scalar(args[:, 2, 1, :], args[:, 2, 0, :], -1.0, None, ALU.mult)
                link(V.tensor_scalar(args[:, 0:2, 1, :], args[:, 0:2, 0, :], -1.0, 0.0, ALU.mult, ALU.min))
                V.tensor_scalar(args[:, 0:2, 0, :], args[:, 0:2, 0, :], 0.0, None, ALU.min).then_inc(S("hg_args"), 1)
                flat = lambda v: v.rearrange("p i t -> p (i t)")
                dve.wait_ge(S("hg_exp"), 1)
                for side, v in enumerate((cq, kc)):
                    V.tensor_tensor(args[:, :, side, :], args[:, :, side, :],
                                    flat(v).unsqueeze(1).broadcast_to([P, 3, 2 * T]), ALU.mult).then_inc(S("qk_levels"), 1)
                dve.wait_ge(S("hg_exp"), 3)
                link(V.tensor_copy(hlast, eB[:, :, CH - 1:T:CH]))
                V.tensor_tensor(eB, eB, cq, ALU.mult)
                V.tensor_tensor(eR, eR, kc, ALU.mult).then_inc(S("kdec_ready"), 1)
                for lv, mask in enumerate(("lv5", "lv4", "diag16")):
                    for par in range(2):
                        b = ph3.read(dve, ("hs", lv, par))
                        quads = lambda v: v.rearrange("p i t c -> p (i t) c")
                        dst = AT2 if lv else AT[:, par]
                        V.tensor_tensor(quads(dst), PS[:, b, :].rearrange("p (q c) -> p q c", q=4),
                                        C(mask).unsqueeze(1).broadcast_to([P, 4, P]), ALU.mult).then_inc(psum_free[b], 1)
                        ph3.freed(dve, ("hs", lv, par))
                        if lv:
                            ins = V.tensor_tensor(AT[:, par], AT[:, par], AT2, ALU.add)
                            if lv == 2:
                                ins.then_inc(S("AT_ready"), 1)
                                dve.wait_ge(S("AT_ready"), par + 1)
                            else:
                                link(ins)
                for par, ns in ((0, (0, 2)), (1, (1,))):
                    b = ph3.read(dve, ("hS", par))
                    for j, n in enumerate(ns):
                        ins = V.tensor_tensor(Sh[:, n], PS[:, b, 2 * j * P:2 * (j + 1) * P].rearrange("p (i c) -> p i c", i=2),
                                              C("blk").unsqueeze(1).broadcast_to([P, 2, P]), ALU.mult)
                    ins.then_inc(psum_free[b], 1)
                    ph3.freed(dve, ("hS", par))
                for n in (1, 2):
                    for i in range(2):
                        ins = V.scalar_tensor_tensor(Sh[:, n, i, :], Sh[:, n - 1, i, :], hlast[:, i, n:n + 1], Sh[:, n, i, :],
                                                     ALU.mult, ALU.add)
                    if n == 1:
                        link(ins)
                ins.then_inc(S("Sh_ready"), 1)
                dve.wait_ge(S("oam_ready"), 3)
                link(V.scalar_tensor_tensor(cat[:, 0:4, :], cat[:, 0:4, :], cl("dn_norm_2"), fT[:, 0:4, :], ALU.mult, ALU.mult))
                V.tensor_tensor(cat[:, 0:4, :], cat[:, 0:4, :], sz, ALU.mult).then_inc(S("oa_ready"), 1)
                link(V.scalar_tensor_tensor(cat[:, 6:8, :], cat[:, 6:8, :], cl("hg_norm_2"), fT[:, 4:6, :], ALU.mult, ALU.mult))
                V.tensor_tensor(cat[:, 6:8, :], cat[:, 6:8, :], cg, ALU.mult).then_inc(S("oc_ready"), 1)

                def add_normed(n, name):
                    dve.wait_ge(S("rs_ready"), n)
                    for k in range(KT):
                        ins = V.scalar_tensor_tensor(fT[:, k, :], fT[:, k, :], cl(name, k), rs, ALU.mult, ALU.mult)
                    link(ins)
                    return V.tensor_tensor(xT[:, :, :], xT[:, :, :], fT, ALU.add)

                link(add_normed(2, "g_mix_post_2"))
                V.tensor_tensor(sc3, xT[:, :, :], xT[:, :, :], ALU.mult).then_inc(S("sq_x2"), 1)
                norm(3, "g_ffn_pre_2")

                def gate(j):
                    dve.wait_ge(S("gelu_ready"), j + 1)
                    V.tensor_tensor(gated[:, 2 * j:2 * j + 2, :], gcv[:, j % 2, 0:2, :], gcv[:, j % 2, 2:4, :], ALU.mult)\
                        .then_inc(S("gated"), 1)

                for j in range(FFT // 2):
                    if j >= 2:
                        dve.wait_ge(S("gated"), j - 1)
                    for v in range(2):
                        b = ph3.read(dve, ("up", j, v))
                        conv([gcv[:, j % 2, 2 * v + i, :] for i in range(2)], [PS[:, b, i * T:(i + 1) * T] for i in range(2)],
                             [[ffn_tap(q_, FFT * v + 2 * j + i) for q_ in range(FFN_CONV)] for i in range(2)])[-1]\
                            .then_inc(psum_free[b], 1)
                        ph3.freed(dve, ("up", j, v))
                    if j:
                        gate(j - 1)
                gate(FFT // 2 - 1)
                add_normed(4, "g_ffn_post_2")
                meet(dve, "dve")
            for t in range(TT):
                for g in range(2):
                    dve.wait_ge(S("out_turned"), 2 * t + g + 1)
                    V.tensor_copy(outt[:, t, g * 512:(g + 1) * 512], PS[:, 2 * t + g, :]).then_inc(S("out_copied"), 1)

        @block.gpsimd
        def _(pool):
            def reset_stages(engines):
                pool.wait_ge(idle, engines)
                pool.drain()
                nums = sorted(q.num for q in stages)
                i = 0
                while i < len(nums):
                    j = i
                    while j + 1 < len(nums) and nums[j + 1] == nums[j] + 1:
                        j += 1
                    pool.sem_clear(range(nums[i], nums[j] + 1))
                    i = j + 1
                for g in go.values():
                    pool.sem_inc(g, 1)

            reset_stages(4)

            reset_stages(4)
            with pool.Fori(0, LAYERS) as L:
                reset_stages(4)


_INS = ['x', 'c', 'ctx', 'c_ctx', 'w_mod', 'b_mod', 'norm1_g', 'norm2_g', 'w_in', 'gla_a2_f', 'gla_ab_f', 'gla_a2_b',
        'gla_ab_b', 'gla_onorm_g', 'pool_w', 'pool_scale', 'w_pool_br', 'w_gla_br', 'w_o', 'router_grp_w',
        'router_grp_b', 'router_exp_w', 'router_exp_b', 'moe_w1', 'moe_w3', 'moe_w2', 'final_norm_g', 'w_in_2',
        'dn_conv_2', 'dn_a_log_2', 'dn_dt_bias_2', 'dn_norm_2', 'hg_lb_2', 'hg_norm_2', 'w_out_2', 'g_mix_pre_2',
        'g_mix_post_2', 'g_ffn_pre_2', 'g_ffn_post_2', 'ffn_w_up_2', 'ffn_conv_2', 'ffn_w_down_2']


def kernel(**inputs):
    import numpy as _np
    import concourse.bacc as _bacc
    from concourse import mybir as _mybir
    from concourse.bass_utils import run_bass_kernel_spmd as _run

    nc = _bacc.Bacc("TRN2", target_bir_lowering=False, num_devices=1)
    arrays, handles = {}, {}
    for name in _INS:
        a = _np.ascontiguousarray(inputs[name])
        arrays[f"in_{name}_dram"] = a
        handles[name] = nc.dram_tensor(f"in_{name}_dram", a.shape, _mybir.dt.from_np(a.dtype), kind="ExternalInput").ap()
    table = constants()[1]
    arrays["consts_dram"] = table
    handles["consts"] = nc.dram_tensor("consts_dram", table.shape, _mybir.dt.float32, kind="ExternalInput").ap()
    out = nc.dram_tensor("out_0_dram", (1, 256, 1024), _mybir.dt.float32, kind="ExternalOutput").ap()
    build(nc, handles, out)
    r = _run(nc, [arrays], core_ids=[0])
    return r.results[0]["out_0_dram"]
```

```python
from contextlib import ExitStack

import numpy as np

import concourse.bass as bass
from concourse import mybir

ALU = mybir.AluOpType
ACT = mybir.ActivationFunctionType
F32 = mybir.dt.float32
I32 = mybir.dt.int32
AX = mybir.AxisListType

P = 128
D = 1024
T = 256
KT = D // P
TT = T // P
CH = 64
NCH = T // CH
EPS = 1e-6
BIG = 1e30
NEG = -3e38

POOL_W = 512
POOL_G = 4
GRID_W = 64
ROWS = T // GRID_W
PADW = GRID_W + 16
GH = 4
GDK = 512
GDV = 1024
GATE_NORM = 16.0
N_GRP = 4
N_EXP = 32
D_EXP = 512
SLOTS = 64
PAIRS = N_EXP // 2

DN = 512
DNH = 4
DN_CONV = 4
SA = 256
SAH = 4
SAD = 64
TOPK = 64
HG = 256
D_FF = 2816
FFT = D_FF // P
FFN_CONV = 3
LAYERS = 2

U0, Q0, K0, V0, G0, GT0, LR0 = 0, 512, 1024, 1536, 2560, 3584, 5632
AQ0, AK0, AV0, AZ0, AB0, BQ0, BK0, BV0, BQI0, BKI0, BWI0, CQ0, CI0 = (
    0, 512, 1024, 1536, 2048, 2056, 2312, 2376, 2440, 2696, 2760, 2764, 3276)

SLAB = 4096


def constants():
    i = np.arange(P)
    r, c = i[:, None], i[None, :]
    same = (r // CH) == (c // CH)
    parts = {
        "ident": r == c,
        "ones": np.ones((P, P)),
        "incl": same & (r <= c),
        "rev": same & (r >= c),
        "blk": same,
        "before": r < c,
    }
    for lv in range(6):
        b = 1 << lv
        parts[f"lv{lv}"] = ((r // (2 * b)) == (c // (2 * b))) & ((r // b) % 2 == 0) & ((c // b) % 2 == 1)
    parts["diag16"] = ((r // 16) == (c // 16)) & (r <= c)
    parts["iota"] = np.broadcast_to(np.arange(SLOTS), (P, SLOTS))
    parts["desc"] = np.broadcast_to(N_EXP - np.arange(N_EXP), (P, N_EXP))
    parts["thr"] = np.broadcast_to(np.arange(4) * SLOTS, (P, 4))
    t = np.arange(T)
    adm = []
    for tt in range(TT):
        q = (tt * P + i)[:, None] // CH
        adm.append(np.where(t[None, :] // CH <= q, 0.0, -BIG))
    parts["adm"] = np.concatenate(adm, 1)
    cnt = []
    g = np.arange(GRID_W)
    for w in (2, 4, 8, 16):
        cnt.append(1.0 / (np.minimum(g + w // 2, GRID_W) - np.maximum(g - w // 2, 0)))
    parts["rcnt"] = np.broadcast_to(np.concatenate(cnt), (P, 4 * GRID_W))
    parts["reset"] = np.broadcast_to(np.concatenate([t != 0, t % CH != 0]), (P, 2 * T))
    parts["eps"] = np.full((P, 1), EPS)
    parts["one"] = np.ones((P, 1))
    offs, arrs, at = {}, [], 0
    for k, v in parts.items():
        v = np.asarray(v, np.float32)
        offs[k] = (at, v.shape[1])
        at += v.shape[1]
        arrs.append(v)
    return offs, np.ascontiguousarray(np.concatenate(arrs, 1))


ROWS_A = [("c", 8), ("c_ctx", 8), ("norm1_g", 8), ("norm2_g", 8), ("b_mod", 48), ("gla_ab_f", 4), ("gla_ab_b", 4),
          ("pool_scale", 4), ("gla_onorm_g", 2), ("final_norm_g", 8)]
ROWS_B = [("g_mix_pre_2", 8), ("g_mix_post_2", 8), ("g_ffn_pre_2", 8), ("g_ffn_post_2", 8), ("dn_conv_2", 48),
          ("dn_norm_2", 1), ("hg_norm_2", 1), ("hg_lb_2", 2)]
NA = sum(n for _, n in ROWS_A)
NB = sum(n for _, n in ROWS_B)
NC3 = FFN_CONV * 2 * FFT
NC_HEAD = P - NB
LCOLS = NB + NC3


def row_at(rows, name):
    at = 0
    for n, k in rows:
        if n == name:
            return at
        at += k
    raise KeyError(name)


def build(nc, W, out):
    offs, _ = constants()
    ctx = ExitStack()
    with ctx:
        def sb(name, shape, dt=F32):
            return ctx.enter_context(nc.sbuf_tensor(name, shape, dt))

        sems = {}

        def sem(name):
            if name not in sems:
                sems[name] = ctx.enter_context(nc.semaphore(name))
            return sems[name]

        cst = sb("cst", [P, sum(n for _, n in offs.values())])

        def C(name):
            a, n = offs[name]
            return cst[:, a:a + n]

        ring = sb("ring", [P, 6, SLAB])
        colsA = sb("colsA", [P, NA])
        colsL = sb("colsL", [P, 2, LCOLS])
        logs = sb("logs", [P, 2, 8])
        lbc = sb("lbc", [P, 2, 4])
        mods = sb("mods", [P, 48, 2])
        ada = sb("ada", [P, 8, KT])
        small = sb("small", [P, 64])
        ARENA = 22100
        arena = sb("arena", [P, ARENA])
        xT = sb("xT", [P, KT, T])

        class Area:

            def __init__(self, view, size):
                self.view, self.size, self.at = view, size, 0

            def take(self, *dims):
                n = int(np.prod(dims))
                assert self.at + n <= self.size, (self.at, n, self.size)
                v = self.view[:, self.at:self.at + n]
                self.at += n
                if len(dims) == 1:
                    return v
                names = "abcd"[:len(dims)]
                return v.rearrange("p (%s) -> p %s" % (" ".join(names), " ".join(names)),
                                   **{k: d for k, d in zip(names[1:], dims[1:])})

        ringflat = ring[:, :, :].rearrange("p s n -> p (s n)")

        PS = ctx.enter_context(nc.psum_tensor("PS", [P, 8, 512], F32))

        def colA(name, j=0, n=1):
            a = row_at(ROWS_A, name) + j
            return colsA[:, a:a + n]

        params_in = sem("params_in")
        x_in = sem("x_in")
        first_in = sem("first_params_in")
        router_in = sem("router_weights_in")
        consts_in = sem("consts_in")
        wl = [sem(f"slab_in{i}") for i in range(3)]
        wm = [sem(f"mod_slab_in{i}") for i in range(2)]
        ml = [sem(f"expert_in{i}") for i in range(6)]
        w1_read, w3_read, y_full = sem("w1_read"), sem("w3_read"), sem("y_full")
        ll = [sem(f"layer_slab_in{i}") for i in range(3)]
        go = {n: sem(f"go_{n}") for n in ("pe", "sp", "act", "dve")}
        out_done = sem("out_done")
        psum_full = sem("psum_full")
        psum_free = [sem(f"psum_free{b}") for b in range(8)]
        idle = sem("idle")
        stages = [psum_full, *psum_free, idle, *ll]

        def S(name):
            if name not in sems:
                stages.append(sem(name))
            return sems[name]

        class Phase:

            def __init__(self):
                self.units = []

            def bank(self, pe, key):
                u = len(self.units)
                self.units.append(key)
                if u >= 8:
                    pe.wait_ge(psum_free[u % 8], u // 8)
                return u % 8

            def read(self, eng, key):
                u = self.units.index(key)
                eng.wait_ge(psum_full, u + 1)
                return u % 8

            def freed(self, eng, key):
                u = self.units.index(key)
                eng.wait_ge(psum_free[u % 8], u // 8 + 1)

        ph1, ph2, ph3 = Phase(), Phase(), Phase()

        class Chain:

            def __init__(self, eng, name):
                self.eng, self.s, self.n = eng, S(name), 0

            def __call__(self, ins):
                self.n += 1
                ins.then_inc(self.s, 1)
                self.eng.wait_ge(self.s, self.n)

        def meet(eng, n):
            eng.drain().then_inc(idle, 1)
            eng.wait_ge(go[n], 1)
            eng.nop().then_inc(go[n], -1)

        out_T = out.rearrange("a t d -> (a t) d")

        A1 = Area(arena, ARENA)
        X1 = Area(ringflat[:, 3 * SLAB:], 3 * SLAB)
        hboth = A1.take(KT, 2 * T)
        vtok = A1.take(4, GDV)
        kT = A1.take(GH, 2 * T)
        qT = A1.take(GH, T)
        la_flat = A1.take(2 * GH * 2 * T)
        la = la_flat.rearrange("p (d h t) -> p d h t", d=2, h=GH)
        krt = A1.take(2, TT, GDK)
        s0 = A1.take(2, GH, 256)
        sg = A1.take(KT, T)
        poolw = A1.take(POOL_G, P)
        rowsA = sg.rearrange("p k t -> p (k t)")[0:NA, 0:P]
        rowsB = sg.rearrange("p k t -> p (k t)")[:, P:3 * P].rearrange("p (l n) -> p l n", l=2)
        rowsC = sg.rearrange("p k t -> p (k t)")[0:NC3 - NC_HEAD, 3 * P:5 * P].rearrange("p (l n) -> p l n", l=2)
        cum_flat = X1.take(2 * GH * 2 * T)
        cum = cum_flat.rearrange("p (d h t) -> p d h t", d=2, h=GH)
        qdki = X1.take(2 * 2 * GH * T)
        qd = qdki[:, 0:2 * GH * T].rearrange("p (d h t) -> p d h t", d=2, h=GH)
        ki = qdki[:, 2 * GH * T:].rearrange("p (d h t) -> p d h t", d=2, h=GH)
        e1 = X1.take(GH, T)
        e2 = X1.take(GH, T)
        lrT = X1.take(2 * T)
        a2 = X1.take(2, GDK)
        wlr = X1.take(KT, 32)
        xraw = cum_flat.rearrange("p (s t d) -> p s t d", s=2, t=TT)
        sqb = la_flat.rearrange("p (k t) -> p k t", k=KT)
        rstd = e1.rearrange("p h t -> p (h t)")[:, 0:2 * T]
        mslots = [v.rearrange("p (k n) -> p k n", k=KT) for v in (cum_flat, qdki)]
        msums = {}
        for i, j in enumerate((2, 3)):
            for v in range(2):
                msums[(j, v)] = vtok[:, 2 * i + v, 0:512]
        for j in range(4, 12):
            msums[(j, 0)] = la_flat[:, (j - 4) * 512:(j - 3) * 512]
        Sx = la_flat[:, 0:3072].rearrange("p (i d n v) -> p i d n v", i=2, d=2, n=3)
        scT = e1.rearrange("p h (t c) -> p h t c", t=TT)
        oT = cum_flat[:, 0:2048].rearrange("p (j t) -> p j t", j=KT)
        osq = cum_flat[:, 2048:4096].rearrange("p (j t) -> p j t", j=KT)
        pads = [qdki[:, i * 1280:(i + 1) * 1280].rearrange("p (g r w) -> p g r w", g=POOL_G, r=ROWS) for i in range(3)]
        pooled = e2
        yp = kT.rearrange("p h t -> p (h t)")[:, 0:1024].rearrange("p (g t) -> p g t", g=POOL_G)

        def gates(j):
            if j < 4:
                return hboth[:, 4 + j:6 + j, 0:T]
            if j < 8:
                return kT.rearrange("p h t -> p (h t)")[:, 1024 + (j - 4) * T:1024 + (j - 2) * T].rearrange("p (j t) -> p j t", j=2)
            return vtok.rearrange("p a b -> p (a b)")[:, (j - 8) * T:(j - 6) * T].rearrange("p (j t) -> p j t", j=2)

        mixed = krt.rearrange("p d t n -> p (d t n)").rearrange("p (j t) -> p j t", j=KT)
        csil = small[:, 0:16].rearrange("p (v k) -> p k v", v=2)
        lastx = small[:, 16:48].rearrange("p (d h n) -> p d h n", d=2, h=GH)
        dec = ada[:, 4:8, :].rearrange("p a b -> p (a b)").rearrange("p (d h n) -> p d h n", d=2, h=GH)
        lastc = small[:, 48:52]

        def mod(m, v, k):
            return mods[:, 8 * m + k, v:v + 1]

        A2 = Area(arena, ARENA)
        h2T = A2.take(KT, T)
        h2n = A2.take(KT, T)
        h2t = A2.take(TT, D)
        hg = A2.take(KT, P)
        s1 = A2.take(512)
        hidt = A2.take(512)
        hid = A2.take(4, P)
        ytok = A2.take(D)
        PT = A2.take(T)
        sel = A2.take(TT, 2, SLOTS)
        selw = A2.take(TT, 2, SLOTS)
        rw = A2.take(KT, N_GRP + N_EXP)
        rb = A2.take(N_GRP + N_EXP)
        rstd2 = A2.take(T)
        lg = A2.take(TT, N_GRP + N_EXP)
        m32 = [A2.take(TT, N_EXP) for _ in range(8)]
        m8 = [A2.take(TT, N_GRP) for _ in range(4)]
        m1 = [A2.take(TT) for _ in range(10)]
        totals = A2.take(N_EXP)
        ranks = A2.take(TT, N_EXP + 2)
        weights = A2.take(TT, N_EXP + 2)
        mx1 = A2.take(4)
        rounds_i = A2.take(1).bitcast(I32)

        A3 = Area(arena, ARENA)
        X3 = Area(ringflat[:, 3 * SLAB:], 3 * SLAB)
        hT = A3.take(KT, T)
        cat = A3.take(KT, T)
        sc3 = A3.take(KT, T)
        cs = A3.take(12, T)
        sz = A3.take(DNH, T)
        eG = A3.take(DNH, T)
        DT = A3.take(DNH, TT, P)
        MT = A3.take(DNH, TT, P)
        QK = A3.take(DNH, TT, P)
        XI = A3.take(DNH, TT, P)
        XIT = A3.take(DNH, TT, P)
        BT = [A3.take(DNH, TT, P) for _ in range(2)]
        Z = A3.take(DNH, TT, P)
        kd = A3.take(TT, DNH, P)
        kvb = sc3.rearrange("p k t -> p (k t)").rearrange("p (a t h c) -> p a t h c", a=2, t=TT, h=DNH)
        kb, vb = kvb[:, 0], kvb[:, 1]
        gx, bx = Z, BT[1]
        u = BT[0].rearrange("p h t c -> p (h t c)").rearrange("p (t h c) -> p t h c", t=TT, h=DNH)
        wk = BT[1].rearrange("p h t c -> p h (t c)")
        Sd = [v.rearrange("p h t c -> p (h t c)")[:, i * 512:(i + 1) * 512].rearrange("p (h v) -> p h v", h=DNH)
              for v, i in ((XI, 0), (XI, 1), (Z, 0))]
        qb = X3.take(2, T)
        kbb = X3.take(T)
        qi = X3.take(2, T)
        kii = X3.take(T)
        vtk = X3.take(TT, SAD)
        cq = X3.take(2, T)
        cf = X3.take(2, T)
        cit = X3.take(TT, HG)
        cg = X3.take(2, T)
        kc = X3.take(2, T)
        room = 3 * SLAB - X3.at
        shared = X3.take(room)
        XB = Area(shared, room)
        relu = XB.take(2, 2, T)
        score = XB.take(TT, T)
        work = XB.take(TT, T)
        pr = XB.take(TT, SAH, T)
        pT = XB.take(SAH, TT, T)
        XC = Area(shared, room)
        args = XC.take(3, 2, 2 * T)
        Bc = XC.take(2, T)
        eB = XC.take(2, T)
        eR = XC.take(2, T)
        AT = XC.take(2, 2, TT, P)
        AT2 = XC.take(2, TT, P)
        kdt = XC.take(TT, HG)
        Sh = XC.take(3, 2, P)
        col = sb("col", [P, LCOLS + 8])
        tok = sb("tok", [P, 120])
        TK = Area(tok, 120)
        ab = TK.take(TT, 8)
        beta, gt, zt, Gc, eGc, eRc, bG = (TK.take(TT, 4) for _ in range(7))
        glast = TK.take(4, 4)
        wi = TK.take(TT, 4)
        hlast = TK.take(2, NCH)
        m8k = TK.take(TT, 8)
        gated = A3.view[:, 4096:4096 + FFT * T].rearrange("p (f t) -> p f t", f=FFT)
        gcv = A3.view[:, 10240:10240 + 2048].rearrange("p (b j t) -> p b j t", b=2, j=4)
        fT = A3.view[:, 12288:12288 + 2048].rearrange("p (k t) -> p k t", k=KT)
        fsq = A3.view[:, 14336:14336 + 2048].rearrange("p (k t) -> p k t", k=KT)
        rs = A3.view[:, 16384:16384 + 256]
        rsb = A3.view[:, 14336:14336 + 2048]
        outt = fT.rearrange("p k t -> p (k t)").rearrange("p (t d) -> p t d", t=TT)

        def cl(name, j=0, n=1):
            a = row_at(ROWS_B, name) + j
            return col[:, a:a + n]

        def ffn_tap(j, f):
            return col[:, NB + j * 2 * FFT + f:NB + j * 2 * FFT + f + 1]

        PARAMS = []
        at = 0
        for name, n in ROWS_A:
            PARAMS.append((rowsA[at:at + n, :], W[name].rearrange(
                {1: "(r p) -> r p", 2: "a (r p) -> (a r) p"}[len(W[name].shape)], p=P)))
            at += n
        N_FIRST = len(PARAMS)
        for l in range(LAYERS):
            at = 0
            for name, n in ROWS_B:
                v = W[name][l]
                if name == "dn_conv_2":
                    v = v.rearrange("a (r p) -> (a r) p", p=P)
                elif name != "hg_norm_2":
                    v = v.rearrange("(r p) -> r p", p=P)
                if name == "hg_norm_2":
                    for i in range(2):
                        PARAMS.append((rowsB[at:at + 1, l, i * 64:(i + 1) * 64], v.rearrange("(r p) -> r p", r=1)))
                else:
                    PARAMS.append((rowsB[at:at + n, l, :], v))
                at += n
            v = W["ffn_conv_2"][l].rearrange("a (r p) -> (a r) p", p=P)
            PARAMS.append((rowsB[NB:P, l, :], v[0:NC_HEAD, :]))
            PARAMS.append((rowsC[:, l, :], v[NC_HEAD:NC3, :]))
            for i, name in enumerate(("dn_a_log_2", "dn_dt_bias_2")):
                PARAMS.append((logs[:, l, 4 * i:4 * i + 4], W[name][l].partition_broadcast(P)))
        PARAMS.append((wlr, W["w_in"][0][:, LR0:LR0 + 32].rearrange("(k p) n -> p k n", p=P)))
        PARAMS.append((poolw, W["pool_w"][0].rearrange("g c e -> c g e")))
        PARAMS.append((a2[0:16, 0, :], W["gla_a2_f"][0]))
        PARAMS.append((a2[16:32, 1, :], W["gla_a2_b"][0]))
        N_PARAM = len(PARAMS)

        def cols(w, a, n=512):
            return w[:, a:a + n].rearrange("(k p) n -> p k n", p=P)

        wmod, win = W["w_mod"][0], W["w_in"][0]
        SL1 = [("mod", j, cols(wmod, 512 * j)) for j in range(3)]
        SL1 += [("k", 0, cols(win, K0)), ("v", 0, cols(win, V0)), ("v", 1, cols(win, V0 + 512)),
                ("q", 0, cols(win, Q0)), ("g", 0, cols(win, G0)),
                ("g", 1, cols(win, G0 + 512)), ("u", 0, cols(win, U0))]
        SL1 += [("gate", j, cols(win, GT0 + 512 * j)) for j in range(4)]
        SL1 += [("pbr", 0, W["w_pool_br"][0].rearrange("(k p) n -> p k n", p=P)),
                ("gbr", 0, cols(W["w_gla_br"][0], 0)), ("gbr", 1, cols(W["w_gla_br"][0], 512)),
                ("wo", 0, cols(W["w_o"][0], 0)), ("wo", 1, cols(W["w_o"][0], 512))]
        where1 = {(n, j): i for i, (n, j, _) in enumerate(SL1)}
        MSLOT = {j: (j % 2 == 1) * 1 for j in range(3, 12)}
        mloads = {j: 16 * len([i for i in range(3, j + 1) if i % 2 == j % 2]) for j in range(3, 12)}
        msum_at = {j: 2 * (j - 1) if j < 4 else j + 1 for j in range(2, 12)}
        last_unit1 = {}

        def lw(name, L, r0, r1, c0, c1):
            return W[name][bass.ds(L, 1), r0:r1, c0:c1].rearrange("a (k p) n -> p (a k) n", p=P)

        SL3 = []
        for name, a, b_ in (("b", AB0, BQI0), ("bi", BQI0, CQ0), ("aq", AQ0, AK0), ("ak", AK0, AV0), ("av", AV0, AZ0),
                            ("cqf", CQ0, CI0), ("cig", CI0, CI0 + 512), ("az", AZ0, AB0)):
            SL3.append((name, 0, [("w_in_2", 0, D, a, b_, 0)]))
        for j in range(2):
            SL3.append(("out", j, [("w_out_2", 0, D, 512 * j, 512 * j + 512, 0)]))
        for j in range(FFT // 2):
            SL3.append(("up", j, [("ffn_w_up_2", 0, D, 256 * j, 256 * j + 256, 0),
                                  ("ffn_w_up_2", 0, D, D_FF + 256 * j, D_FF + 256 * j + 256, 256)]))
        for j in range(0, FFT, 4):
            SL3.append(("down", j // 4, [("ffn_w_down_2", j * P, min(j + 4, FFT) * P, 0, D, 0)]))
        where3 = {(n, j): i for i, (n, j, _) in enumerate(SL3)}
        loads3, total3 = [], [0, 0, 0]
        for i, (_, _, parts) in enumerate(SL3):
            total3[i % 3] += 16 * len(parts)
            loads3.append(total3[i % 3])
        last_unit3 = {}

        KV_UNITS = (((0, 0), (1, 2)), ((0, 1), (1, 3)), ((0, 2),), ((1, 1),))

        def slot(i, k=KT):
            return ring[:, i % 3, :].rearrange("p (k n) -> p k n", k=k)

        block = ctx.enter_context(nc.Block())

        @block.tensor
        def _(pe):
            mm = nc.tensor.matmul

            def tiles(ph, key, parts, K, start=0):
                b = ph.bank(pe, key)
                for place, lhsT, rhs in parts:
                    for k in range(K):
                        last = mm(PS[:, b, place] if not isinstance(place, tuple) else PS[place[0], b, place[1]],
                                  lhsT(k), rhs(k), start=(k == 0), stop=(k == K - 1))
                last.then_inc(psum_full, 1)

            def slab(name, j, k=KT):
                i = where1[(name, j)]
                pe.wait_ge(wl[i % 3], 16 * (i // 3 + 1))
                return slot(i, k)

            pe.wait_ge(consts_in, 16)
            pe.wait_ge(x_in, 32)
            for s, name in enumerate(("ctxT", "xT")):
                for kp in range(KT // 2):
                    b = ph1.bank(pe, (name, kp))
                    for k in (0, 1):
                        for t in range(TT):
                            last = nc.tensor.transpose(PS[:, b, k * T + t * P:k * T + (t + 1) * P],
                                                       xraw[:, s, t, (2 * kp + k) * P:(2 * kp + k + 1) * P], C("ident"))
                    last.then_inc(psum_full, 1)
            pe.wait_ge(first_in, 16 * N_FIRST)
            b = ph1.bank(pe, "colsA")
            nc.tensor.transpose(PS[:, b, 0:NA], rowsA[:, :], C("ident")[0:NA, 0:NA]).then_inc(psum_full, 1)
            def modulation(j):
                b = ph1.bank(pe, ("mod", j))
                w = slab("mod", j)
                for f in range(4):
                    for k in range(KT):
                        last = mm(PS[:, b, 2 * f:2 * f + 2], w[:, k, f * P:(f + 1) * P], csil[:, k, :],
                                  start=(k == 0), stop=(k == KT - 1))
                last.then_inc(psum_full, 1)
                last_unit1[where1[("mod", j)]] = ("mod", j)

            def modulation_sums(j, vectors=1):
                b = ph1.bank(pe, ("mod", j))
                pe.wait_ge(S("mod_sum"), msum_at[j])
                for f in range(4):
                    for v in range(vectors):
                        last = mm(PS[:, b, 2 * f + v:2 * f + v + 1], msums[(j, v)][:, f * P:(f + 1) * P], C("one"),
                                  start=True, stop=True)
                last.then_inc(psum_full, 1)

            pe.wait_ge(S("silu_c"), 1)
            modulation(0)
            pe.wait_ge(S("squares"), 2)
            tiles(ph1, "ms", [(slice(0, 512), lambda k: C("ones"), lambda k: sqb[:, k, :])], KT)
            modulation(1)
            modulation_sums(2, 2)
            modulation_sums(3, 2)

            def when_ready(counts, view):
                seen = set()

                def rows(k):
                    if k not in seen:
                        seen.add(k)
                        for name, n in counts(k):
                            pe.wait_ge(S(name), n)
                    return view(k)
                return rows


            def project(name, j, key, rhs, ntile=4, k=KT):
                w = slab(name, j, k)
                n = 2 * T if name == "k" else T
                per = 512 // n
                for g in range(ntile // per):
                    tiles(ph1, (key, j, g), [
                        (slice(i * n, (i + 1) * n), lambda k, f=g * per + i: w[:, k, f * P:(f + 1) * P], rhs)
                        for i in range(per)], k)
                last_unit1[where1[(name, j)]] = (key, j, ntile // per - 1)

            hx = lambda k: hboth[:, k, T:2 * T]
            project("k", 0, "k", when_ready(lambda k: (("h1_context", k + 1), ("h1_tokens", k + 1)),
                                            lambda k: hboth[:, k, :]))
            modulation_sums(4)
            pe.wait_ge(params_in, 16 * (N_PARAM - N_FIRST))
            b = ph1.bank(pe, "colsL")
            for l in range(LAYERS):
                nc.tensor.transpose(PS[:, b, l * LCOLS:l * LCOLS + P], rowsB[:, l, :], C("ident"))
                n = NC3 - NC_HEAD
                last = nc.tensor.transpose(PS[:, b, l * LCOLS + P:(l + 1) * LCOLS], rowsC[:, l, :],
                                           C("ident")[0:n, 0:n])
            last.then_inc(psum_full, 1)
            for j in range(2):
                w = slab("v", j)
                for t in range(4):
                    tiles(ph1, ("v", j, t), [(slice(0, 512), lambda k: hboth[:, k, t * P:(t + 1) * P],
                                              lambda k: w[:, k, :])], KT)
                last_unit1[where1[("v", j)]] = ("v", j, 3)
                for m in ((5, 6, 7), (8, 9))[j]:
                    modulation_sums(m)
            tiles(ph1, "lr", [((slice(0, 32), slice(0, 512)), lambda k: wlr[:, k, :], lambda k: hboth[:, k, :])], KT)
            modulation_sums(10)
            modulation_sums(11)
            ph1.freed(pe, "lr")
            for d in range(2):
                for h in range(GH):
                    tiles(ph1, ("z", d, h), [(slice(0, 512), lambda k: a2[0:32, d, h * P:(h + 1) * P],
                                              lambda k: lrT[0:32, :])], 1)
            project("q", 0, "q", hx)
            project("g", 0, "g", hx)
            project("g", 1, "g", hx)

            def by_token(name, src, waits):
                for d in range(2):
                    pe.wait_ge(S(waits), d + 1)
                    for t in range(TT):
                        b = ph1.bank(pe, (name, d, t))
                        for h in range(GH):
                            last = nc.tensor.transpose(PS[:, b, h * P:(h + 1) * P], src[d][:, h, t * P:(t + 1) * P],
                                                       C("ident"))
                        last.then_inc(psum_full, 1)

            by_token("krc", (e1, e2), "krc_ready")
            project("u", 0, "u", hx)
            for d in range(2):
                for t in range(TT):
                    ph1.freed(pe, ("krc", d, t))
            for d in range(2):
                for hp in range(2):
                    tiles(ph1, ("s0", d, hp), [
                        (slice(i * 256, (i + 1) * 256),
                         lambda t, h=2 * hp + i: krt[:, d, t, h * P:(h + 1) * P],
                         lambda t, h=2 * hp + i: vtok[:, t, h * 256:(h + 1) * 256]) for i in range(2)], TT)
            by_token("krx", (e1, e2), "krx_ready")
            pe.wait_ge(S("qdki_ready"), 4)
            for h in range(GH):
                b = ph1.bank(pe, ("sc", h))
                for d in range(2):
                    for t in range(TT):
                        at = slice(t * P, (t + 1) * P)
                        o = (2 * d + t) * P
                        last = mm(PS[:, b, o:o + P], ki[:, d, h, at], qd[:, d, h, at], start=True, stop=True)
                last.then_inc(psum_full, 1)
            for d in range(2):
                for t in range(TT):
                    ph1.freed(pe, ("krx", d, t))
            for h in range(GH):
                for n, group in enumerate(KV_UNITS):
                    b = ph1.bank(pe, ("kv", h, n))
                    for d, c in group:
                        r = slice(CH * (c % 2), CH * (c % 2) + CH)
                        last = mm(PS[:, b, d * 256:(d + 1) * 256], krt[r, d, c // 2, h * P:(h + 1) * P],
                                  vtok[r, 2 + c // 2, h * 256:(h + 1) * 256], start=True, stop=True)
                    last.then_inc(psum_full, 1)
                w = slab("gate", h // 2)
                tiles(ph1, ("gate", h // 2, h % 2), [(slice(i * T, (i + 1) * T),
                                                      lambda k, f=2 * (h % 2) + i: w[:, k, f * P:(f + 1) * P], hx)
                                                     for i in range(2)], KT)
                last_unit1[where1[("gate", h // 2)]] = ("gate", h // 2, h % 2)
                pe.wait_ge(S("sc_ready"), h + 1)
                for n in (2, 3):
                    ph1.freed(pe, ("kv", h, n))
                b = ph1.bank(pe, ("o", h))
                for vt in range(2):
                    for t in range(TT):
                        o = vt * T + t * P
                        vs = slice(h * 256 + vt * P, h * 256 + (vt + 1) * P)
                        mm(PS[:, b, o:o + P], vtok[:, 2 + t, vs], scT[:, h, t, :], start=(vt == 0 and t == 0),
                           stop=False, skip_group_check=True)
                        for c in (2 * t, 2 * t + 1):
                            for d in range(2):
                                n = c if d == 0 else NCH - 1 - c
                                st = (s0[:, d, h, vt * P:(vt + 1) * P] if n == 0 else
                                      Sx[:, h % 2, d, n - 1, vt * P:(vt + 1) * P])
                                oo = o + CH * (c % 2)
                                last = mm(PS[:, b, oo:oo + CH], st, qd[:, d, h, c * CH:(c + 1) * CH],
                                          start=False,
                                          stop=(vt == 1 and c == NCH - 1 and d == 1), skip_group_check=True)
                last.then_inc(psum_full, 1)
            project("gate", 2, "gate", hx)
            pe.wait_ge(S("osq_ready"), 1)
            for hp in range(2):
                tiles(ph1, ("oms", hp), [(slice(i * T, (i + 1) * T), lambda k: C("ones"),
                                          lambda k, h=2 * hp + i: osq[:, 2 * h + k, :]) for i in range(2)], 2)
            project("gate", 3, "gate", hx)
            pe.wait_ge(S("pooled_ready"), 1)
            for g in range(2):
                tiles(ph1, ("yp", g), [(slice(i * T, (i + 1) * T), lambda k, f=2 * g + i: poolw[:, f, :],
                                        lambda k, f=2 * g + i: pooled[:, f, :]) for i in range(2)], 1)
            for g in range(2):
                ph1.freed(pe, ("yp", g))
            w = slab("pbr", 0, 4)
            for g in range(4):
                tiles(ph1, ("pbr", g), [(slice(i * T, (i + 1) * T), lambda k, f=2 * g + i: w[:, k, f * P:(f + 1) * P],
                                         lambda k: yp[:, k, :]) for i in range(2)], 4)
            last_unit1[where1[("pbr", 0)]] = ("pbr", 3)
            pe.wait_ge(S("og_ready"), 1)
            for j in range(2):
                project("gbr", j, "gbr", lambda k: oT[:, k, :])
            mixed_rows = when_ready(lambda k: (("mixed_ready", k // 2 + 1),), lambda k: mixed[:, k, :])
            for j in range(2):
                project("wo", j, "wo", mixed_rows)
            b = ph1.bank(pe, "ms2")
            for k in range(KT):
                if k % 2 == 0:
                    pe.wait_ge(S("sq2"), k // 2 + 1)
                last = mm(PS[:, b, 0:T], C("ones"), h2n[:, k, :], start=(k == 0), stop=(k == KT - 1))
            last.then_inc(psum_full, 1)
            pe.wait_ge(S("h2_ready"), KT)
            meet(pe, "pe")

            pe.wait_ge(router_in, 64)
            b = ph2.bank(pe, "route")
            for t in range(TT):
                for k in range(KT):
                    mm(PS[:, b, t * 64:t * 64 + 36], h2T[:, k, t * P:(t + 1) * P], rw[:, k, :], start=(k == 0), stop=False)
                last = mm(PS[:, b, t * 64:t * 64 + 36], C("ones")[0:1, :], rb[0:1, :], start=False, stop=True)
            last.then_inc(psum_full, 1)
            for t in range(TT):
                for g in range(2):
                    b = ph2.bank(pe, ("h2t", t, g))
                    for k in range(4):
                        last = nc.tensor.transpose(PS[:, b, k * P:(k + 1) * P], h2T[:, 4 * g + k, t * P:(t + 1) * P],
                                                   C("ident"))
                    last.then_inc(psum_full, 1)
            pe.wait_ge(S("chosen"), 1)
            b = ph2.bank(pe, "rank")
            mm(PS[:, b, 0:32], C("before"), m32[0][:, 0], start=True, stop=True)
            mm(PS[:, b, 32:64], C("ones"), m32[0][:, 0], start=True, stop=False)
            mm(PS[:, b, 32:64], C("before"), m32[0][:, 1], start=False, stop=True)
            mm(PS[:, b, 64:96], C("ones"), m32[0][:, 0], start=True, stop=False)
            mm(PS[:, b, 64:96], C("ones"), m32[0][:, 1], start=False, stop=True).then_inc(psum_full, 1)
            for key in list(ph2.units):
                ph2.freed(pe, key)
            pe.wait_ge(S("moe_zeroed"), 2)
            for b in range(4):
                last = mm(PS[:, b, :], ytok[:, 0:P], ytok[:, 0:512], start=True, stop=True)
                if b in (2, 3):
                    last.then_inc(S("gathered") if b == 2 else S("pt_turned"), 1)
            pe.wait_ge(S("rounds_ready"), 1)
            rounds = pe.value_load(rounds_i[0:1, 0:1])

            def scatter():
                for f in range(KT):
                    last = mm(PS[:, f // 2, (f % 2) * T:(f % 2 + 1) * T], ytok[:, f * P:(f + 1) * P], PT,
                              start=False, stop=False, skip_group_check=True)
                return last

            def expert_slab(s, k):
                return ring[:, s, :].rearrange("p (k n) -> p k n", k=k)

            with pe.Fori(0, rounds) as r:
                with pe.Fori(0, PAIRS) as p:
                    i1 = pe.snap(r * PAIRS + p + 1)
                    pe.wait_ge(S("sel_ready"), i1)
                    pe.wait_ge(S("hid_ready"), i1)
                    for f in range(KT):
                        for t in range(TT):
                            last = mm(PS[:, 4 + f // 4, (f % 4) * P:(f % 4 + 1) * P], h2t[:, t, f * P:(f + 1) * P],
                                      sel[:, t].rearrange("p e s -> p (e s)"), start=(t == 0), stop=(t == TT - 1))
                    last.then_inc(S("gathered"), 1)
                    pe.wait_ge(S("y_lo"), i1)
                    pe.wait_ge(S("y_hi"), i1)
                    pe.wait_ge(S("pt_ready"), i1)
                    scatter()
                    pe.wait_ge(S("selw_ready"), i1)
                    for t in range(TT):
                        last = nc.tensor.transpose(PS[:, 6, t * P:(t + 1) * P],
                                                   selw[:, t].rearrange("p e s -> p (e s)"), C("ident"))
                    last.then_inc(S("pt_turned"), 1)
                    pe.wait_ge(S("hg_lo"), i1)
                    pe.wait_ge(S("hg_hi"), i1)
                    for j in range(2):
                        for e in range(2):
                            pe.wait_ge(ml[2 * j + e], i1 * 16)
                        for k in range(KT):
                            for e in range(2):
                                last = mm(PS[e * SLOTS:(e + 1) * SLOTS, 4 + j, :], hg[:, k, e * SLOTS:(e + 1) * SLOTS],
                                          expert_slab(2 * j + e, KT)[:, k, :], start=(k == 0), stop=(k == KT - 1))
                        last.then_inc(w3_read if j else w1_read, 1)
                    pe.wait_ge(S("hidt_ready"), i1)
                    for f in range(4):
                        last = nc.tensor.transpose(PS[:, 4, f * P:(f + 1) * P], hidt[:, f * P:(f + 1) * P], C("ident"))
                    last.then_inc(S("hid_turned"), 1)
                    pe.wait_ge(S("pt_ready"), i1 + 1)
                    pe.wait_ge(S("hid_ready"), i1 + 1)
                    for e in range(2):
                        pe.wait_ge(ml[4 + e], i1 * 16)
                    for n in range(2):
                        for f in range(4):
                            for e in range(2):
                                last = mm(PS[e * SLOTS:(e + 1) * SLOTS, 6 + n, :], hid[:, f, e * SLOTS:(e + 1) * SLOTS],
                                          expert_slab(4 + e, 4)[:, f, n * 512:(n + 1) * 512], start=(f == 0), stop=(f == 3))
                    last.then_inc(y_full, 1)
            pe.wait_ge(S("evacuated"), 2)
            scatter().then_inc(S("moe_out"), 1)
            for k in range(KT):
                if k % 4 == 0:
                    pe.wait_ge(S("sq3"), k // 4 + 1)
                last = mm(PS[:, 4, 0:T], C("ones"), h2n[:, k, :], start=(k == 0), stop=(k == KT - 1))
            last.then_inc(S("ms3"), 1)
            meet(pe, "pe")

            half = lambda i: slice(i * T, (i + 1) * T)

            def slab3(name, j=0, k=KT, n=512):
                i = where3[(name, j)]
                pe.wait_ge(ll[i % 3], loads3[i])
                return ring[:, i % 3, 0:k * n].rearrange("p (k n) -> p k n", k=k)

            def by_feature(w, key, c0, ntile, rhs, K=KT):
                for g in range(0, ntile, 2):
                    tiles(ph3, (key, g // 2), [(half(i), lambda k, f=g + i: w[:, k, c0 + f * P:c0 + (f + 1) * P], rhs)
                                               for i in range(2)], K)

            def square_sums(key, src, waits):
                b = ph3.bank(pe, key)
                for k in range(KT):
                    if k in waits:
                        waits[k]()
                    last = mm(PS[:, b, half(0)], C("ones"), src[:, k, :], start=(k == 0), stop=(k == KT - 1))
                last.then_inc(psum_full, 1)

            def stage(name, n=1):
                return lambda: pe.wait_ge(S(name), n)

            def turn(key, parts):
                b = ph3.bank(pe, key)
                for i, v in enumerate(parts):
                    last = nc.tensor.transpose(PS[:, b, i * P:(i + 1) * P], v, C("ident"))
                last.then_inc(psum_full, 1)

            with pe.Fori(0, LAYERS) as L:
                h = lambda k: hT[:, k, :]
                square_sums("ms0", sc3, {})

                w = slab3("b", n=BQI0 - AB0)

                def by_tok(w, c0, n, t):
                    return (lambda k: hT[:, k, t * P:(t + 1) * P], lambda k: w[:, k, c0:c0 + n])

                first = when_ready(lambda k: (("h_ready3", k + 1),), h)
                tiles(ph3, "ab", [(slice(t * 8, t * 8 + 8), lambda k, t=t: first(k)[:, t * P:(t + 1) * P],
                                   lambda k: w[:, k, 0:8]) for t in range(TT)], KT)
                by_feature(w, "bq", BQ0 - AB0, 2, h)
                twice = lambda w, c0: [((slice(i * 64, i * 64 + 64), half(0)), lambda k: w[:, k, c0:c0 + 64], h)
                                       for i in range(2)]
                tiles(ph3, "bk", twice(w, BK0 - AB0), KT)
                tiles(ph3, "bv", [(slice(t * SAD, (t + 1) * SAD), *by_tok(w, BV0 - AB0, SAD, t)) for t in range(TT)], KT)
                last_unit3[where3[("b", 0)]] = "bv"
                w = slab3("bi", n=CQ0 - BQI0)
                by_feature(w, "qi", 0, 2, h)
                tiles(ph3, "ki", twice(w, BKI0 - BQI0), KT)
                tiles(ph3, "wi", [(slice(t * 4, t * 4 + 4), *by_tok(w, BWI0 - BQI0, 4, t)) for t in range(TT)], KT)
                last_unit3[where3[("bi", 0)]] = "wi"
                for key in (("qi", 0), "ki"):
                    ph3.freed(pe, key)
                at = lambda t: slice(t * P, (t + 1) * P)

                def pairs_by_rows(key, lhs, rhs, t):
                    for par in range(2):
                        r_ = slice(64 * par, 64 * par + 64)
                        tiles(ph3, (key, t, par), [(half(i), lambda k, i=i: lhs[r_, i, at(t)], lambda k: rhs[r_, :])
                                                   for i in range(2)], 1)

                for t in range(TT):
                    pairs_by_rows("is", qi, kii, t)
                for name in ("aq", "ak", "av"):
                    by_feature(slab3(name), name, 0, 4, h)
                    last_unit3[where3[(name, 0)]] = (name, 1)
                pe.wait_ge(S("qk_squares"), 1)
                for g in range(4):
                    tiles(ph3, ("l2", g), [(half(i), lambda k: C("ones"), lambda k, f=2 * g + i: sc3[:, f, :])
                                           for i in range(2)], 1)
                w = slab3("cqf")
                by_feature(w, "cq", 0, 2, h)
                by_feature(w, "cf", 256, 2, h)
                last_unit3[where3[("cqf", 0)]] = ("cf", 0)
                pe.wait_ge(S("g_ready"), 1)
                b = ph3.bank(pe, "G")
                for i, m in enumerate(("incl", "blk")):
                    for t in range(TT):
                        o = (2 * i + t) * 4
                        last = mm(PS[:, b, o:o + 4], C(m), gt[:, t, :], start=True, stop=True)
                last.then_inc(psum_full, 1)
                pe.wait_ge(S("gx_ready"), 2)
                for name, src, m in (("Gb", gx, "incl"), ("bb", bx, "ident")):
                    for g in range(2):
                        tiles(ph3, (name, g), [(slice((2 * i + t) * P, (2 * i + t + 1) * P),
                                                lambda k, i=i, t=t: src[:, 2 * g + i, t, :], lambda k: C(m))
                                               for i in range(2) for t in range(TT)], 1)
                for key in (("bq", 0), "bk"):
                    ph3.freed(pe, key)
                for t in range(TT):
                    pairs_by_rows("lg", qb, kbb, t)
                pe.wait_ge(S("qk_normed"), 2)
                qn, kn, vn = cs[:, 0:4, :], cs[:, 4:8, :], cs[:, 8:12, :]
                at = lambda t: slice(t * P, (t + 1) * P)
                quads = lambda f: [(slice((2 * i + t) * P, (2 * i + t + 1) * P), *f(i, t)) for i in range(2) for t in range(TT)]
                for name, r_ in (("kk", kn), ("qk", qn)):
                    for g in range(2):
                        tiles(ph3, (name, g), quads(lambda i, t: (lambda k: kn[:, 2 * g + i, at(t)],
                                                                  lambda k: r_[:, 2 * g + i, at(t)])), 1)
                for t in range(TT):
                    turn(("kt", t), [kn[:, h_, at(t)] for h_ in range(DNH)])
                for t in range(TT):
                    turn(("vt", t), [vn[:, h_, at(t)] for h_ in range(DNH)])
                for g in range(2):
                    pe.wait_ge(S("B_ready"), g + 1)
                    turn(("Z", 0, g), [BT[0][:, 2 * g + i, t, :] for i in range(2) for t in range(TT)])
                w = slab3("cig")
                tiles(ph3, "ci", [(slice(t * HG, (t + 1) * HG), *by_tok(w, 0, HG, t)) for t in range(TT)], KT)
                for lv in range(1, 6):
                    for g in range(2):
                        pe.wait_ge(S("B_ready"), 2 * lv + g + 1)
                        if lv == 1:
                            ph3.freed(pe, ("Z", 0, g))
                        else:
                            ph3.freed(pe, ("XZ", lv - 1, g))
                        tiles(ph3, ("Z", lv, g), quads(lambda i, t: (lambda k: BT[lv % 2][:, 2 * g + i, t, :],
                                                                     lambda k: XI[:, 2 * g + i, t, :])), 1)
                    for g in range(2):
                        ph3.freed(pe, ("Z", lv, g))
                        if lv == 1:
                            pe.wait_ge(S("X0T_ready"), g + 1)
                        else:
                            ph3.freed(pe, ("ZX", lv - 1, g))
                        if lv < 5:
                            tiles(ph3, ("XZ", lv, g), quads(lambda i, t: (lambda k: XIT[:, 2 * g + i, t, :],
                                                                          lambda k: Z[:, 2 * g + i, t, :])), 1)
                        tiles(ph3, ("ZX", lv, g), quads(lambda i, t: (lambda k: Z[:, 2 * g + i, t, :],
                                                                      lambda k: XIT[:, 2 * g + i, t, :])), 1)
                    if lv == 2:
                        pe.wait_ge(S("p_ready"), TT)
                        for i in range(SAH):
                            turn(("pt", i), [pr[:, t, i, at(s_)] for s_ in range(TT) for t in range(TT)])
                    if lv == 3:
                        for i in range(SAH):
                            ph3.freed(pe, ("pt", i))
                        ph3.freed(pe, "bv")
                        b = ph3.bank(pe, "ob")
                        for par in range(2):
                            for i in range(2):
                                for s_ in range(TT):
                                    last = mm(PS[64 * par:64 * par + 64, b, half(i)], vtk[:, s_, :],
                                              pT[:, 2 * i + par, s_, :], start=(s_ == 0), stop=(s_ == TT - 1))
                        last.then_inc(psum_full, 1)
                for g in range(2):
                    ph3.freed(pe, ("ZX", 5, g))
                pe.wait_ge(S("kvb_ready"), 6)
                for t in range(TT):
                    tiles(ph3, ("u0", t), [(slice(i * P, (i + 1) * P), lambda k, i=i: XIT[:, i, t, :],
                                            lambda k, i=i: vb[:, t, i, :]) for i in range(DNH)], 1)
                for g in range(2):
                    tiles(ph3, ("wk", g), quads(lambda i, t: (lambda k: kb[:, t, 2 * g + i, :],
                                                              lambda k: XIT[:, 2 * g + i, t, :])), 1)
                for t in range(TT):
                    ph3.freed(pe, ("u0", t))
                for g in range(2):
                    ph3.freed(pe, ("wk", g))
                pe.wait_ge(S("qdec_ready"), 1)
                fill = ((slab3("cig"), ("cg", 0), 256), (slab3("az"), ("az", 0), 0), (slab3("az"), ("az", 1), 256))

                def filler(n):
                    w, key, c0 = fill[n]
                    tiles(ph3, key, [(half(i), lambda k, f=i: w[:, k, c0 + f * P:c0 + (f + 1) * P], h)
                                     for i in range(2)], KT)

                last_unit3[where3[("cig", 0)]] = ("cg", 0)
                last_unit3[where3[("az", 0)]] = ("az", 1)

                for n in range(NCH):
                    t, r_ = n // 2, slice(CH * (n % 2), CH * (n % 2) + CH)
                    if n:
                        ph3.freed(pe, ("dS", n - 1))
                        tiles(ph3, ("wS", n), [((r_, slice(i * P, (i + 1) * P)),
                                                lambda k, i=i: wk[:, i, n * CH:(n + 1) * CH],
                                                lambda k, i=i: Sd[n - 1][:, i, :]) for i in range(DNH)], 1)
                        ph3.freed(pe, ("wS", n))
                    if n < NCH - 1:
                        tiles(ph3, ("dS", n), [(slice(i * P, (i + 1) * P), lambda k, i=i: kd[r_, t, i, :],
                                                lambda k, i=i: u[r_, t, i, :]) for i in range(DNH)], 1)
                    if n == 0:
                        filler(0)
                        pe.wait_ge(S("qk_levels"), 2)
                    else:
                        lv = n - 1
                        for par in range(2):
                            r_ = slice(64 * par, 64 * par + 64)
                            tiles(ph3, ("hs", lv, par), [
                                (slice((2 * i + t) * P, (2 * i + t + 1) * P),
                                 lambda k, i=i, t=t: args[r_, lv, 1, i * T + t * P:i * T + (t + 1) * P],
                                 lambda k, i=i, t=t: args[r_, lv, 0, i * T + t * P:i * T + (t + 1) * P])
                                for i in range(2) for t in range(TT)], 1)
                        if n == 1:
                            filler(1)
                            pe.wait_ge(S("kdec_ready"), 1)
                            turn("hkt", [eR[:, i, at(t)] for t in range(TT) for i in range(2)])
                        elif n == 2:
                            filler(2)
                ph3.freed(pe, "hkt")
                ph3.freed(pe, "ci")
                for par, ns in ((0, (0, 2)), (1, (1,))):
                    tiles(ph3, ("hS", par), [
                        (slice((2 * j + i) * P, (2 * j + i + 1) * P),
                         lambda k, n=n, i=i: kdt[64 * par:64 * par + 64, n // 2, i * P:(i + 1) * P],
                         lambda k, n=n, i=i: cit[64 * par:64 * par + 64, n // 2, i * P:(i + 1) * P])
                        for j, n in enumerate(ns) for i in range(2)], 1)
                for g in range(2):
                    ph3.freed(pe, ("qk", g))
                for g in range(2):
                    b = ph3.bank(pe, ("oa", g))
                    first = True
                    for i in range(2):
                        f = 2 * g + i
                        for t in range(TT):
                            mm(PS[:, b, i * T + t * P:i * T + (t + 1) * P], u[:, t, f, :], QK[:, f, t, :], start=first,
                               stop=False, skip_group_check=True)
                            first = False
                        for n in range(1, NCH):
                            o = i * T + n * CH
                            last = mm(PS[:, b, o:o + CH], Sd[n - 1][:, f, :], eG[:, f, n * CH:(n + 1) * CH], start=False,
                                      stop=(i == 1 and n == NCH - 1), skip_group_check=True)
                    last.then_inc(psum_full, 1)
                pe.wait_ge(S("oa_squares"), 1)
                for g in range(2):
                    tiles(ph3, ("oam", g), [(half(i), lambda k: C("ones"), lambda k, f=2 * g + i: sc3[:, f, :])
                                            for i in range(2)], 1)
                pe.wait_ge(S("Sh_ready"), 1)
                pe.wait_ge(S("qdec2_ready"), 1)
                b = ph3.bank(pe, "oc")
                for i in range(2):
                    for n in range(1, NCH):
                        o = i * T + n * CH
                        mm(PS[:, b, o:o + CH], Sh[:, n - 1, i, :], eB[:, i, n * CH:(n + 1) * CH],
                           start=(i == 0 and n == 1), stop=False, skip_group_check=True)
                pe.wait_ge(S("AT_ready"), 2)
                for par in range(2):
                    for i in range(2):
                        for t in range(TT):
                            last = mm(PS[64 * par:64 * par + 64, b, i * T + t * P:i * T + (t + 1) * P],
                                      cit[:, t, (2 * i + par) * 64:(2 * i + par + 1) * 64], AT[:, par, i, t, :],
                                      start=False, stop=(par == 1 and i == 1 and t == TT - 1), skip_group_check=True)
                last.then_inc(psum_full, 1)
                pe.wait_ge(S("oc_squares"), 1)
                tiles(ph3, "ocm", [(half(i), lambda k: C("blk"), lambda k, i=i: sc3[:, 6 + i, :]) for i in range(2)], 1)
                ph3.freed(pe, "ob")
                pe.wait_ge(S("oa_ready"), 1)
                waited = []

                def mixers(k):
                    if k == 6 and not waited:
                        pe.wait_ge(S("oc_ready"), 1)
                        waited.append(k)
                    return cat[:, k, :]

                for j in range(2):
                    by_feature(slab3("out", j), ("out", j), 0, 4, mixers)
                    last_unit3[where3[("out", j)]] = (("out", j), 1)
                square_sums("ms1", fsq, {2 * g: stage("sq_f", g + 1) for g in range(4)})
                square_sums("ms2", sc3, {0: stage("sq_x2"), 4: stage("sq_x2", 2)})
                second = when_ready(lambda k: (("h_ready3", KT + k + 1),), h)
                for j in range(FFT // 2):
                    w = slab3("up", j)
                    w2 = ring[:, where3[("up", j)] % 3, :].rearrange("p (v k n) -> p v k n", v=2, k=KT)
                    for v in range(2):
                        tiles(ph3, ("up", j, v), [(half(i), lambda k, i=i: w2[:, v, k, i * P:(i + 1) * P], second)
                                                  for i in range(2)], KT)
                    last_unit3[where3[("up", j)]] = ("up", j, 1)
                banks = [ph3.bank(pe, ("down", g)) for g in range(4)]
                for j in range(0, FFT, 4):
                    kk_ = min(4, FFT - j)
                    w = slab3("down", j // 4, kk_, D)
                    pe.wait_ge(S("gated"), min(j + 4, FFT) // 2)
                    for f in range(KT):
                        for k in range(kk_):
                            last = mm(PS[:, banks[f // 2], half(f % 2)], w[:, k, f * P:(f + 1) * P], gated[:, j + k, :],
                                      start=(f % 2 == 0 and j + k == 0), stop=(f % 2 == 1 and j + k == FFT - 1),
                                      skip_group_check=True)
                            if j + k == FFT - 1 and f % 2 == 1:
                                last.then_inc(psum_full, 1)
                    if j + 4 < FFT:
                        last.then_inc(S("down_read"), 1)
                square_sums("ms3", fsq, {2 * g: stage("sq_f", g + 5) for g in range(4)})
                meet(pe, "pe")
            for t in range(TT):
                for g in range(2):
                    for k in range(4):
                        last = nc.tensor.transpose(PS[:, 2 * t + g, k * P:(k + 1) * P],
                                                   xT[:, 4 * g + k, t * P:(t + 1) * P], C("ident"))
                    last.then_inc(S("out_turned"), 1)

        @block.sync
        def _(sp):
            sp.dma_start(cst[:, :], W["consts"]).then_inc(consts_in, 16)
            for dst, src in PARAMS[0:N_FIRST]:
                sp.dma_start(dst, src).then_inc(first_in, 16)
            for s, name in enumerate(("ctx", "x")):
                sp.dma_start(xraw[:, s, :, :], W[name][0].rearrange("(t p) d -> p t d", p=P)).then_inc(x_in, 16)

            def mod_slab(j):
                sp.dma_start(mslots[MSLOT[j]], cols(wmod, 512 * j)).then_inc(wm[MSLOT[j]], 16)

            for i, (name, j, src) in enumerate(SL1):
                if i == 3:
                    mod_slab(3)
                elif i == 6:
                    ph1.read(sp, ("xT", 3))
                    mod_slab(4)
                    for m in range(5, 12):
                        sp.wait_ge(S("mod_sum"), msum_at[m - 2])
                        mod_slab(m)
                if i >= 3:
                    if SL1[i - 3][0:2] == ("mod", 2):
                        sp.wait_ge(S("mod_sum"), msum_at[2])
                    else:
                        ph1.read(sp, last_unit1[i - 3])
                sp.dma_start(slot(i, src.shape[1]), src).then_inc(wl[i % 3], 16)
            sp.wait_ge(S("og_ready"), 1)
            ph1.read(sp, ("yp", 1))
            sp.dma_start(rw[:, :, 0:N_GRP], W["router_grp_w"][0].rearrange("(k p) n -> p k n", p=P)).then_inc(router_in, 16)
            sp.dma_start(rw[:, :, N_GRP:], W["router_exp_w"][0].rearrange("(k p) n -> p k n", p=P)).then_inc(router_in, 16)
            sp.dma_start(rb[0:1, 0:N_GRP], W["router_grp_b"]).then_inc(router_in, 16)
            sp.dma_start(rb[0:1, N_GRP:], W["router_exp_b"]).then_inc(router_in, 16)

            def expert_weights(e):
                for name, s, o, k in (("moe_w1", 0, 0, KT), ("moe_w1", 1, 1, KT), ("moe_w3", 2, 0, KT),
                                      ("moe_w3", 3, 1, KT), ("moe_w2", 4, 0, 4), ("moe_w2", 5, 1, 4)):
                    yield s, W[name][0][bass.ds(e + o, 1)].rearrange("a (k p) n -> p (a k) n", p=P), k

            def fetch(s, src, k):
                sp.dma_start(ring[:, s, :].rearrange("p (k n) -> p k n", k=k), src).then_inc(ml[s], 16)

            first = {s: (src, k) for s, src, k in expert_weights(0)}
            fetch(4, *first[4])
            fetch(5, *first[5])
            ph1.read(sp, ("gbr", 1, 1))
            fetch(3, *first[3])
            for i in range(len(SL1) - 3, len(SL1)):
                ph1.read(sp, last_unit1[i])
                fetch(i % 3, *first[i % 3])
            meet(sp, "sp")
            sp.wait_ge(S("rounds_ready"), 1)
            visits = sp.snap(sp.value_load(rounds_i[0:1, 0:1]) * PAIRS)
            with sp.Fori(1, visits) as v:
                reads = (w1_read, w1_read, w3_read, w3_read, y_full, y_full)
                for (s, src, k), q in zip(expert_weights((v % PAIRS) * 2), reads):
                    sp.wait_ge(q, v)
                    fetch(s, src, k)
            meet(sp, "sp")
            with sp.Fori(0, LAYERS) as L:
                for i, (name, j, parts) in enumerate(SL3):
                    if i >= 3:
                        before = i - 3
                        if before in last_unit3:
                            ph3.read(sp, last_unit3[before])
                        else:
                            sp.wait_ge(S("down_read"), SL3[before][1] + 1)
                    for q, (wn, r0, r1, c0, c1, o) in enumerate(parts):
                        k, n = (r1 - r0) // P, c1 - c0
                        base = q * k * n if len(parts) > 1 else 0
                        sp.dma_start(ring[:, i % 3, base:base + k * n].rearrange("p (k n) -> p k n", k=k),
                                     lw(wn, L, r0, r1, c0, c1)).then_inc(ll[i % 3], 16)
                meet(sp, "sp")
            sp.wait_ge(S("out_copied"), 4)
            sp.dma_start(out_T.rearrange("(t p) d -> p t d", p=P), outt).then_inc(out_done, 16)
            sp.wait_ge(out_done, 16)

        @block.scalar
        def _(act):
            A = nc.scalar.activation
            link = Chain(act, "act_step")

            def rsqrt_mean(view, n, src, b=None, after=None):
                ins = A(view, src, ACT.Ln, scale=1.0 / n, bias=C("eps")[0:view.shape[0], :])
                ins.then_inc(psum_free[b], 1)
                after(act)
                return A(view, view, ACT.Exp, scale=-0.5)

            for kp in range(4):
                b = ph1.read(act, ("ctxT", kp))
                A(hboth[:, 2 * kp:2 * kp + 2, 0:T], PS[:, b, :].rearrange("p (k t) -> p k t", k=2),
                  ACT.Copy).then_inc(psum_free[b], 1)
            ph1.freed(act, "colsA")
            A(csil, colsA[:, 0:16].rearrange("p (v k) -> p k v", v=2), ACT.Silu).then_inc(S("silu_c"), 1)
            ph1.freed(act, ("ctxT", 3))
            A(sqb[:, :, 0:T], hboth[:, :, 0:T], ACT.Square).then_inc(S("squares"), 1)
            b = ph1.read(act, "ms")
            rsqrt_mean(rstd, D, PS[:, b, :], b, lambda e: ph1.freed(e, "ms")).then_inc(S("rstd_ready"), 1)
            act.wait_ge(S("ada_ready"), 1)
            act.wait_ge(S("normed"), 2)
            for k in range(KT):
                A(hboth[:, k, 0:T], hboth[:, k, 0:T], ACT.Identity, bias=mod(0, 1, k),
                  scale=ada[:, 1, k:k + 1]).then_inc(S("h1_context"), 1)
            for j in range(2):
                for t in range(4):
                    b = ph1.read(act, ("v", j, t))
                    A(vtok[:, t, j * 512:(j + 1) * 512], PS[:, b, :], ACT.Copy).then_inc(psum_free[b], 1)
            act.wait_ge(S("cols_ready"), 1)
            A(lbc[:, 1, 0:2], lbc[:, 1, 0:2], ACT.Sigmoid).then_inc(S("lb_ready"), 1)
            b = ph1.read(act, "lr")
            A(lrT[0:32, :], PS[0:32, b, :], ACT.Copy).then_inc(psum_free[b], 1)
            for d in range(2):
                for h in range(GH):
                    act.wait_ge(S("absz"), d * GH + h + 1)
                    ins = A(cum[:, d, h, :], cum[:, d, h, :], ACT.Exp)
            link(ins)
            for d in range(2):
                for h in range(GH):
                    A(cum[:, d, h, :], cum[:, d, h, :], ACT.Ln, bias=C("one")).then_inc(S("lnz"), 1)
            for g in range(2):
                b = ph1.read(act, ("q", 0, g))
                A(qT[:, 2 * g:2 * g + 2, :], PS[:, b, :].rearrange("p (h t) -> p h t", h=2), ACT.Copy,
                  scale=float((GDK // GH) ** -0.5)).then_inc(psum_free[b], 1)
            for j in range(2):
                for g in range(2):
                    b = ph1.read(act, ("g", j, g))
                    A(sg[:, 4 * j + 2 * g:4 * j + 2 * g + 2, :], PS[:, b, :].rearrange("p (h t) -> p h t", h=2),
                      ACT.Silu).then_inc(psum_free[b], 1)
            inv = 1.0 / GATE_NORM
            for d, e in ((0, e1), (1, e2)):
                act.wait_ge(S("krc_arg"), d + 1)
                A(e, e, ACT.Exp, scale=inv).then_inc(S("krc_exp"), 1)
            for g in range(2):
                b = ph1.read(act, ("u", 0, g))
                A(hboth[:, 2 * g:2 * g + 2, 0:T], PS[:, b, :].rearrange("p (h t) -> p h t", h=2),
                  ACT.Copy).then_inc(psum_free[b], 1)
            act.wait_ge(S("decays"), 1)
            A(dec, lastx, ACT.Exp, scale=inv).then_inc(S("dec_ready"), 1)
            for d in range(2):
                if d:
                    act.wait_ge(S("cumb_ready"), 1)
                A(qd[:, d], cum[:, d, :, T:2 * T], ACT.Exp, scale=inv).then_inc(S("qdki_exp"), 1)
                A(ki[:, d], cum[:, d, :, T:2 * T], ACT.Exp, scale=-inv).then_inc(S("qdki_exp"), 1)
            for d, e in ((0, e1), (1, e2)):
                act.wait_ge(S("krx_arg" if d == 0 else "cumb_ready"), 1)
                A(e, e, ACT.Exp, scale=inv).then_inc(S("krx_exp"), 1)
            for d in range(2):
                for hp in range(2):
                    b = ph1.read(act, ("s0", d, hp))
                    A(s0[:, d, 2 * hp:2 * hp + 2, :], PS[:, b, :].rearrange("p (h v) -> p h v", h=2),
                      ACT.Copy).then_inc(psum_free[b], 1)
            def gate_sigmoid(j, g):
                b = ph1.read(act, ("gate", j, g))
                A(gates(4 * j + 2 * g), PS[:, b, :].rearrange("p (h t) -> p h t", h=2),
                  ACT.Sigmoid).then_inc(psum_free[b], 1)

            for h in range(GH):
                gate_sigmoid(h // 2, h % 2)
                b = ph1.read(act, ("o", h))
                A(oT[:, 2 * h:2 * h + 2, :], PS[:, b, :].rearrange("p (j t) -> p j t", j=2),
                  ACT.Copy).then_inc(psum_free[b], 1)
            ph1.freed(act, ("o", GH - 1))
            A(osq, oT, ACT.Square).then_inc(S("osq_ready"), 1)
            for g in range(2):
                gate_sigmoid(2, g)
            orstd = e1.rearrange("p h t -> p (h t)")
            for hp in range(2):
                b = ph1.read(act, ("oms", hp))
                A(orstd[:, hp * 512:(hp + 1) * 512], PS[:, b, :], ACT.Ln, scale=1.0 / 256, bias=C("eps"))\
                    .then_inc(psum_free[b], 1)
            for hp in range(2):
                ph1.freed(act, ("oms", hp))
            A(orstd, orstd, ACT.Exp, scale=-0.5).then_inc(S("orstd_ready"), 1)
            for g in range(2):
                gate_sigmoid(3, g)
            for g in range(4):
                act.wait_ge(S("x1_new"), g + 1)
                A(h2n[:, 2 * g:2 * g + 2, :], xT[:, 2 * g:2 * g + 2, :], ACT.Square).then_inc(S("sq2"), 1)
            b = ph1.read(act, "ms2")
            rsqrt_mean(rstd2, D, PS[:, b, 0:T], b, lambda e: ph1.freed(e, "ms2")).then_inc(S("rstd2_ready"), 1)
            for k in range(KT):
                act.wait_ge(S("normed2"), k + 1)
                A(h2T[:, k, :], h2n[:, k, :], ACT.Identity, bias=mod(3, 0, k)).then_inc(S("h2_ready"), 1)
            meet(act, "act")

            act.wait_ge(S("route_arg"), 1)
            A(m8[1], m8[0], ACT.Exp).then_inc(S("route_exp"), 1)
            for t in range(TT):
                for g in range(2):
                    b = ph2.read(act, ("h2t", t, g))
                    A(h2t[:, t, g * 512:(g + 1) * 512], PS[:, b, :], ACT.Copy).then_inc(psum_free[b], 1)
            act.wait_ge(S("route_arg"), 2)
            A(m1[3], m1[2], ACT.Exp).then_inc(S("route_exp"), 1)
            act.wait_ge(S("rounds_ready"), 1)
            rounds = act.value_load(rounds_i[0:1, 0:1])
            with act.Fori(0, rounds) as r:
                with act.Fori(0, PAIRS) as p:
                    i1 = act.snap(r * PAIRS + p + 1)
                    act.wait_ge(S("gathered"), i1 + 1)
                    A(hg[:, 0:4, :], PS[:, 4, :].rearrange("p (k s) -> p k s", k=4), ACT.Copy).then_inc(S("hg_lo"), 1)
                    act.wait_ge(w1_read, i1)
                    A(s1, PS[:, 4, :], ACT.Silu).then_inc(S("s1_ready"), 1)
                    act.wait_ge(S("hid_turned"), i1)
                    A(hid.rearrange("p f s -> p (f s)"), PS[:, 4, :], ACT.Copy).then_inc(S("hid_ready"), 1)
                    act.wait_ge(y_full, i1)
                    A(ytok[:, 0:512], PS[:, 6, :], ACT.Copy).then_inc(S("y_lo"), 1)
            act.drain().then_inc(S("evacuated"), 1)
            link = Chain(act, "act_step")
            for i in range(2):
                act.wait_ge(S("x2_new"), i + 1)
                A(h2n[:, 4 * i:4 * i + 4, :], xT[:, 4 * i:4 * i + 4, :], ACT.Square).then_inc(S("sq3"), 1)
            act.wait_ge(S("ms3"), 1)
            link(A(rstd2, PS[:, 4, 0:T], ACT.Ln, scale=1.0 / D, bias=C("eps")))
            A(rstd2, rstd2, ACT.Exp, scale=-0.5).then_inc(S("rstd3_ready"), 1)
            for i in range(2):
                act.wait_ge(S("x3_new"), i + 1)
                A(sc3[:, 4 * i:4 * i + 4, :], xT[:, 4 * i:4 * i + 4, :], ACT.Square)
            meet(act, "act")

            v2 = lambda v: v.rearrange("p (j t) -> p j t", j=2)
            with act.Fori(0, LAYERS) as L:
                link = Chain(act, "act_step")

                def rs3(view, n, key, width=T):
                    b = ph3.read(act, key)
                    return rsqrt_mean(view, n, PS[:, b, 0:width], b, lambda e: ph3.freed(e, key))

                def rs3_all(view, parts):
                    for i, (n, key) in enumerate(parts):
                        b = ph3.read(act, key)
                        A(view[:, i * 512:(i + 1) * 512], PS[:, b, :], ACT.Ln, scale=1.0 / n, bias=C("eps"))\
                            .then_inc(psum_free[b], 1)
                    for n, key in parts:
                        ph3.freed(act, key)
                    return A(view, view, ACT.Exp, scale=-0.5)

                def evac(key, dst, fn=ACT.Copy, **kw):
                    b = ph3.read(act, key)
                    A(dst, v2(PS[:, b, :]), fn, **kw).then_inc(psum_free[b], 1)

                rs3(rs, D, "ms0").then_inc(S("rs_ready"), 1)
                b = ph3.read(act, "ab")
                A(ab, PS[:, b, 0:16].rearrange("p (t n) -> p t n", t=TT), ACT.Copy).then_inc(psum_free[b], 1)
                ph3.freed(act, "ab")
                A(beta, ab[:, :, 0:4], ACT.Sigmoid).then_inc(S("beta_ready"), 1)
                act.wait_ge(S("zt_ready"), 1)
                A(col[:, LCOLS:LCOLS + 4], col[:, LCOLS:LCOLS + 4], ACT.Exp).then_inc(S("alog_exp"), 1)
                link(A(eRc, eRc, ACT.Exp))
                A(eRc, eRc, ACT.Ln, bias=C("one")).then_inc(S("softplus"), 1)
                evac(("bq", 0), qb)
                b = ph3.read(act, "bk")
                A(kbb, PS[:, b, 0:T], ACT.Copy).then_inc(psum_free[b], 1)
                b = ph3.read(act, "bv")
                A(vtk, PS[:, b, 0:TT * SAD].rearrange("p (t n) -> p t n", t=TT), ACT.Copy).then_inc(psum_free[b], 1)
                evac(("qi", 0), qi)
                b = ph3.read(act, "ki")
                A(kii, PS[:, b, 0:T], ACT.Copy).then_inc(psum_free[b], 1)
                b = ph3.read(act, "wi")
                A(wi, PS[:, b, 0:8].rearrange("p (t n) -> p t n", t=TT), ACT.Copy, scale=float(4 ** -0.5 * 64 ** -0.5))\
                    .then_inc(psum_free[b], 1)
                for t in range(TT):
                    for par in range(2):
                        if t:
                            act.wait_ge(S("relu_used"), par + 1)
                        evac(("is", t, par), relu[:, par], ACT.Relu)
                act.wait_ge(S("conv_ready"), 1)
                link(A(cs[:, 0:8, :], cs[:, 0:8, :], ACT.Silu))
                A(sc3[:, :, :], cs[:, 0:8, :], ACT.Square).then_inc(S("qk_squares"), 1)
                act.wait_ge(S("conv_ready"), 2)
                A(cs[:, 8:12, :], cs[:, 8:12, :], ACT.Silu).then_inc(S("v_silu"), 1)
                rs3_all(rsb, [(1.0, ("l2", g)) for g in range(4)]).then_inc(S("l2_ready"), 1)
                evac(("cq", 0), cq, ACT.Silu)
                evac(("cf", 0), cf, ACT.Sigmoid)
                act.wait_ge(S("Gc_ready"), 1)
                A(eGc, Gc, ACT.Exp).then_inc(S("eGc_ready"), 1)
                A(eRc, eRc, ACT.Exp).then_inc(S("eGc_ready"), 1)
                act.wait_ge(S("DT_arg"), 2)
                A(DT, DT, ACT.Exp).then_inc(S("DT_exp"), 1)
                for g in range(2):
                    b = ph3.read(act, ("Gb", g))
                    A(eG[:, 2 * g:2 * g + 2, :], v2(PS[:, b, :]), ACT.Exp).then_inc(psum_free[b], 1)
                act.wait_ge(S("fg_ready"), 1)
                A(cf, cf, ACT.Ln).then_inc(S("lf_ready"), 1)
                for t in range(TT):
                    act.wait_ge(S("p_arg"), t + 1)
                    A(pr[:, t], pr[:, t], ACT.Exp, scale=SAD ** -0.5).then_inc(S("p_exp"), 1)
                b = ph3.read(act, "ci")
                A(cit, PS[:, b, :].rearrange("p (t n) -> p t n", t=TT), ACT.Copy).then_inc(psum_free[b], 1)
                z4 = lambda v, g: v[:, 2 * g:2 * g + 2].rearrange("p h t c -> p (h t c)")
                for lv in range(1, 6):
                    for g in range(2):
                        b = ph3.read(act, ("Z", lv, g))
                        A(z4(Z, g), PS[:, b, :], ACT.Copy).then_inc(psum_free[b], 1)
                    if lv == 3:
                        for i in range(SAH):
                            b = ph3.read(act, ("pt", i))
                            A(pT[:, i], v2(PS[:, b, :]), ACT.Copy).then_inc(psum_free[b], 1)
                    if lv == 4:
                        evac("ob", cat[:, 4:6, :])
                for t in range(TT):
                    b = ph3.read(act, ("u0", t))
                    A(u[:, t].rearrange("p h c -> p (h c)"), PS[:, b, :], ACT.Copy).then_inc(psum_free[b], 1)
                for g in range(2):
                    evac(("wk", g), wk[:, 2 * g:2 * g + 2, :])
                act.wait_ge(S("hg_args"), 1)
                A(args, args, ACT.Exp).then_inc(S("hg_exp"), 1)
                A(eB, Bc, ACT.Exp).then_inc(S("hg_exp"), 1)
                A(eR, eR, ACT.Exp).then_inc(S("hg_exp"), 1)
                evac(("cg", 0), cg, ACT.Silu)
                evac(("az", 0), sz[:, 0:2, :], ACT.Silu)
                b = ph3.read(act, "hkt")
                A(kdt, PS[:, b, :].rearrange("p (t n) -> p t n", t=TT), ACT.Copy).then_inc(psum_free[b], 1)
                evac(("az", 1), sz[:, 2:4, :], ACT.Silu)
                for g in range(2):
                    evac(("oa", g), cat[:, 2 * g:2 * g + 2, :])
                ph3.freed(act, ("oa", 1))
                A(sc3[:, 0:4, :], cat[:, 0:4, :], ACT.Square).then_inc(S("oa_squares"), 1)
                rs3_all(fT[:, 0:4, :].rearrange("p k t -> p (k t)"), [(P, ("oam", g)) for g in range(2)])\
                    .then_inc(S("oam_ready"), 1)
                evac("oc", cat[:, 6:8, :])
                ph3.freed(act, "oc")
                A(sc3[:, 6:8, :], cat[:, 6:8, :], ACT.Square).then_inc(S("oc_squares"), 1)
                rs3(fT[:, 4:6, :].rearrange("p k t -> p (k t)"), 64, "ocm", 512).then_inc(S("oam_ready"), 1)

                def squares(key):
                    for g in range(4):
                        b = ph3.read(act, key(g))
                        A(fsq[:, 2 * g:2 * g + 2, :], v2(PS[:, b, :]), ACT.Square).then_inc(S("sq_f"), 1)

                squares(lambda g: (("out", g // 2), g % 2))
                rs3(rs, D, "ms1").then_inc(S("rs_ready"), 1)

                def squares_of_x(n):
                    for i in range(2):
                        act.wait_ge(S("x_new"), n + i + 1)
                        A(sc3[:, 4 * i:4 * i + 4, :], xT[:, 4 * i:4 * i + 4, :], ACT.Square).then_inc(S("sq_x2"), 1)

                squares_of_x(0)
                rs3(rs, D, "ms2").then_inc(S("rs_ready"), 1)
                for j in range(FFT // 2):
                    ph3.freed(act, ("up", j, 0))
                    A(gcv[:, j % 2, 0:2, :], gcv[:, j % 2, 0:2, :], ACT.Gelu_apprx_tanh).then_inc(S("gelu_ready"), 1)
                squares(lambda g: ("down", g))
                rs3(rs, D, "ms3").then_inc(S("rs_ready"), 1)
                squares_of_x(2)
                meet(act, "act")

        @block.vector
        def _(dve):
            V = nc.vector
            link = Chain(dve, "vec_step")
            V.memset(a2[0:32, :, :], 0.0).then_inc(S("a2_zero"), 1)
            for kp in range(4):
                b = ph1.read(dve, ("xT", kp))
                V.tensor_copy(xT[:, 2 * kp:2 * kp + 2, :], PS[:, b, :].rearrange("p (k t) -> p k t", k=2))\
                    .then_inc(psum_free[b], 1)
            b = ph1.read(dve, "colsA")
            V.tensor_copy(colsA[:, :], PS[:, b, 0:NA]).then_inc(psum_free[b], 1)
            ph1.freed(dve, "colsA")
            ph1.freed(dve, ("xT", 3))
            V.tensor_tensor(sqb[:, :, T:2 * T], xT[:, :, :], xT[:, :, :], ALU.mult).then_inc(S("squares"), 1)

            def mod_sum(j, vectors=1):
                if j == 2:
                    i = where1[("mod", 2)]
                    dve.wait_ge(wl[i % 3], 16 * (i // 3 + 1))
                    w = slot(i)
                else:
                    dve.wait_ge(wm[MSLOT[j]], mloads[j])
                    w = mslots[MSLOT[j]]
                for k in range(KT):
                    for v in range(vectors):
                        dst = msums[(j, v)]
                        if k == 0:
                            ins = V.tensor_scalar(dst, w[:, k, :], csil[:, k, v:v + 1], None, ALU.mult)
                        else:
                            ins = V.scalar_tensor_tensor(dst, w[:, k, :], csil[:, k, v:v + 1], dst, ALU.mult, ALU.add)
                        if k == KT - 1:
                            ins.then_inc(S("mod_sum"), 1)
                    if k < KT - 1:
                        link(ins)

            dve.wait_ge(S("silu_c"), 1)
            mod_sum(2, 2)
            dve.wait_ge(S("rstd_ready"), 1)
            V.tensor_tensor(hboth[:, :, T:2 * T], xT[:, :, :],
                            rstd[:, T:2 * T].unsqueeze(1).broadcast_to([P, KT, T]), ALU.mult).then_inc(S("normed"), 1)
            V.tensor_tensor(hboth[:, :, 0:T], hboth[:, :, 0:T],
                            rstd[:, 0:T].unsqueeze(1).broadcast_to([P, KT, T]), ALU.mult).then_inc(S("normed"), 1)
            mod_sum(3, 2)
            bm = row_at(ROWS_A, "b_mod")

            def modulate(j):
                b = ph1.read(dve, ("mod", j))
                n = 2 if j < 4 else 1
                V.tensor_tensor(mods[:, 4 * j:4 * j + 4, 0:n], PS[:, b, 0:8].rearrange("p (j v) -> p j v", v=2)[:, :, 0:n],
                                colsA[:, bm + 4 * j:bm + 4 * j + 4].unsqueeze(2).broadcast_to([P, 4, n]),
                                ALU.add).then_inc(psum_free[b], 1)

            for j in range(4):
                modulate(j)
            ph1.freed(dve, ("mod", 3))
            for v in range(2):
                ins = V.scalar_tensor_tensor(ada[:, v, :], mods[:, 8:16, v], 1.0, colA("norm1_g", 0, 8), ALU.add, ALU.mult)
                if v == 0:
                    link(ins)
            ins.then_inc(S("ada_ready"), 1)
            dve.wait_ge(S("ada_ready"), 1)
            for k in range(KT):
                V.tensor_scalar(hboth[:, k, T:2 * T], hboth[:, k, T:2 * T], ada[:, 0, k:k + 1], mod(0, 0, k), ALU.mult, ALU.add)\
                    .then_inc(S("h1_tokens"), 1)
            for h in range(GH):
                if h == 2:
                    mod_sum(4)
                b = ph1.read(dve, ("k", 0, h))
                V.tensor_copy(kT[:, h, :], PS[:, b, :]).then_inc(psum_free[b], 1)
            mod_sum(5)
            modulate(4)
            b = ph1.read(dve, "colsL")
            V.tensor_copy(colsL[:, :, :], PS[:, b, 0:2 * LCOLS].rearrange("p (l n) -> p l n", l=2)).then_inc(psum_free[b], 1)
            ph1.freed(dve, "colsL")
            o = row_at(ROWS_B, "hg_lb_2")
            link(V.memset(lbc[:, 0, 0:2], 0.0))
            link(V.memset(lbc[:, 0, 2:4], 1.0))
            V.tensor_tensor(lbc[:, 1, 0:2], colsL[:, 1, o:o + 2], colsL[:, 0, o:o + 2], ALU.subtract)\
                .then_inc(S("cols_ready"), 1)
            for j in (6, 7, 8):
                mod_sum(j)
            for j in (5, 6, 7):
                modulate(j)
            for j in (9, 10, 11):
                mod_sum(j)
            for j in (8, 9, 10, 11):
                modulate(j)
            ph1.freed(dve, ("mod", 11))
            dve.wait_ge(S("lb_ready"), 1)
            V.tensor_scalar(lbc[:, 1, 2:4], lbc[:, 1, 0:2], -1.0, 1.0, ALU.mult, ALU.add)
            for d in range(2):
                for h in range(GH):
                    b = ph1.read(dve, ("z", d, h))
                    bias = colA("gla_ab_f" if d == 0 else "gla_ab_b", h)
                    V.tensor_scalar(la[:, d, h, :], PS[:, b, :], bias, 0.0, ALU.add, ALU.min)
                    V.tensor_scalar(cum[:, d, h, :], PS[:, b, :], bias, None, ALU.add).then_inc(psum_free[b], 1)
                    ph1.freed(dve, ("z", d, h))
                    V.scalar_tensor_tensor(cum[:, d, h, :], cum[:, d, h, :], -1.0, cum[:, d, h, :], ALU.mult,
                                           ALU.min).then_inc(S("absz"), 1)
            for d in range(2):
                for h in range(GH):
                    dve.wait_ge(S("lnz"), d * GH + h + 1)
                    link(V.tensor_tensor(la[:, d, h, :], la[:, d, h, :], cum[:, d, h, :], ALU.subtract))
                    link(V.tensor_tensor_scan(cum[:, d, h, :], C("reset"), la[:, d, h, :], 0.0, ALU.mult, ALU.add))
            link(V.tensor_copy(lastc, cum[:, 0, :, T - 1]))
            V.tensor_tensor(e1, lastc.unsqueeze(2).broadcast_to([P, GH, T]), cum[:, 0, :, 0:T], ALU.subtract)\
                .then_inc(S("krc_arg"), 1)
            V.tensor_tensor(e2, cum[:, 1, :, 0:T], la[:, 1, :, 0:T], ALU.subtract).then_inc(S("krc_arg"), 1)
            V.tensor_copy(lastx, cum[:, :, :, T + CH - 1:2 * T:CH]).then_inc(S("decays"), 1)
            dve.wait_ge(S("decays"), 1)
            for d, e in ((0, e1), (1, e2)):
                dve.wait_ge(S("krc_exp"), d + 1)
                V.tensor_tensor(e, e, kT[:, :, 0:T], ALU.mult).then_inc(S("krc_ready"), 1)
            for d in range(2):
                for t in range(TT):
                    b = ph1.read(dve, ("krc", d, t))
                    V.tensor_copy(krt[:, d, t, :], PS[:, b, :]).then_inc(psum_free[b], 1)
            V.tensor_tensor(e1.rearrange("p h (n c) -> p h n c", n=NCH), lastx[:, 0].unsqueeze(3).broadcast_to([P, GH, NCH, CH]),
                            cum[:, 0, :, T:2 * T].rearrange("p h (n c) -> p h n c", n=NCH), ALU.subtract)\
                .then_inc(S("krx_arg"), 1)
            link(V.tensor_tensor(e2, cum[:, 1, :, T:2 * T], la[:, 1, :, T:2 * T], ALU.subtract))
            V.tensor_tensor(cum[:, 1, :, T:2 * T].rearrange("p h (n c) -> p h n c", n=NCH),
                            lastx[:, 1].unsqueeze(3).broadcast_to([P, GH, NCH, CH]),
                            e2.rearrange("p h (n c) -> p h n c", n=NCH), ALU.subtract).then_inc(S("cumb_ready"), 1)
            ph1.freed(dve, ("q", 0, 1))
            for d in range(2):
                dve.wait_ge(S("qdki_exp"), 2 * d + 1)
                V.tensor_tensor(qd[:, d], qd[:, d], qT, ALU.mult).then_inc(S("qdki_ready"), 1)
                dve.wait_ge(S("qdki_exp"), 2 * d + 2)
                V.tensor_tensor(ki[:, d], ki[:, d], kT[:, :, T:2 * T], ALU.mult).then_inc(S("qdki_ready"), 1)
            for d, e in ((0, e1), (1, e2)):
                dve.wait_ge(S("krx_exp"), d + 1)
                V.tensor_tensor(e, e, kT[:, :, T:2 * T], ALU.mult).then_inc(S("krx_ready"), 1)
            for d in range(2):
                for t in range(TT):
                    b = ph1.read(dve, ("krx", d, t))
                    V.tensor_copy(krt[:, d, t, :], PS[:, b, :]).then_inc(psum_free[b], 1)
            for h in range(GH):
                b = ph1.read(dve, ("sc", h))
                both = PS[:, b, :].rearrange("p (d t c) -> p d t c", d=2, t=TT)
                V.tensor_tensor(scT[:, h], both[:, 0], C("incl").unsqueeze(1).broadcast_to([P, TT, P]), ALU.mult)
                o2 = e2[:, h, :].rearrange("p (t c) -> p t c", t=TT)
                V.tensor_tensor(o2, both[:, 1], C("rev").unsqueeze(1).broadcast_to([P, TT, P]), ALU.mult)\
                    .then_inc(psum_free[b], 1)
                ph1.freed(dve, ("sc", h))
                V.tensor_tensor(scT[:, h], scT[:, h], o2, ALU.add).then_inc(S("sc_ready"), 1)
            for d in range(2):
                for hp in range(2):
                    ph1.freed(dve, ("s0", d, hp))
            dve.wait_ge(S("dec_ready"), 1)
            for h in range(GH):
                if h >= 2:
                    ph1.read(dve, ("o", h - 2))
                banks = [ph1.read(dve, ("kv", h, n)) for n in range(4)]

                def update(d, n):
                    c = n if d == 0 else NCH - 1 - n
                    prev = s0[:, d, h, :] if n == 0 else Sx[:, h % 2, d, n - 1, :]
                    b = banks[[(d, c) in g for g in KV_UNITS].index(True)]
                    return V.scalar_tensor_tensor(Sx[:, h % 2, d, n, :], prev, dec[:, d, h, c:c + 1],
                                                  PS[:, b, d * 256:(d + 1) * 256], ALU.mult, ALU.add)

                update(0, 0)
                link(update(1, 0))
                update(0, 1).then_inc(psum_free[banks[1]], 1)
                update(1, 1).then_inc(psum_free[banks[0]], 1)
                for n in range(2):
                    ph1.freed(dve, ("kv", h, n))
                update(0, 2).then_inc(psum_free[banks[2]], 1)
                update(1, 2).then_inc(psum_free[banks[3]], 1)
            for g in range(2):
                ph1.freed(dve, ("u", 0, g))
            ph1.read(dve, ("o", GH - 1))
            link(V.memset(qdki[:, 0:1280], 0.0))
            u4 = hboth[:, 0:4, 0:T].rearrange("p g (r w) -> p g r w", r=ROWS)
            for g in range(POOL_G):
                ins = V.tensor_copy(pads[0][:, g, :, 8:8 + GRID_W], u4[:, g])
            link(ins)
            src = pads[0]
            pg = pooled.rearrange("p g (r w) -> p g r w", r=ROWS)
            rc = C("rcnt").rearrange("p (g w) -> p g w", g=POOL_G)
            for g in range(POOL_G):
                half = 1 << g
                a, z = {0: (1, 80), 1: (2, 79), 2: (4, 77), 3: (8, 73)}[g]
                dst = pads[1 + g % 2]
                if g == 0:
                    ins = V.tensor_tensor(dst[:, :, :, a:z], src[:, :, :, a - 1:z - 1], src[:, :, :, a:z], ALU.add)
                else:
                    q = half // 2
                    for gg in range(g, POOL_G):
                        ins = V.tensor_tensor(dst[:, gg, :, a:z], src[:, gg, :, a - q:z - q], src[:, gg, :, a + q:z + q], ALU.add)
                link(ins)
                ins = V.tensor_tensor(pg[:, g], dst[:, g, :, 8:8 + GRID_W],
                                      rc[:, g].unsqueeze(1).broadcast_to([P, ROWS, GRID_W]), ALU.mult)
                src = dst
            link(ins)
            V.tensor_tensor(pooled, pooled, hboth[:, 0:4, 0:T], ALU.subtract).then_inc(S("pooled_ready"), 1)
            dve.wait_ge(S("orstd_ready"), 1)
            orstd = e1
            o4 = oT.rearrange("p (h v) t -> p h v t", h=GH)
            link(V.tensor_tensor(o4, o4, orstd.unsqueeze(2).broadcast_to([P, GH, 2, T]), ALU.mult))
            for j in range(2):
                ph1.freed(dve, ("g", j, 1))
            for j in range(KT):
                ins = V.scalar_tensor_tensor(oT[:, j, :], oT[:, j, :], colA("gla_onorm_g", j % 2), sg[:, j, :],
                                             ALU.mult, ALU.mult)
            ins.then_inc(S("og_ready"), 1)
            for g in range(2):
                b = ph1.read(dve, ("yp", g))
                for i in range(2):
                    ins = V.tensor_scalar(yp[:, 2 * g + i, :], PS[:, b, i * T:(i + 1) * T],
                                          colA("pool_scale", 2 * g + i), None, ALU.mult)
                ins.then_inc(psum_free[b], 1)
            ph1.freed(dve, ("gate", 3, 1))
            for g in range(4):
                b = ph1.read(dve, ("pbr", g))
                V.tensor_tensor(mixed[:, 2 * g:2 * g + 2, :], PS[:, b, :].rearrange("p (j t) -> p j t", j=2),
                                gates(2 * g), ALU.mult).then_inc(psum_free[b], 1)
            ph1.freed(dve, ("pbr", 3))
            for j in range(2):
                for g in range(2):
                    b = ph1.read(dve, ("gbr", j, g))
                    o = 4 * j + 2 * g
                    V.tensor_tensor(sg[:, o:o + 2, :], PS[:, b, :].rearrange("p (j t) -> p j t", j=2),
                                    gates(8 + o), ALU.mult).then_inc(psum_free[b], 1)
                    ph1.freed(dve, ("gbr", j, g))
                    V.tensor_tensor(mixed[:, o:o + 2, :], mixed[:, o:o + 2, :], sg[:, o:o + 2, :], ALU.add)\
                        .then_inc(S("mixed_ready"), 1)
            for j in range(2):
                for g in range(2):
                    b = ph1.read(dve, ("wo", j, g))
                    for i in range(2):
                        k = 4 * j + 2 * g + i
                        ins = V.scalar_tensor_tensor(xT[:, k, :], PS[:, b, i * T:(i + 1) * T], mod(2, 0, k), xT[:, k, :],
                                                     ALU.mult, ALU.add)
                    ins.then_inc(psum_free[b], 1)
                    ph1.freed(dve, ("wo", j, g))
                    dve.sem_inc(S("x1_new"), 1)
            link(V.scalar_tensor_tensor(ada[:, 2, :], mods[:, 32:40, 0], 1.0, colA("norm2_g", 0, 8), ALU.add, ALU.mult))
            dve.wait_ge(S("rstd2_ready"), 1)
            for k in range(KT):
                V.scalar_tensor_tensor(h2n[:, k, :], xT[:, k, :], ada[:, 2, k:k + 1], rstd2, ALU.mult, ALU.mult)\
                    .then_inc(S("normed2"), 1)
            meet(dve, "dve")

            link = Chain(dve, "vec_step")
            V.memset(ytok, 0.0).then_inc(S("moe_zeroed"), 1)
            V.memset(PT, 0.0).then_inc(S("moe_zeroed"), 1)
            b = ph2.read(dve, "route")
            V.tensor_copy(lg, PS[:, b, 0:128].rearrange("p (t n) -> p t n", t=TT)[:, :, 0:36]).then_inc(psum_free[b], 1)
            ph2.freed(dve, "route")

            def first_of_max(view, out, n, scratch):
                link(V.tensor_reduce(scratch, view, AX.X, ALU.max))
                link(V.tensor_tensor(out, view, scratch.unsqueeze(2).broadcast_to([P, TT, n]), ALU.is_equal))
                link(V.tensor_tensor(out, out, C("desc")[:, 0:n].unsqueeze(1).broadcast_to([P, TT, n]), ALU.mult))
                link(V.tensor_reduce(m1[9], out, AX.X, ALU.max))
                link(V.tensor_tensor(out, out, m1[9].unsqueeze(2).broadcast_to([P, TT, n]), ALU.is_equal))

            first_of_max(lg[:, :, 0:4], m8[2], N_GRP, m1[0])
            V.tensor_tensor(m8[0], lg[:, :, 0:4], m1[0].unsqueeze(2).broadcast_to([P, TT, N_GRP]), ALU.subtract)\
                .then_inc(S("route_arg"), 1)
            link(V.tensor_scalar(m8[3], m8[2], BIG, -BIG, ALU.mult, ALU.add))
            e4 = lambda v: v.rearrange("p t (g e) -> p t g e", g=N_GRP)
            for i in range(TT):
                ins = V.tensor_tensor(e4(m32[1])[:, i], lg[:, i, 4:36].rearrange("p (g e) -> p g e", g=N_GRP),
                                      m8[2][:, i].unsqueeze(2).broadcast_to([P, N_GRP, 8]), ALU.mult)
            link(ins)
            for i in range(TT):
                ins = V.tensor_tensor(e4(m32[1])[:, i], e4(m32[1])[:, i], m8[3][:, i].unsqueeze(2).broadcast_to([P, N_GRP, 8]),
                                      ALU.add)
            link(ins)
            first_of_max(m32[1], m32[2], N_EXP, m1[1])
            link(V.scalar_tensor_tensor(m32[3], m32[2], -2 * BIG, m32[1], ALU.mult, ALU.add))
            first_of_max(m32[3], m32[4], N_EXP, m1[4])
            V.tensor_tensor(m32[0], m32[2], m32[4], ALU.add).then_inc(S("chosen"), 1)
            V.tensor_tensor(m1[2], m1[4], m1[1], ALU.subtract).then_inc(S("route_arg"), 1)
            dve.wait_ge(S("route_exp"), 2)
            link(V.tensor_reduce(m1[5], m8[1], AX.X, ALU.add))
            link(V.tensor_scalar(m1[6], m1[3], 1.0, None, ALU.add))
            link(V.tensor_tensor(m1[5], m1[5], m1[6], ALU.mult))
            link(V.reciprocal(m1[5], m1[5]))
            link(V.tensor_tensor(m1[6], m1[5], m1[3], ALU.mult))
            link(V.tensor_tensor(m32[5], m32[2], m1[5].unsqueeze(2).broadcast_to([P, TT, N_EXP]), ALU.mult))
            link(V.tensor_tensor(m32[6], m32[4], m1[6].unsqueeze(2).broadcast_to([P, TT, N_EXP]), ALU.mult))
            link(V.tensor_tensor(weights[:, :, 0:N_EXP], m32[5], m32[6], ALU.add))
            link(V.tensor_copy(weights[:, :, N_EXP:], weights[:, :, 0:2]))
            b = ph2.read(dve, "rank")
            link(V.scalar_tensor_tensor(m32[7], PS[:, b, 0:64].rearrange("p (t n) -> p t n", t=TT), 1.0, m32[0],
                                        ALU.add, ALU.mult))
            V.tensor_copy(totals, PS[:, b, 64:96]).then_inc(psum_free[b], 1)
            ph2.freed(dve, "rank")
            link(V.tensor_scalar(ranks[:, :, 0:N_EXP], m32[7], -1.0, None, ALU.add))
            link(V.tensor_scalar(ranks[:, :, N_EXP:], ranks[:, :, 0:2], -float(SLOTS), None, ALU.add))
            link(V.tensor_reduce(mx1[:, 0:1], totals, AX.X, ALU.max))
            link(V.tensor_tensor(m8[3][:, 0], mx1[:, 0:1].broadcast_to([P, 4]), C("thr"), ALU.is_gt))
            link(V.tensor_reduce(mx1[:, 1:2], m8[3][:, 0], AX.X, ALU.add))
            V.tensor_copy(rounds_i, mx1[:, 1:2]).then_inc(S("rounds_ready"), 1)
            dve.wait_ge(S("rounds_ready"), 1)
            rounds = dve.value_load(rounds_i[0:1, 0:1])
            link(V.memset(s1, 0.0))
            dve.sem_inc(S("y_hi"), 1)
            dve.sem_inc(S("y_lo"), 1)
            dve.sem_inc(S("pt_ready"), 1)
            dve.sem_inc(S("hid_ready"), 1)
            def masks(two):
                V.tensor_tensor(sel, C("iota").unsqueeze(1).unsqueeze(1).broadcast_to([P, TT, 2, SLOTS]),
                                ranks[:, :, two].unsqueeze(3).broadcast_to([P, TT, 2, SLOTS]),
                                ALU.is_equal).then_inc(S("sel_ready"), 1)

            def weigh(two):
                V.tensor_tensor(selw, sel, weights[:, :, two].unsqueeze(3).broadcast_to([P, TT, 2, SLOTS]),
                                ALU.mult).then_inc(S("selw_ready"), 1)

            masks(slice(0, 2))
            dve.wait_ge(S("sel_ready"), 1)
            weigh(slice(0, 2))
            with dve.Fori(0, rounds) as r:
                with dve.Fori(0, PAIRS) as p:
                    i1 = dve.snap(r * PAIRS + p + 1)
                    dve.wait_ge(S("gathered"), i1 + 1)
                    V.tensor_copy(hg[:, 4:8, :], PS[:, 5, :].rearrange("p (k s) -> p k s", k=4)).then_inc(S("hg_hi"), 1)
                    dve.wait_ge(S("pt_turned"), i1 + 1)
                    V.tensor_copy(PT, PS[:, 6, 0:T]).then_inc(S("pt_ready"), 1)
                    masks(bass.ds(p * 2 + 2, 2))
                    dve.wait_ge(S("sel_ready"), i1 + 1)
                    weigh(bass.ds(p * 2 + 2, 2))
                    dve.wait_ge(S("s1_ready"), i1)
                    dve.wait_ge(w3_read, i1)
                    V.tensor_tensor(hidt, s1, PS[:, 5, :], ALU.mult).then_inc(S("hidt_ready"), 1)
                    dve.wait_ge(y_full, i1)
                    V.tensor_copy(ytok[:, 512:1024], PS[:, 7, :]).then_inc(S("y_hi"), 1)
                V.tensor_scalar(ranks, ranks, -float(SLOTS), None, ALU.add).then_inc(S("ranks_moved"), 1)
                dve.wait_ge(S("ranks_moved"), r + 1)
            dve.drain().then_inc(S("evacuated"), 1)
            dve.wait_ge(S("moe_out"), 1)
            for k in range(KT):
                ins = V.scalar_tensor_tensor(xT[:, k, :], PS[:, k // 2, (k % 2) * T:(k % 2 + 1) * T], mod(5, 0, k),
                                             xT[:, k, :], ALU.mult, ALU.add)
                if k % 4 == 3:
                    ins.then_inc(S("x2_new"), 1)
            dve.wait_ge(S("rstd3_ready"), 1)
            for k in range(KT):
                ins = V.scalar_tensor_tensor(xT[:, k, :], xT[:, k, :], colA("final_norm_g", k), rstd2, ALU.mult, ALU.mult)
                if k % 4 == 3:
                    ins.then_inc(S("x3_new"), 1)
            meet(dve, "dve")

            v2 = lambda v: v.rearrange("p (j t) -> p j t", j=2)
            with dve.Fori(0, LAYERS) as L:
                link = Chain(dve, "vec_step")
                link(V.tensor_copy(col[:, 0:LCOLS], colsL[:, bass.ds(L, 1), :].rearrange("p a n -> p (a n)")))
                link(V.tensor_copy(col[:, LCOLS:], logs[:, bass.ds(L, 1), :].rearrange("p a n -> p (a n)")))
                link(V.tensor_copy(small[:, 0:4], lbc[:, bass.ds(L, 1), :].rearrange("p a n -> p (a n)")))

                def norm(n, name):
                    dve.wait_ge(S("rs_ready"), n)
                    for k in range(KT):
                        V.scalar_tensor_tensor(hT[:, k, :], xT[:, k, :], cl(name, k), rs, ALU.mult, ALU.mult)\
                            .then_inc(S("h_ready3"), 1)

                norm(1, "g_mix_pre_2")


                dve.wait_ge(S("beta_ready"), 1)
                bc = lambda v: v.unsqueeze(1).broadcast_to([P, TT, 4])
                link(V.tensor_tensor(zt, ab[:, :, 4:8], bc(col[:, LCOLS + 4:LCOLS + 8]), ALU.add))
                V.scalar_tensor_tensor(eRc, zt, -1.0, zt, ALU.mult, ALU.min).then_inc(S("zt_ready"), 1)
                link(V.tensor_scalar(zt, zt, 0.0, None, ALU.max))
                dve.wait_ge(S("softplus"), 1)
                link(V.tensor_tensor(zt, zt, eRc, ALU.add))
                dve.wait_ge(S("alog_exp"), 1)
                link(V.tensor_tensor(zt, zt, bc(col[:, LCOLS:LCOLS + 4]), ALU.mult))
                V.tensor_scalar(gt, zt, -1.0, None, ALU.mult).then_inc(S("g_ready"), 1)
                dve.wait_ge(S("g_ready"), 1)
                per_head = lambda v: v.rearrange("p t h -> p h t").unsqueeze(3).broadcast_to([P, DNH, TT, P])
                V.tensor_copy(gx, per_head(gt)).then_inc(S("gx_ready"), 1)
                V.tensor_copy(bx, per_head(beta)).then_inc(S("gx_ready"), 1)
                def conv(dsts, srcs, taps):
                    n = len(taps[0])
                    for d in range(n):
                        done = []
                        for dst, src, w in zip(dsts, srcs, taps):
                            if d == 0:
                                done.append(V.tensor_scalar(dst, src, w[-1], None, ALU.mult))
                            else:
                                done.append(V.scalar_tensor_tensor(dst[:, d:], src[:, 0:T - d], w[n - 1 - d], dst[:, d:],
                                                                   ALU.mult, ALU.add))
                        if d < n - 1:
                            link(done[-1])
                    return done

                def conv_tiles(q_, name):
                    for g in range(2):
                        b = ph3.read(dve, (name, g))
                        fs = [4 * q_ + 2 * g + i for i in range(2)]
                        conv([cs[:, f, :] for f in fs], [PS[:, b, i * T:(i + 1) * T] for i in range(2)],
                             [[cl("dn_conv_2", 12 * j + f) for j in range(DN_CONV)] for f in fs])[-1]\
                            .then_inc(psum_free[b], 1)
                        ph3.freed(dve, (name, g))
                ph3.freed(dve, "wi")

                def index_scores(t):
                    n = 0
                    for par in range(2):
                        ph3.freed(dve, ("is", t, par))
                        for i in range(2):
                            wcol = wi[:, t, 2 * i + par:2 * i + par + 1]
                            other = C("adm")[:, t * T:(t + 1) * T] if n == 0 else score[:, t, :]
                            ins = V.scalar_tensor_tensor(score[:, t, :], relu[:, par, i, :], wcol, other, ALU.mult, ALU.add)
                            n += 1
                            if i == 1:
                                ins.then_inc(S("relu_used"), 1)
                                dve.wait_ge(S("relu_used"), 2 * t + par + 1)
                            else:
                                link(ins)

                for t in range(TT):
                    index_scores(t)
                NEGV = NEG
                for r_ in range(TOPK // 8):
                    for t in range(TT):
                        ins = V.max(m8k[:, t, :], (score if r_ == 0 else work)[:, t, :])
                    link(ins)
                    for t in range(TT):
                        ins = V.match_replace(out=work[:, t, :], in_to_replace=m8k[:, t, :],
                                              in_values=(score if r_ == 0 else work)[:, t, :], imm_value=NEGV)
                    link(ins)
                link(V.tensor_tensor(work, work, score, ALU.not_equal))
                link(V.tensor_scalar(score, work, BIG, -BIG, ALU.mult, ALU.add))
                conv_tiles(0, "aq")
                conv_tiles(1, "ak")
                dve.sem_inc(S("conv_ready"), 1)
                conv_tiles(2, "av")
                dve.sem_inc(S("conv_ready"), 1)
                dve.wait_ge(S("l2_ready"), 1)
                rq = rsb.rearrange("p (h t) -> p h t", h=8)
                V.scalar_tensor_tensor(cs[:, 0:4, :], cs[:, 0:4, :], float(P ** -0.5), rq[:, 0:4, :], ALU.mult, ALU.mult)\
                    .then_inc(S("qk_normed"), 1)
                dve.wait_ge(S("v_silu"), 1)
                V.tensor_tensor(cs[:, 4:8, :], cs[:, 4:8, :], rq[:, 4:8, :], ALU.mult).then_inc(S("qk_normed"), 1)
                b = ph3.read(dve, "G")
                G4 = PS[:, b, 0:16].rearrange("p (i t h) -> p i t h", i=2, t=TT)
                link(V.tensor_copy(Gc, G4[:, 0]))
                V.tensor_tensor(eRc, G4[:, 1], Gc, ALU.subtract).then_inc(psum_free[b], 1)
                ph3.freed(dve, "G")
                dve.sem_inc(S("Gc_ready"), 1)
                for g in range(2):
                    b = ph3.read(dve, ("Gb", g))
                    for i in range(2):
                        for t in range(TT):
                            o = (2 * i + t) * P
                            ins = V.tensor_scalar(DT[:, 2 * g + i, t, :], PS[:, b, o:o + P], Gc[:, t, 2 * g + i:2 * g + i + 1],
                                                  0.0, ALU.subtract, ALU.min)
                    ins.then_inc(S("DT_arg"), 1)
                dve.wait_ge(S("eGc_ready"), 2)
                link(V.tensor_tensor(bG, beta, eGc, ALU.mult))
                dve.wait_ge(S("DT_exp"), 1)
                f4 = lambda v: v.rearrange("p h t c -> p (h t) c")
                link(V.tensor_tensor(f4(DT), f4(DT), C("incl").unsqueeze(1).broadcast_to([P, 8, P]), ALU.mult))
                z4 = lambda v, g: v[:, 2 * g:2 * g + 2].rearrange("p h t c -> p (h t c)")
                for g in range(2):
                    ph3.freed(dve, ("Gb", g))
                for g in range(2):
                    b = ph3.read(dve, ("bb", g))
                    V.tensor_tensor(z4(MT, g), PS[:, b, :], z4(DT, g), ALU.mult).then_inc(psum_free[b], 1)
                    ph3.freed(dve, ("bb", g))
                ph3.freed(dve, ("cf", 0))
                for i in range(2):
                    ins = V.tensor_scalar(cf[:, i, :], cf[:, i, :], small[:, 2 + i:3 + i], small[:, i:i + 1], ALU.mult, ALU.add)
                link(ins)
                V.tensor_scalar(kc, cf, -1.0, 1.0, ALU.mult, ALU.add)\
                    .then_inc(S("fg_ready"), 1)
                for g in range(2):
                    b = ph3.read(dve, ("kk", g))
                    V.tensor_tensor(z4(MT, g), PS[:, b, :], z4(MT, g), ALU.mult).then_inc(psum_free[b], 1)
                    ph3.freed(dve, ("kk", g))
                dve.sem_inc(S("MT_ready"), 1)
                for t in range(TT):
                    for par in range(2):
                        b = ph3.read(dve, ("lg", t, par))
                        V.tensor_tensor(pr[:, t].rearrange("p (i q) s -> p q i s", q=2)[:, par], v2(PS[:, b, :]),
                                        score[:, t, :].unsqueeze(1).broadcast_to([P, 2, T]), ALU.add)\
                            .then_inc(psum_free[b], 1)
                    for par in range(2):
                        ph3.freed(dve, ("lg", t, par))
                    link(V.tensor_reduce(ab[:, t, 0:4], pr[:, t], AX.X, ALU.max))
                    V.tensor_tensor(pr[:, t], pr[:, t], ab[:, t, 0:4].unsqueeze(2).broadcast_to([P, SAH, T]),
                                    ALU.subtract).then_inc(S("p_arg"), 1)
                for g in range(2):
                    b = ph3.read(dve, ("qk", g))
                    V.tensor_tensor(z4(QK, g), PS[:, b, :], z4(DT, g), ALU.mult).then_inc(psum_free[b], 1)
                h3 = lambda v: v.unsqueeze(2).broadcast_to([P, DNH, P])
                for t in range(TT):
                    b = ph3.read(dve, ("kt", t))
                    p3 = PS[:, b, :].rearrange("p (h c) -> p h c", h=DNH)
                    V.tensor_tensor(kd[:, t], p3, h3(eRc[:, t]), ALU.mult).then_inc(S("kvb_ready"), 1)
                    V.tensor_tensor(kb[:, t], p3, h3(bG[:, t]), ALU.mult).then_inc(psum_free[b], 1)
                    ph3.freed(dve, ("kt", t))
                    dve.sem_inc(S("kvb_ready"), 1)
                for t in range(TT):
                    b = ph3.read(dve, ("vt", t))
                    V.tensor_tensor(vb[:, t], PS[:, b, :].rearrange("p (h c) -> p h c", h=DNH), h3(beta[:, t]), ALU.mult)\
                        .then_inc(psum_free[b], 1)
                    ph3.freed(dve, ("vt", t))
                    dve.sem_inc(S("kvb_ready"), 1)

                ident4 = C("ident").unsqueeze(1).broadcast_to([P, 4, P])
                for g in range(2):
                    dve.wait_ge(S("B_ready"), g + 1)
                    V.tensor_tensor(f4(XIT[:, 2 * g:2 * g + 2]), ident4, f4(BT[0][:, 2 * g:2 * g + 2]), ALU.subtract)\
                        .then_inc(S("X0T_ready"), 1)
                for g in range(2):
                    b = ph3.read(dve, ("Z", 0, g))
                    V.tensor_tensor(f4(XI[:, 2 * g:2 * g + 2]), ident4, PS[:, b, :].rearrange("p (q c) -> p q c", q=4),
                                    ALU.subtract).then_inc(psum_free[b], 1)
                def soften(t):
                    dve.wait_ge(S("p_exp"), t + 1)
                    link(V.tensor_reduce(ab[:, t, 0:4], pr[:, t], AX.X, ALU.add))
                    link(V.reciprocal(ab[:, t, 4:8], ab[:, t, 0:4]))
                    V.tensor_tensor(pr[:, t], pr[:, t], ab[:, t, 4:8].unsqueeze(2).broadcast_to([P, SAH, T]),
                                    ALU.mult).then_inc(S("p_ready"), 1)
                soften(0)
                for lv in range(1, 6):
                    for g in range(2):
                        if lv < 5:
                            b = ph3.read(dve, ("XZ", lv, g))
                            V.tensor_tensor(z4(XI, g), z4(XI, g), PS[:, b, :], ALU.subtract).then_inc(psum_free[b], 1)
                        b = ph3.read(dve, ("ZX", lv, g))
                        V.tensor_tensor(z4(XIT, g), z4(XIT, g), PS[:, b, :], ALU.subtract).then_inc(psum_free[b], 1)
                    for g in range(2):
                        if lv < 5:
                            ph3.freed(dve, ("XZ", lv, g))
                        ph3.freed(dve, ("ZX", lv, g))
                    if lv == 1:
                        soften(1)
                dve.wait_ge(S("lf_ready"), 1)
                ph3.freed(dve, "ob")
                for i in range(2):
                    ins = V.tensor_tensor_scan(Bc[:, i, :], C("reset")[:, T:2 * T], cf[:, i, :], 0.0, ALU.mult, ALU.add)
                link(ins)
                for v_, size in enumerate((64, 32, 16)):
                    by_block = lambda v: v.rearrange("p (m c) -> p m c", c=size)
                    Bb = by_block(Bc.rearrange("p i t -> p (i t)"))
                    ins = V.tensor_tensor(by_block(args[:, v_, 0, :]), Bb,
                                          Bb[:, :, size // 2 - 1:size // 2].broadcast_to([P, 2 * T // size, size]), ALU.subtract)
                Bb = Bc.rearrange("p i (n c) -> p (i n) c", c=CH)
                link(V.tensor_tensor(eR.rearrange("p i (n c) -> p (i n) c", c=CH),
                                     Bb[:, :, CH - 1:CH].broadcast_to([P, 2 * NCH, CH]), Bb, ALU.subtract))
                link(V.tensor_scalar(args[:, 2, 0, :], args[:, 2, 0, :], 80.0, -80.0, ALU.min, ALU.max))
                V.tensor_scalar(args[:, 2, 1, :], args[:, 2, 0, :], -1.0, None, ALU.mult)
                link(V.tensor_scalar(args[:, 0:2, 1, :], args[:, 0:2, 0, :], -1.0, 0.0, ALU.mult, ALU.min))
                V.tensor_scalar(args[:, 0:2, 0, :], args[:, 0:2, 0, :], 0.0, None, ALU.min).then_inc(S("hg_args"), 1)
                def level_scores(lv, mask):
                    for par in range(2):
                        b = ph3.read(dve, ("hs", lv, par))
                        quads = lambda v: v.rearrange("p i t c -> p (i t) c")
                        dst = AT2 if lv else AT[:, par]
                        V.tensor_tensor(quads(dst), PS[:, b, :].rearrange("p (q c) -> p q c", q=4),
                                        C(mask).unsqueeze(1).broadcast_to([P, 4, P]), ALU.mult).then_inc(psum_free[b], 1)
                        ph3.freed(dve, ("hs", lv, par))
                        if lv:
                            ins = V.tensor_tensor(AT[:, par], AT[:, par], AT2, ALU.add)
                            if lv == 2:
                                ins.then_inc(S("AT_ready"), 1)
                                dve.wait_ge(S("AT_ready"), par + 1)
                            else:
                                link(ins)
                for t in range(TT):
                    ph3.freed(dve, ("u0", t))
                for n in range(NCH):
                    t, r_ = n // 2, slice(CH * (n % 2), CH * (n % 2) + CH)
                    if n:
                        b = ph3.read(dve, ("wS", n))
                        ur = u[r_, t].rearrange("p h c -> p (h c)")
                        V.tensor_tensor(ur, ur, PS[r_, b, :], ALU.subtract).then_inc(psum_free[b], 1)
                    if n < NCH - 1:
                        b = ph3.read(dve, ("dS", n))
                        for i in range(DNH):
                            p3 = PS[:, b, i * P:(i + 1) * P]
                            if n == 0:
                                ins = V.tensor_copy(Sd[0][:, i, :], p3)
                            else:
                                ins = V.scalar_tensor_tensor(Sd[n][:, i, :], Sd[n - 1][:, i, :], glast[:, i, n:n + 1], p3,
                                                             ALU.mult, ALU.add)
                        ins.then_inc(psum_free[b], 1)
                        ph3.freed(dve, ("dS", n))
                    if n == 0:
                        flat = lambda v: v.rearrange("p i t -> p (i t)")
                        dve.wait_ge(S("hg_exp"), 1)
                        for side, v in enumerate((cq, kc)):
                            V.tensor_tensor(args[:, :, side, :], args[:, :, side, :],
                                            flat(v).unsqueeze(1).broadcast_to([P, 3, 2 * T]), ALU.mult)\
                                .then_inc(S("qk_levels"), 1)
                    else:
                        level_scores(n - 1, ("lv5", "lv4", "diag16")[n - 1])
                for par, ns in ((0, (0, 2)), (1, (1,))):
                    b = ph3.read(dve, ("hS", par))
                    for j, n in enumerate(ns):
                        ins = V.tensor_tensor(Sh[:, n], PS[:, b, 2 * j * P:2 * (j + 1) * P].rearrange("p (i c) -> p i c", i=2),
                                              C("blk").unsqueeze(1).broadcast_to([P, 2, P]), ALU.mult)
                    ins.then_inc(psum_free[b], 1)
                    ph3.freed(dve, ("hS", par))
                for n in (1, 2):
                    for i in range(2):
                        ins = V.scalar_tensor_tensor(Sh[:, n, i, :], Sh[:, n - 1, i, :], hlast[:, i, n:n + 1], Sh[:, n, i, :],
                                                     ALU.mult, ALU.add)
                    if n == 1:
                        link(ins)
                ins.then_inc(S("Sh_ready"), 1)
                dve.wait_ge(S("oam_ready"), 1)
                link(V.scalar_tensor_tensor(cat[:, 0:4, :], cat[:, 0:4, :], cl("dn_norm_2"), fT[:, 0:4, :], ALU.mult, ALU.mult))
                V.tensor_tensor(cat[:, 0:4, :], cat[:, 0:4, :], sz, ALU.mult).then_inc(S("oa_ready"), 1)
                dve.wait_ge(S("oam_ready"), 2)
                link(V.scalar_tensor_tensor(cat[:, 6:8, :], cat[:, 6:8, :], cl("hg_norm_2"), fT[:, 4:6, :], ALU.mult, ALU.mult))
                V.tensor_tensor(cat[:, 6:8, :], cat[:, 6:8, :], cg, ALU.mult).then_inc(S("oc_ready"), 1)

                def add_normed(n, name, key):
                    dve.wait_ge(S("rs_ready"), n)
                    for i in range(2):
                        for k in range(4 * i, 4 * i + 4):
                            b = ph3.read(dve, key(k // 2))
                            ins = V.scalar_tensor_tensor(fT[:, k, :], PS[:, b, (k % 2) * T:(k % 2 + 1) * T], cl(name, k), rs,
                                                         ALU.mult, ALU.mult)
                            if k % 2:
                                ins.then_inc(psum_free[b], 1)
                        ph3.freed(dve, key(2 * i))
                        ph3.freed(dve, key(2 * i + 1))
                        V.tensor_tensor(xT[:, 4 * i:4 * i + 4, :], xT[:, 4 * i:4 * i + 4, :], fT[:, 4 * i:4 * i + 4, :], ALU.add)\
                            .then_inc(S("x_new"), 1)

                add_normed(2, "g_mix_post_2", lambda g: (("out", g // 2), g % 2))
                dve.wait_ge(S("x_new"), 2)
                norm(3, "g_ffn_pre_2")

                def gate(j):
                    dve.wait_ge(S("gelu_ready"), j + 1)
                    V.tensor_tensor(gated[:, 2 * j:2 * j + 2, :], gcv[:, j % 2, 0:2, :], gcv[:, j % 2, 2:4, :], ALU.mult)\
                        .then_inc(S("gated"), 1)

                for j in range(FFT // 2):
                    if j >= 2:
                        dve.wait_ge(S("gated"), j - 1)
                    for v in range(2):
                        b = ph3.read(dve, ("up", j, v))
                        conv([gcv[:, j % 2, 2 * v + i, :] for i in range(2)], [PS[:, b, i * T:(i + 1) * T] for i in range(2)],
                             [[ffn_tap(q_, FFT * v + 2 * j + i) for q_ in range(FFN_CONV)] for i in range(2)])[-1]\
                            .then_inc(psum_free[b], 1)
                        ph3.freed(dve, ("up", j, v))
                    if j:
                        gate(j - 1)
                gate(FFT // 2 - 1)
                add_normed(4, "g_ffn_post_2", lambda g: ("down", g))
                meet(dve, "dve")
            for t in range(TT):
                for g in range(2):
                    dve.wait_ge(S("out_turned"), 2 * t + g + 1)
                    V.tensor_copy(outt[:, t, g * 512:(g + 1) * 512], PS[:, 2 * t + g, :]).then_inc(S("out_copied"), 1)

        @block.gpsimd
        def _(pool):
            def reset_stages(engines):
                pool.wait_ge(idle, engines)
                pool.drain()
                nums = sorted(q.num for q in stages)
                i = 0
                while i < len(nums):
                    j = i
                    while j + 1 < len(nums) and nums[j + 1] == nums[j] + 1:
                        j += 1
                    pool.sem_clear(range(nums[i], nums[j] + 1))
                    i = j + 1
                for g in go.values():
                    pool.sem_inc(g, 1)

            pool.wait_ge(S("a2_zero"), 1)
            for dst, src in PARAMS[N_FIRST:]:
                pool.dma_start(dst, src).then_inc(params_in, 16)
            reset_stages(4)
            reset_stages(4)
            with pool.Fori(0, LAYERS) as L:
                link = Chain(pool, "pool_step")
                for g in range(2):
                    ph3.freed(pool, ("Gb", g))
                pool.wait_ge(S("qk_normed"), 1)
                link(nc.gpsimd.tensor_copy(glast, eG[:, :, CH - 1:T:CH]))
                nc.gpsimd.tensor_tensor(eG, eG, cs[:, 0:4, :], ALU.mult).then_inc(S("qdec_ready"), 1)
                pool.wait_ge(S("MT_ready"), 1)
                for lv in range(6):
                    for g in range(2):
                        if lv == 1:
                            ph3.freed(pool, ("bb", g))
                        elif lv >= 2:
                            ph3.freed(pool, ("Z", lv - 2, g))
                            if lv == 2:
                                pool.wait_ge(S("X0T_ready"), g + 1)
                        f4 = lambda v: v.rearrange("p h t c -> p (h t) c")
                        nc.gpsimd.tensor_tensor(f4(BT[lv % 2][:, 2 * g:2 * g + 2]), f4(MT[:, 2 * g:2 * g + 2]),
                                                C(f"lv{lv}").unsqueeze(1).broadcast_to([P, 4, P]), ALU.mult)\
                            .then_inc(S("B_ready"), 1)
                pool.wait_ge(S("hg_exp"), 3)
                link(nc.gpsimd.tensor_copy(hlast, eB[:, :, CH - 1:T:CH]))
                nc.gpsimd.tensor_tensor(eR, eR, kc, ALU.mult).then_inc(S("kdec_ready"), 1)
                nc.gpsimd.tensor_tensor(eB, eB, cq, ALU.mult).then_inc(S("qdec2_ready"), 1)
                reset_stages(4)


_INS = ['x', 'c', 'ctx', 'c_ctx', 'w_mod', 'b_mod', 'norm1_g', 'norm2_g', 'w_in', 'gla_a2_f', 'gla_ab_f', 'gla_a2_b',
        'gla_ab_b', 'gla_onorm_g', 'pool_w', 'pool_scale', 'w_pool_br', 'w_gla_br', 'w_o', 'router_grp_w',
        'router_grp_b', 'router_exp_w', 'router_exp_b', 'moe_w1', 'moe_w3', 'moe_w2', 'final_norm_g', 'w_in_2',
        'dn_conv_2', 'dn_a_log_2', 'dn_dt_bias_2', 'dn_norm_2', 'hg_lb_2', 'hg_norm_2', 'w_out_2', 'g_mix_pre_2',
        'g_mix_post_2', 'g_ffn_pre_2', 'g_ffn_post_2', 'ffn_w_up_2', 'ffn_conv_2', 'ffn_w_down_2']


def kernel(**inputs):
    import numpy as _np
    import concourse.bacc as _bacc
    from concourse import mybir as _mybir
    from concourse.bass_utils import run_bass_kernel_spmd as _run

    nc = _bacc.Bacc("TRN2", target_bir_lowering=False, num_devices=1)
    arrays, handles = {}, {}
    for name in _INS:
        a = _np.ascontiguousarray(inputs[name])
        arrays[f"in_{name}_dram"] = a
        handles[name] = nc.dram_tensor(f"in_{name}_dram", a.shape, _mybir.dt.from_np(a.dtype), kind="ExternalInput").ap()
    table = constants()[1]
    arrays["consts_dram"] = table
    handles["consts"] = nc.dram_tensor("consts_dram", table.shape, _mybir.dt.float32, kind="ExternalInput").ap()
    out = nc.dram_tensor("out_0_dram", (1, 256, 1024), _mybir.dt.float32, kind="ExternalOutput").ap()
    build(nc, handles, out)
    r = _run(nc, [arrays], core_ids=[0])
    return r.results[0]["out_0_dram"]
```
